# Optimizing a Trainium2 kernel written in Bass

```python
import functools
import jax, jax.numpy as jnp
from jax import lax
import numpy as np

D_MODEL = 1024
BATCH = 1
SEQ = 256
DEPTH = 1
DEC_BATCH = 8
DEC_SEQ = 8
PAST_LEN = 1024
PAGE_SIZE = 128

ATT_HEADS = 8
ATT_KV_HEADS = 2
HEAD_DIM = 64
ROPE_DIM = HEAD_DIM // 4
ROPE_THETA = 500000.0
IDX_HEADS = 8
IDX_DIM = 64
IDX_ROPE_DIM = IDX_DIM // 4
TOPK_MAX = 256
Q_BLOCK = 128
RET_HEADS = 8
RET_DK = 64
RET_DV = 128
RET_THETA = 10000.0
RET_CHUNK = 128
N_EXPERTS = 32
TOP_K = 4
D_FF = D_MODEL
SWIGLU_LIMIT = 7.0
SWIGLU_ALPHA = 1.702
MOE_BLOCK = 128
NORM_EPS = 1e-6
GN_EPS = 1e-5
ATT_OUT = ATT_HEADS * HEAD_DIM
RET_OUT = RET_HEADS * RET_DV
IN_SPLITS = (ATT_HEADS * HEAD_DIM, ATT_KV_HEADS * HEAD_DIM, ATT_KV_HEADS * HEAD_DIM,
             IDX_HEADS * IDX_DIM, IDX_DIM, IDX_HEADS,
             RET_HEADS * RET_DK, RET_HEADS * RET_DK, RET_OUT, RET_OUT,
             D_MODEL, D_MODEL)
D_IN = sum(IN_SPLITS)

kernel_name = 'hybrid_dsa_retention_moe_step'

def _rmsnorm(x, g):
    xf = x.astype(jnp.float32)
    y = xf * lax.rsqrt(jnp.mean(xf * xf, axis=-1, keepdims=True) + NORM_EPS)
    return (y * g.astype(jnp.float32)).astype(x.dtype)

def _rope(x, pos, rot_dim, theta):
    half = rot_dim // 2
    inv = theta ** (-jnp.arange(half, dtype=jnp.float32) * (2.0 / rot_dim))
    ang = pos.astype(jnp.float32)[:, None] * inv[None, :]
    cos = jnp.cos(ang)[:, None, :]
    sin = jnp.sin(ang)[:, None, :]
    xr = x[..., :rot_dim].astype(jnp.float32)
    x1, x2 = xr[..., :half], xr[..., half:]
    rot = jnp.concatenate([x1 * cos - x2 * sin, x2 * cos + x1 * sin], axis=-1).astype(x.dtype)
    return jnp.concatenate([rot, x[..., rot_dim:]], axis=-1)

def _index_scores(iq, ik, iw):
    dots = jnp.einsum('bthi,bsi->bths', iq, ik, preferred_element_type=jnp.float32) * (IDX_DIM ** -0.5)
    w = iw.astype(jnp.float32) * (IDX_HEADS ** -0.5)
    return jnp.einsum('bths,bth->bts', jax.nn.relu(dots), w)

def _sparse_attend(q, k_sel, v_sel, valid):
    b, t, h, d = q.shape
    qg = q.reshape(b, t, ATT_KV_HEADS, h // ATT_KV_HEADS, d)
    s = jnp.einsum('btjgd,btnjd->btjgn', qg, k_sel, preferred_element_type=jnp.float32) * (HEAD_DIM ** -0.5)
    s = jnp.where(valid[:, :, None, None, :], s, -jnp.inf)
    p = jax.nn.softmax(s, axis=-1).astype(v_sel.dtype)
    o = jnp.einsum('btjgn,btnjd->btjgd', p, v_sel)
    return o.reshape(b, t, h * d)

def _dsa_prompt(q, k, v, iq, ik, iw):
    b, s = q.shape[:2]
    topk = min(TOPK_MAX, s // 4)
    nb = s // Q_BLOCK
    key_pos = jnp.arange(s)
    gather = jax.vmap(lambda a, i: a[i])

    def block(args):
        qb, iqb, iwb, qpos = args
        scores = _index_scores(iqb, ik, iwb)
        causal = key_pos[None, None, :] <= qpos[None, :, None]
        scores = jnp.where(causal, scores, -jnp.inf)
        _, idx = lax.top_k(scores, topk)
        valid = idx <= qpos[None, :, None]
        return _sparse_attend(qb, gather(k, idx), gather(v, idx), valid)

    to_blocks = lambda a: a.reshape(b, nb, Q_BLOCK, *a.shape[2:]).swapaxes(0, 1)
    out = lax.map(block, (to_blocks(q), to_blocks(iq), to_blocks(iw), jnp.arange(s).reshape(nb, Q_BLOCK)))
    return out.swapaxes(0, 1).reshape(b, s, ATT_OUT)

def _dsa_sample(q, k, v, iq, ik, iw, cache_k, cache_v, cache_ik, page_table):
    db, t = q.shape[:2]
    n_pages = PAST_LEN // PAGE_SIZE
    n_keys = PAST_LEN + t
    topk = min(TOPK_MAX, n_keys // 4)
    ik_past = cache_ik[page_table].reshape(db, n_pages * PAGE_SIZE, IDX_DIM)
    ik_all = jnp.concatenate([ik_past, ik.astype(ik_past.dtype)], axis=1)
    scores = _index_scores(iq, ik_all, iw)
    qpos = PAST_LEN + jnp.arange(t)
    causal = jnp.arange(n_keys)[None, None, :] <= qpos[None, :, None]
    scores = jnp.where(causal, scores, -jnp.inf)
    _, idx = lax.top_k(scores, topk)
    valid = idx <= qpos[None, :, None]
    in_past = idx < PAST_LEN
    pidx = jnp.minimum(idx, PAST_LEN - 1)
    phys_page = jnp.take_along_axis(page_table, (pidx // PAGE_SIZE).reshape(db, -1), axis=1).reshape(idx.shape)
    phys_row = phys_page * PAGE_SIZE + pidx % PAGE_SIZE
    nidx = jnp.clip(idx - PAST_LEN, 0, t - 1)
    gather = jax.vmap(lambda a, i: a[i])
    flat_k = cache_k.reshape(-1, ATT_KV_HEADS, HEAD_DIM)
    flat_v = cache_v.reshape(-1, ATT_KV_HEADS, HEAD_DIM)
    sel = in_past[..., None, None]
    k_sel = jnp.where(sel, flat_k[phys_row], gather(k, nidx).astype(flat_k.dtype))
    v_sel = jnp.where(sel, flat_v[phys_row], gather(v, nidx).astype(flat_v.dtype))
    return _sparse_attend(q, k_sel.astype(q.dtype), v_sel.astype(q.dtype), valid)

def _ret_log_gamma():
    return jnp.log(1.0 - 2.0 ** (-5.0 - jnp.arange(RET_HEADS, dtype=jnp.float32)))

def _retention_chunk(state, q, k, v, log_gamma):
    c = q.shape[1]
    i = jnp.arange(c, dtype=jnp.float32)
    diff = i[:, None] - i[None, :]
    decay = jnp.where(diff >= 0, jnp.exp(jnp.maximum(diff, 0.0)[None] * log_gamma[:, None, None]), 0.0)
    qf = q.astype(jnp.float32)
    kf = k.astype(jnp.float32) * (RET_DK ** -0.5)
    vf = v.astype(jnp.float32)
    scores = jnp.einsum('bihd,bjhd->bhij', qf, kf) * decay[None]
    o = jnp.einsum('bhij,bjhv->bihv', scores, vf)
    q_decay = jnp.exp((i + 1.0)[:, None] * log_gamma[None, :])
    o = o + jnp.einsum('bihd,bhdv->bihv', qf * q_decay[None, :, :, None], state)
    k_decay = jnp.exp((c - 1.0 - i)[:, None] * log_gamma[None, :])
    new_state = (state * jnp.exp(c * log_gamma)[None, :, None, None]
                 + jnp.einsum('bjhd,bjhv->bhdv', kf * k_decay[None, :, :, None], vf))
    return new_state, o

def _retention_prompt(q, k, v):
    b, s = q.shape[:2]
    nc = s // RET_CHUNK
    lg = _ret_log_gamma()
    to_chunks = lambda a: a.reshape(b, nc, RET_CHUNK, *a.shape[2:]).swapaxes(0, 1)
    s0 = jnp.zeros((b, RET_HEADS, RET_DK, RET_DV), jnp.float32)
    s_final, o = lax.scan(lambda st, xs: _retention_chunk(st, xs[0], xs[1], xs[2], lg), s0,
                          (to_chunks(q), to_chunks(k), to_chunks(v)))
    return o.swapaxes(0, 1).reshape(b, s, RET_HEADS, RET_DV), s_final

def _retention_sample(q, k, v, state):
    new_state, o = _retention_chunk(state.astype(jnp.float32), q, k, v, _ret_log_gamma())
    return o, new_state

def _head_groupnorm(o):
    mu = jnp.mean(o, axis=-1, keepdims=True)
    var = jnp.mean(jnp.square(o - mu), axis=-1, keepdims=True)
    return (o - mu) * lax.rsqrt(var + GN_EPS)

def _moe(h, w_router, b_router, w_gate_up, b_gate_up, w_down, b_down):
    lead = h.shape[:-1]
    x = h.reshape(-1, D_MODEL)
    n_tok = x.shape[0]
    logits = jnp.einsum('td,de->te', x, w_router, preferred_element_type=jnp.float32) + b_router.astype(jnp.float32)
    top_val, top_idx = lax.top_k(logits, TOP_K)
    gates = jax.nn.softmax(top_val, axis=-1)
    n_asg = n_tok * TOP_K
    e_f = top_idx.reshape(-1)
    tok_f = jnp.arange(n_asg, dtype=jnp.int32) // TOP_K
    w_f = gates.reshape(-1)
    order = jnp.argsort(e_f)
    e_s, tok_s, w_s = e_f[order], tok_f[order], w_f[order]
    counts = jnp.bincount(e_f, length=N_EXPERTS)
    padded = (counts + MOE_BLOCK - 1) // MOE_BLOCK * MOE_BLOCK
    start = jnp.cumsum(counts) - counts
    pend = jnp.cumsum(padded)
    pstart = pend - padded
    dest = pstart[e_s] + jnp.arange(n_asg) - start[e_s]
    n_blocks = -(-n_asg // MOE_BLOCK) + N_EXPERTS
    n_rows = n_blocks * MOE_BLOCK
    row_tok = jnp.zeros((n_rows,), jnp.int32).at[dest].set(tok_s)
    row_w = jnp.zeros((n_rows,), jnp.float32).at[dest].set(w_s)
    blk_expert = jnp.minimum(jnp.searchsorted(pend, jnp.arange(n_blocks) * MOE_BLOCK, side='right'), N_EXPERTS - 1)

    def expert_block(args):
        toks, e = args
        gu = x[toks] @ w_gate_up[e] + b_gate_up[e]
        g = jnp.minimum(gu[:, :D_FF], SWIGLU_LIMIT)
        u = jnp.clip(gu[:, D_FF:], -SWIGLU_LIMIT, SWIGLU_LIMIT)
        act = (u + 1.0) * (g * jax.nn.sigmoid(SWIGLU_ALPHA * g))
        return act @ w_down[e] + b_down[e]

    out = lax.map(expert_block, (row_tok.reshape(n_blocks, MOE_BLOCK), blk_expert))
    out = out.reshape(n_rows, D_MODEL).astype(jnp.float32) * row_w[:, None]
    y = jax.ops.segment_sum(out, row_tok, num_segments=n_tok)
    return y.astype(h.dtype).reshape(*lead, D_MODEL)

def _layer(x, c, pos, attend, retain, g_mix, g_ffn, w_ada, b_ada, w_in, w_pa, w_pb, w_o,
           w_router, b_router, w_gate_up, b_gate_up, w_down, b_down):
    b, s, _ = x.shape
    mod = (jnp.einsum('bd,de->be', jax.nn.silu(c), w_ada) + b_ada)[:, None, :]
    sh1, sc1, gt1, sh2, sc2, gt2 = jnp.split(mod, 6, axis=-1)
    h = _rmsnorm(x, g_mix) * (1.0 + sc1) + sh1
    z = jnp.einsum('bsd,de->bse', h, w_in)
    q, k, v, iq, ik, iw, rq, rk, rv, rg, ga, gb = jnp.split(z, np.cumsum(IN_SPLITS)[:-1].tolist(), axis=-1)
    q = _rope(q.reshape(b, s, ATT_HEADS, HEAD_DIM), pos, ROPE_DIM, ROPE_THETA)
    k = _rope(k.reshape(b, s, ATT_KV_HEADS, HEAD_DIM), pos, ROPE_DIM, ROPE_THETA)
    v = v.reshape(b, s, ATT_KV_HEADS, HEAD_DIM)
    iq = _rope(iq.reshape(b, s, IDX_HEADS, IDX_DIM), pos, IDX_ROPE_DIM, ROPE_THETA)
    ik = _rope(ik.reshape(b, s, 1, IDX_DIM), pos, IDX_ROPE_DIM, ROPE_THETA)[:, :, 0]
    rq = _rope(rq.reshape(b, s, RET_HEADS, RET_DK), pos, RET_DK, RET_THETA)
    rk = _rope(rk.reshape(b, s, RET_HEADS, RET_DK), pos, RET_DK, RET_THETA)
    rv = rv.reshape(b, s, RET_HEADS, RET_DV)
    a_out = attend(q, k, v, iq, ik, iw)
    r_out, r_state = retain(rq, rk, rv)
    r_out = _head_groupnorm(r_out).reshape(b, s, RET_OUT).astype(x.dtype) * jax.nn.silu(rg)
    merged = jax.nn.sigmoid(ga) * (a_out @ w_pa) + jax.nn.sigmoid(gb) * (r_out @ w_pb)
    x = x + gt1 * (merged @ w_o)
    h2 = _rmsnorm(x, g_ffn) * (1.0 + sc2) + sh2
    x = x + gt2 * _moe(h2, w_router, b_router, w_gate_up, b_gate_up, w_down, b_down)
    return x, (k, v, ik, r_state)

def setup_inputs(seed: int = 0) -> dict:
    key = jax.random.key(seed)
    ks = jax.random.split(key, 26)
    f32 = jnp.float32
    nrm = lambda kk, shape, scale: scale * jax.random.normal(kk, shape, f32)
    n_pages = PAST_LEN // PAGE_SIZE
    n_used = DEC_BATCH * n_pages
    n_pool = n_used + max(1, n_used // 4)
    page_table = jax.random.permutation(ks[7], n_pool)[:n_used].reshape(DEC_BATCH, n_pages).astype(jnp.int32)
    return {
        'x_prompt': nrm(ks[0], (BATCH, SEQ, D_MODEL), 1.0),
        'x_sample': nrm(ks[1], (DEC_BATCH, DEC_SEQ, D_MODEL), 1.0),
        'cache_k': nrm(ks[2], (DEPTH, n_pool, PAGE_SIZE, ATT_KV_HEADS, HEAD_DIM), 1.0),
        'cache_v': nrm(ks[3], (DEPTH, n_pool, PAGE_SIZE, ATT_KV_HEADS, HEAD_DIM), 1.0),
        'cache_ik': nrm(ks[4], (DEPTH, n_pool, PAGE_SIZE, IDX_DIM), 1.0),
        'state_ret': nrm(ks[5], (DEPTH, DEC_BATCH, RET_HEADS, RET_DK, RET_DV), 0.3),
        'page_table': page_table,
        'c_prompt': nrm(ks[6], (BATCH, D_MODEL), 1.0),
        'c_sample': nrm(ks[8], (DEC_BATCH, D_MODEL), 1.0),
        'norm_mix_g': 1.0 + nrm(ks[9], (DEPTH, D_MODEL), 0.01),
        'norm_ffn_g': 1.0 + nrm(ks[10], (DEPTH, D_MODEL), 0.01),
        'norm_final_g': 1.0 + nrm(ks[11], (D_MODEL,), 0.01),
        'w_ada': nrm(ks[12], (DEPTH, D_MODEL, 6 * D_MODEL), 0.5 * D_MODEL ** -0.5),
        'b_ada': nrm(ks[13], (DEPTH, 6 * D_MODEL), 0.01),
        'w_in': nrm(ks[14], (DEPTH, D_MODEL, D_IN), D_MODEL ** -0.5),
        'w_branch_a': nrm(ks[15], (DEPTH, ATT_OUT, D_MODEL), ATT_OUT ** -0.5),
        'w_branch_b': nrm(ks[16], (DEPTH, RET_OUT, D_MODEL), RET_OUT ** -0.5),
        'w_out': nrm(ks[17], (DEPTH, D_MODEL, D_MODEL), D_MODEL ** -0.5),
        'w_router': nrm(ks[18], (DEPTH, D_MODEL, N_EXPERTS), D_MODEL ** -0.5),
        'b_router': nrm(ks[19], (DEPTH, N_EXPERTS), 0.01),
        'w_gate_up': nrm(ks[20], (DEPTH, N_EXPERTS, D_MODEL, 2 * D_FF), D_MODEL ** -0.5),
        'b_gate_up': nrm(ks[21], (DEPTH, N_EXPERTS, 2 * D_FF), 0.01),
        'w_down': nrm(ks[22], (DEPTH, N_EXPERTS, D_FF, D_MODEL), D_FF ** -0.5),
        'b_down': nrm(ks[23], (DEPTH, N_EXPERTS, D_MODEL), 0.01),
    }

def reference(x_prompt, x_sample, cache_k, cache_v, cache_ik, state_ret, page_table, c_prompt, c_sample,
              norm_mix_g, norm_ffn_g, norm_final_g, w_ada, b_ada, w_in, w_branch_a, w_branch_b, w_out,
              w_router, b_router, w_gate_up, b_gate_up, w_down, b_down):
    pos_p = jnp.arange(x_prompt.shape[1])
    pos_s = PAST_LEN + jnp.arange(x_sample.shape[1])
    hp, hs = x_prompt, x_sample
    k_p, v_p, ik_p, r_p = [], [], [], []
    k_s, v_s, ik_s, r_s = [], [], [], []
    for l in range(DEPTH):
        lw = (norm_mix_g[l], norm_ffn_g[l], w_ada[l], b_ada[l], w_in[l], w_branch_a[l], w_branch_b[l], w_out[l],
              w_router[l], b_router[l], w_gate_up[l], b_gate_up[l], w_down[l], b_down[l])
        hp, (kk, vv, ii, rr) = _layer(hp, c_prompt, pos_p, _dsa_prompt, _retention_prompt, *lw)
        k_p.append(kk); v_p.append(vv); ik_p.append(ii); r_p.append(rr)
        attend_s = functools.partial(_dsa_sample, cache_k=cache_k[l], cache_v=cache_v[l],
                                     cache_ik=cache_ik[l], page_table=page_table)
        retain_s = functools.partial(_retention_sample, state=state_ret[l])
        hs, (kk, vv, ii, rr) = _layer(hs, c_sample, pos_s, attend_s, retain_s, *lw)
        k_s.append(kk); v_s.append(vv); ik_s.append(ii); r_s.append(rr)
    y_prompt = _rmsnorm(hp, norm_final_g)
    y_sample = _rmsnorm(hs, norm_final_g)
    return (y_prompt, y_sample, jnp.stack(k_p), jnp.stack(v_p), jnp.stack(ik_p), jnp.stack(r_p),
            jnp.stack(k_s), jnp.stack(v_s), jnp.stack(ik_s), jnp.stack(r_s))


_drawn_inputs = setup_inputs


def setup_inputs(seed=0):
    import zlib

    import numpy as np

    out = dict(_drawn_inputs(seed))
    spreads = {}
    factors = {'norm_mix_g': 3.977,
     'norm_ffn_g': 3.512,
     'norm_final_g': 32.015,
     'b_router': 4.116,
     'b_gate_up': 8.0,
     'b_down': 59.28}
    for name, (base, spread) in spreads.items():
        noise = np.random.default_rng([zlib.crc32(name.encode()), seed]).standard_normal(out[name].shape)
        drawn = base * np.exp(spread * noise) if base else spread * noise
        out[name] = __import__('jax').numpy.asarray(drawn.astype(out[name].dtype))
    for name, factor in factors.items():
        out[name] = (out[name] * factor).astype(out[name].dtype)
    return out
```

```python
from contextlib import ExitStack

import numpy as np

import concourse.bass as bass
from concourse import mybir

F32 = mybir.dt.float32
BF16 = mybir.dt.bfloat16
I32 = mybir.dt.int32
U32 = mybir.dt.uint32
ALU = mybir.AluOpType
ACT = mybir.ActivationFunctionType
AX = mybir.AxisListType

P = 128
D = 1024
KT = D // P
SEQ = 256
DB, DS = 8, 8
NS = DB * DS
NPOOL = 80
PAST, PAGE = 1024, 128
NPAGES = PAST // PAGE
KEYS = PAST + DS
NE, TOPK, DFF = 32, 4, 1024
TOK = (P, P, NS)
NTOK = SEQ + NS
BANK = 512
EPS, GN_EPS = 1e-6, 1e-5
ATT_SCALE = 64 ** -0.5
NEG = -1.0e30
TAKEN = -3.0e38

CQ, CK, CV, CIQ, CIK, CIW, CRQ, CRK, CRV, CRG, CGA, CGB, DIN = (
    0, 512, 640, 768, 1280, 1344, 1352, 1864, 2376, 3400, 4424, 5448, 6472)
NZT = 13
LASTW = DIN - 12 * BANK

CAP = 64
XBLK = (NTOK * TOPK) // (CAP + 1)
NBLK = NE + XBLK


PIECES = ((0, 0), (2, 0), (0, 1), (1, 0), (1, 1))


def lg():
    return np.log(1.0 - 2.0 ** (-5.0 - np.arange(8, dtype=np.float64)))


def constants():
    t = {}
    t["ident"] = np.eye(P)
    pos = np.zeros((P, 3), np.float32)
    pos[:, 0] = np.arange(P)
    pos[:, 1] = P + np.arange(P)
    pos[:NS, 2] = PAST + np.arange(NS) % DS
    def rope(rot, theta):
        half = rot // 2
        inv = (theta ** (-np.arange(half) * 2.0 / rot)).astype(np.float32)
        ang = (pos[:, :, None] * inv).astype(np.float32).astype(np.float64)
        return np.cos(ang).reshape(P, -1), np.sin(ang).reshape(P, -1)
    t["cosq"], t["sinq"] = rope(16, 500000.0)
    t["cosr"], t["sinr"] = rope(64, 10000.0)
    r = np.arange(P)
    t["selp"] = np.tile(((r % 32 == 0) | (r == 9))[:, None], (1, P))
    t["sels"] = ((r % 32)[:, None] == 1 + np.arange(NS)[None, :] // DS) | (r == 9)[:, None]
    i = np.arange(P)
    kdec = np.zeros((P, 3, 8))
    kdec[:, 0] = kdec[:, 1] = np.exp((P - 1.0 - i)[:, None] * lg()) / 8
    kdec[:NS, 2] = np.exp((DS - 1.0 - np.arange(NS) % DS)[:, None] * lg()) / 8
    t["kdec"] = kdec.reshape(P, -1)
    t["qdecs"] = np.tile(np.exp((np.arange(DS) + 1.0)[None, :] * lg()[:, None]).reshape(1, -1), (P, 1))
    gc = np.zeros((P, 4))
    for c in range(4):
        gc[:64, c], gc[64:, c] = np.exp(P * lg()[2 * c]), np.exp(P * lg()[2 * c + 1])
    t["gchunk"] = gc
    bm = np.zeros((P, DB))
    bm[:NS] = np.arange(NS)[:, None] // DS == np.arange(DB)
    t["bm"] = bm
    dm = np.zeros((P, DS))
    dm[:NS] = np.arange(NS)[:, None] % DS == np.arange(DS)
    t["dm"] = dm
    cap = np.full((P, DS), 3.0e38)
    for q in range(NS):
        cap[q, q % DS + 1:] = NEG
    t["caps"] = cap
    sel = np.zeros((P, 120))
    sel[np.arange(NS), 56 + np.arange(NS) % DS] = 1
    t["selw"] = sel
    rep = np.zeros((P, NS))
    rep[:NS] = np.arange(NS)[:, None] % DS == np.arange(NS)[None, :] % DS
    t["rept"] = rep
    t["tri"] = r[:, None] < r[None, :]
    t["ones"] = np.ones((P, P))
    t["iota"] = np.tile(np.arange(CAP)[None, :], (P, 1))
    t["pcol"] = r[:, None] - NE * np.arange(4)[None, :]
    out, at = {}, 0
    cols = []
    for k, v in t.items():
        v = np.asarray(v, np.float32).reshape(P, -1)
        out[k] = (at, v.shape[1])
        cols.append(v)
        at += v.shape[1]
    return out, np.ascontiguousarray(np.concatenate(cols, 1))


CONST_AT, CONST = constants()


def decay_tables():
    i = np.arange(P)
    diff = i[None, :] - i[:, None]
    p = np.where(diff[:, None, :] >= 0, np.exp(np.maximum(diff, 0)[:, None, :] * lg()[None, :, None]), 0.0) / 8
    s = np.zeros((P, 8, NS))
    j = np.arange(NS)
    same = (j[:, None] // DS == j[None, :] // DS) & (j[None, :] >= j[:, None])
    d = np.maximum(j[None, :] - j[:, None], 0)
    s[:NS] = np.where(same[:, None, :], np.exp(d[:, None, :] * lg()[None, :, None]), 0.0) / 8
    q = np.zeros((P, 4, P))
    for c in range(4):
        for h in range(2):
            q[64 * h:64 * h + 64, c] = np.exp((i + 1.0) * lg()[2 * c + h])
    return [np.ascontiguousarray(x.reshape(P, -1), np.float32) for x in (p, s, q)]


def kern(nc, a):
    with ExitStack() as ctx:
        def sb(name, words, dt=F32):
            return ctx.enter_context(nc.sbuf_tensor(name, [P, words], dt))

        def sem(name):
            return ctx.enter_context(nc.semaphore(name))

        ring = sb("ring", 12 * 2048)
        z = sb("z", 3 * DIN)
        xr = sb("xr", 3 * D)
        actT = sb("actT", KT * NTOK)
        aT = sb("aT", 4 * NTOK)
        cst = sb("cst", CONST.shape[1])
        cT = sb("cT", KT * 32)
        st = sb("st", 96)
        rep_b = sb("rep_b", 512, BF16)
        pt = sb("pt", DB * NPAGES, I32)
        ps = ctx.enter_context(nc.psum_tensor("ps", [P, 8 * BANK], F32))

        def const(name):
            at, n = CONST_AT[name]
            return cst[:, at:at + n]

        def bank(b, n=1):
            return ps[:, b * BANK:(b + n) * BANK]

        z3 = z[:, :].rearrange("p (t n) -> p t n", t=3)
        x3 = xr[:, :].rearrange("p (t n) -> p t n", t=3)
        hT = actT[:, :].rearrange("p (k n) -> p k n", k=KT)
        cT3 = cT[:, :].rearrange("p (k n) -> p k n", k=KT)
        wt = [ring[:, s * 4096:(s + 1) * 4096].rearrange("p (k n) -> p k n", k=KT) for s in range(2)]
        S0 = 8192
        def scr(at, n):
            return ring[:, S0 + at:S0 + at + n]
        partA = scr(0, 2048)
        a1p, a1s = scr(2048, 1024), scr(3072, 1024)
        hrow = scr(4096, 3072).rearrange("p (t n) -> p t n", t=3)
        gmix = scr(7168, 1024)
        junk = scr(8192, 1024)
        ident = const("ident")
        sc_s = scr(0, KEYS)
        sc_p = scr(1032, 512).rearrange("p (t n) -> p t n", t=2)
        mask_s = scr(1544, 516).bitcast(BF16)
        mask_p = scr(2060, 512).rearrange("p (t n) -> p t n", t=2)
        kbd = scr(2572, 512).rearrange("p (j n) -> p j n", j=2)
        ikbd = scr(3084, 512).rearrange("p (j n) -> p j n", j=2)
        ikTn = scr(3596, NTOK)
        kTn = scr(3916, NTOK)
        iwx, iwcol = scr(4236, 64), scr(4300, 8)
        vnew = scr(4308, 1024).rearrange("p (b n) -> p b n", b=DB)
        ikn = [scr(5332 + 1024 * s, 1024).rearrange("p (n j d) -> p n j d", n=NPAGES, j=2) for s in range(2)]
        ikT = [scr(7380 + KEYS * s, KEYS) for s in range(2)]
        rel_s = scr(9444, KEYS)
        rel_p = [scr(12288, 1024).rearrange("p (h n) -> p h n", h=8), scr(13312, 2048).rearrange("p (h n) -> p h n", h=8)]
        aT3 = aT[:, :].rearrange("p (c n) -> p c n", c=4)
        kvn = [scr(at, 2048).rearrange("p (n d) -> p n d", n=NPAGES) for at in (5332, 9444, 12288, 14336)]
        kT = [scr(7380 + KEYS * s, KEYS) for s in range(2)]
        p_s = scr(0, KEYS)
        pT_s = scr(11492, 576).rearrange("p (n q) -> p n q", q=NS)
        p_p = scr(12288, 2048).rearrange("p (h n) -> p h n", h=8)
        pT_p = scr(14336, 2048).rearrange("p (s h n) -> p s h n", s=2, h=8)
        rot = [scr(12288 + 512 * i, 512).rearrange("p (h n) -> p h n", h=16) for i in range(4)]
        mx, nm, rs = st[:, 48:56], st[:, 56:64], st[:, 64:72]
        partB = [z3[:, 2, 768:1280]] + [actT[:, 512 * i:512 * i + 512] for i in range(5)] + [
            z3[:, 0, 768:1280], z3[:, 1, 768:1280]]
        qm = scr(0, 2048).rearrange("p (h e n) -> p h e n", h=8, e=4)
        km = [scr(2048 + 1024 * i, 1024).rearrange("p (h b d) -> p h b d", h=8, b=2) for i in range(2)]
        state = scr(4096, 4096).rearrange("p (e h v) -> p e h v", e=4, h=8)
        rbd = scr(8192, 1024).rearrange("p (c j n) -> p c j n", c=4, j=2)
        rkT = scr(9216, 512).rearrange("p (c n) -> p c n", c=4)
        rqdec = scr(9728, 512).rearrange("p (c n) -> p c n", c=4)
        sT = scr(10240, 1024).rearrange("p (h n) -> p h n", h=8)
        sbd = scr(11264, 1024).rearrange("p (c j n) -> p c j n", c=4, j=2)
        s1 = scr(12288, 512).rearrange("p (c n) -> p c n", c=4)
        rkd = scr(12800, 512).rearrange("p (h d) -> p h d", h=8)
        rT = scr(13312, 2560).rearrange("p (k n) -> p k n", k=KT)
        gst, gmv = scr(15872, 48).rearrange("p (h n) -> p h n", h=8), scr(15920, 16).rearrange("p (h n) -> p h n", h=8)
        dec_a, dec_b, qdec_p, dec_s = z3[:, 0, 0:768], z3[:, 1, 0:256], z3[:, 1, 256:768], z3[:, 2, 0:512]
        gt1p, a2p = z3[:, 0, 1352:2376], z3[:, 0, 2376:3400]
        sh2p, gt1s = z3[:, 1, 1352:2376], z3[:, 1, 2376:3400]
        a2s, sh2s = z3[:, 2, 1352:2376], z3[:, 2, 2376:3400]
        gt2p, gt2s = a2s, sh2s
        gffn, gfin = aT[:, 0:1024], sh2p
        h2 = z3[:, :, CRG:CGA]
        tmp3 = z3[:, :, CGB:DIN]
        wr = cT3
        br = aT[:, 1024:1024 + NE]
        def rt(at, n):
            return z3[:, 1, 2376 + at:2376 + at + n]
        lgt, lrep, ex, sel_m, gate_r = (rt(96 * i, 96).rearrange("p (t e) -> p t e", t=3) for i in range(5))
        m8r, m8s, nmr, srt = rt(480, 24), rt(504, 8), rt(512, 3), rt(516, 3)
        cnt, extra, cum, cum2, tot = rt(520, 32), rt(552, 32), rt(584, 32), rt(616, 32), rt(648, 32)
        rx, eidx = rt(680, XBLK), rt(700, XBLK)
        pos_x = rt(720, 3 * XBLK).rearrange("p (t i) -> p t i", t=3)
        gate_x = rt(780, 3 * XBLK).rearrange("p (t i) -> p t i", t=3)
        sel_x = rt(840, 4 * XBLK).rearrange("p (q i) -> p q i", q=4)
        oh = z3[:, 0, 1352:1352 + XBLK * NE].rearrange("p (i e) -> p i e", i=XBLK)
        oh2 = z3[:, 0, 0:XBLK * NE].rearrange("p (i e) -> p i e", i=XBLK)
        gT = aT[:, 0:3 * P]
        bdn = a2p
        ring3 = [ring[:, 2048 * ((k + 4) % 12):2048 * ((k + 4) % 12 + 1)] for k in range(12)]
        acc = tmp3
        xT, xg, aTt, ysb = z3[:, 0, CGA:CGA + 512], z3[:, 1, CGA:CGA + 512], z3[:, 1, CGA + 512:CGB], z3[:, 2, CGA:CGB]
        gb, ub, sgm, bgu = (actT[:, 512 * i:512 * i + 512] for i in range(4))
        ebuf = actT[:, 2048:2304].rearrange("p (q n) -> p q n", q=4)
        S = actT[:, 2304:2496].rearrange("p (t n) -> p t n", t=3)
        Sg = aT[:, 384:768].rearrange("p (t n) -> p t n", t=3)
        SgT = aT[:, 768:1088]
        pos_r = aT[:, 1088:1184].rearrange("p (t e) -> p t e", t=3)
        ikd = scr(15360, 384).rearrange("p (t n) -> p t n", t=3)
        t1, t2, t3, t4 = (scr(10500 + 240 * i, 240).rearrange("p (t h n) -> p t h n", t=3, n=8) for i in range(4))

        w_here = [sem("w_here0"), sem("w_here1")]
        c_here, x_here, g_here, b_here = sem("c_here"), sem("x_here"), sem("g_here"), sem("b_here")
        zeroed, z_zeroed = sem("zeroed"), sem("z_zeroed")
        ct_sig, ct_done = sem("ct_sig"), sem("ct_done")
        tile_done = sem("tile_done")
        part_done, tab_done = sem("part_done"), sem("tab_done")
        ss_done, var_done, rstd_done = sem("ss_done"), sem("var_done"), sem("rstd_done")
        dve_step = sem("dve_step")
        h_done, hT_ready, hT_done = sem("h_done"), sem("hT_ready"), sem("hT_done")
        z_done = sem("z_done")
        o_sem = sem("o_sem")
        pt_here = sem("pt_here")
        ik_here = [sem("ik_here0"), sem("ik_here1")]
        ikd_done, qk_roped = sem("ikd_done"), sem("qk_roped")
        tr_done, tr_act, tr_dve = sem("tr_done"), sem("tr_act"), sem("tr_dve")
        iwx_done, iw_mm, iw_done = sem("iwx_done"), sem("iw_mm"), sem("iw_done")
        pdot_done, prel_done, psc_done, pcap_done = sem("pdot_done"), sem("prel_done"), sem("psc_done"), sem("pcap_done")
        ikt_tr, ikt_done, sdot_done, srel_done, ssel_done = (
            sem("ikt_tr"), sem("ikt_done"), sem("sdot_done"), sem("srel_done"), sem("ssel_done"))
        ssc_done, pmask_raw, masks_done = sem("ssc_done"), sem("pmask_raw"), sem("masks_done")
        rep_done = sem("rep_done")
        kv_here = [sem(f"kv_here{i}") for i in range(4)]
        vnew_here = sem("vnew_here")
        rot_done, pool_step = sem("rot_done"), sem("pool_step")
        psc2_done, pmx_done, pexp_done, pp_done = sem("psc2_done"), sem("pmx_done"), sem("pexp_done"), sem("pp_done")
        ppt_tr, ppt_done, ppv_done, pa_done = sem("ppt_tr"), sem("ppt_done"), sem("ppv_done"), sem("pa_done")
        kt_tr, kt_done, ssc2_done, smx_done, sexp_done, sp_done = (
            sem("kt_tr"), sem("kt_done"), sem("ssc2_done"), sem("smx_done"), sem("sexp_done"), sem("sp_done"))
        spt_tr, spt_done, spv_done, sa_done = sem("spt_tr"), sem("spt_done"), sem("spv_done"), sem("sa_done")
        partb_done, gates_done = sem("partb_done"), sem("gates_done")

        ya_mm, ya_done, yb_done = sem("ya_mm"), sem("ya_done"), sem("yb_done")
        kvo, dec_here, st_here, b2_here = sem("kvo"), sem("dec_here"), sem("st_here"), sem("b2_here")
        r_tr, r_ops, r_kT, r_sc, r_sT, r_o, r_gn = (sem(n) for n in ("r_tr", "r_ops", "r_kT", "r_sc", "r_sT", "r_o", "r_gn"))
        rkd_done, r_st, r_s1, gn_var, km_done, ns_mm, ns_done, st_scaled, retp_done = (sem(n) for n in (
            "rkd_done", "r_st", "r_s1", "gn_var", "km_done", "ns_mm", "ns_done", "st_scaled", "retp_done"))
        rows_tr, rows_done, tb_mm, tb_out = sem("rows_tr"), sem("rows_done"), sem("tb_mm"), sem("tb_out")
        gb_sig, x1_done, ss2_done = sem("gb_sig"), sem("x1_done"), sem("ss2_done")
        gf_here, rw_here, h2_done = sem("gf_here"), sem("rw_here"), sem("h2_done")
        lg_mm, m0_done, ex_done, selm_done, pos_mm, gate_done = (sem(n) for n in (
            "lg_mm", "m0_done", "ex_done", "selm_done", "pos_mm", "gate_done"))
        gT_tr, gT_done, ainit_mm, g2_mm, g2_done, late_here, bias_here, flag_done = (sem(n) for n in (
            "gT_tr", "gT_done", "ainit_mm", "g2_mm", "g2_done", "late_here", "bias_here", "flag_done"))
        chunk_here = [sem(f"chunk_here{k}") for k in range(12)]
        chunk_used = sem("chunk_used")
        s_done, sg_done, ebuf_done, x_mm, xg_done, xt_tr, xt_done = (sem(n) for n in (
            "s_done", "sg_done", "ebuf_done", "x_mm", "xg_done", "xt_tr", "xt_done"))
        sgt_tr, sgt_done, g_done, u_done, sig_done, act_done, at_tr, at_done, y_done, cmb_mm, acc_done = (sem(n) for n in (
            "sgt_tr", "sgt_done", "g_done", "u_done", "sig_done", "act_done", "at_tr", "at_done", "y_done", "cmb_mm", "acc_done"))
        ssf_done, yf_done, mul_done, fin_step = sem("ssf_done"), sem("yf_done"), sem("mul_done"), sem("fin_step")

        w_ada = a["w_ada"].rearrange("(k p) n -> p k n", p=P)
        w_in = a["w_in"].rearrange("(k p) n -> p k n", p=P)

        block = ctx.enter_context(nc.Block())

        @block.sync
        def _(sp):
            for i in range(4):
                if i >= 2:
                    sp.wait_ge(tile_done, i - 1)
                sp.dma_start(wt[i % 2], w_ada[:, :, i * BANK:(i + 1) * BANK]).then_inc(w_here[i % 2], 16)
            def load_z_tiles(first, last):
                with sp.Fori(first, last) as it:
                    for s in range(2):
                        sp.wait_ge(tile_done, it * 2 + (3 + s))
                        sp.dma_start(wt[s], w_in[:, :, bass.ds(it * 1024 + s * BANK, BANK)]).then_inc(w_here[s], 16)

            def load_index_keys(b):
                if b == 0:
                    sp.wait_ge(pt_here, 16)
                if b >= 2:
                    sp.wait_ge(ikt_tr, 2 * (b - 1))
                for n in range(NPAGES):
                    page = sp.value_load(pt[0:1, b * NPAGES + n:b * NPAGES + n + 1], min_val=0, max_val=NPOOL - 1)
                    src = a["cache_ik"][bass.ds(page, 1)].rearrange("a s d -> (a s) d")
                    sp.dma_start(ikn[b % 2][:, n, :, :], src.unsqueeze(1).broadcast_to([P, 2, 64])).then_inc(
                        ik_here[b % 2], 16)

            load_z_tiles(0, 1)
            sp.wait_ge(hT_ready, 6)
            load_index_keys(0)
            load_index_keys(1)
            load_z_tiles(1, 4)
            for b in range(2, DB):
                load_index_keys(b)
            load_z_tiles(4, 6)
            sp.wait_ge(tile_done, 15)
            sp.dma_start(wt[0][:, :, 0:LASTW], w_in[:, :, 12 * BANK:DIN]).then_inc(w_here[0], 16)

            def load_tile(n, src, dst=None):
                sp.wait_ge(tile_done, n - 1)
                sp.dma_start(wt[n % 2] if dst is None else dst, src).then_inc(w_here[n % 2], 16)

            def load_attention_keys(b):
                if b == 0:
                    sp.wait_ge(ikt_tr, 2 * DB)
                if b == 1:
                    sp.wait_ge(ssel_done, DB)
                if b == 2:
                    sp.wait_ge(ppv_done, 2)
                if b >= 4:
                    sp.wait_ge(spv_done, b - 3)
                for n in range(NPAGES):
                    page = sp.value_load(pt[0:1, b * NPAGES + n:b * NPAGES + n + 1], min_val=0, max_val=NPOOL - 1)
                    sp.dma_start(kvn[b % 4][:, n, :], a["cache_kv"][bass.ds(page, 1)].rearrange("a s d -> (a s) d")).then_inc(
                        kv_here[b % 4], 16)

            for b in range(DB):
                sp.dma_start(vnew[0:DS, b, :], z3[b * DS:(b + 1) * DS, 2, CV:CIQ]).then_inc(vnew_here, 16)
            load_attention_keys(0)
            load_attention_keys(1)
            for b in range(DB):
                load_tile(17 + b, w_ada[:, :, (4 + b) * BANK:(5 + b) * BANK])
                if b == 1:
                    load_attention_keys(2)
                    load_attention_keys(3)
                if b >= 2 and b + 2 < DB:
                    load_attention_keys(b + 2)
            outs = 0
            for dst, c0, c1 in (("k", CK, CV), ("v", CV, CIQ), ("ik", CIK, CIW)):
                sp.dma_start(a[dst + "_prompt"].rearrange("(t p) n -> p t n", p=P), z3[:, 0:2, c0:c1]).then_inc(kvo, 16)
                sp.dma_start(a[dst + "_sample"], z3[0:NS, 2, c0:c1]).then_inc(kvo, 16)
            sp.wait_ge(kvo, 96)
            sp.wait_ge(ssc2_done, DB)
            sp.dma_start(dec_a, a["dec_p"][:, 0:768]).then_inc(dec_here, 16)
            sp.dma_start(dec_b, a["dec_p"][:, 768:1024]).then_inc(dec_here, 16)
            sp.dma_start(qdec_p, a["qdec_p"]).then_inc(dec_here, 16)
            sp.dma_start(dec_s, a["dec_s"]).then_inc(dec_here, 16)
            sp.wait_ge(partb_done, DB)
            for i in range(8):
                sp.dma_start(partB[i][9:10, :], a["b_ada"][:, (4 + i) * BANK:(5 + i) * BANK]).then_inc(b2_here, 16)
            wta = ring[:, 4096:8192].rearrange("p (c n) -> p c n", c=4)
            load_tile(25, a["w_branch_a"].rearrange("(c p) n -> p c n", p=P), wta)
            sp.wait_ge(spv_done, DB)
            for b in range(DB):
                sp.dma_start(state[64 * (b % 2):64 * (b % 2) + 64, b // 2, :, :],
                             a["state"][b].rearrange("h d v -> d h v")).then_inc(st_here, 16)
            w_b = a["w_branch_b"].rearrange("(k p) n -> p k n", p=P)
            w_o = a["w_out"].rearrange("(k p) n -> p k n", p=P)
            load_tile(26, w_b[:, :, 0:BANK])
            sp.dma_start(wr, a["w_router"].rearrange("(k p) e -> p k e", p=P)).then_inc(rw_here, 16)
            load_tile(27, w_b[:, :, BANK:D])
            sp.dma_start(br, a["b_router"].partition_broadcast(P)).then_inc(rw_here, 16)
            sp.dma_start(gffn, a["norm_ffn_g"].partition_broadcast(P)).then_inc(gf_here, 16)
            sp.wait_ge(retp_done, 1)
            sp.dma_start(a["ret_prompt"].rearrange("(c j) d v -> (j d) c v", j=2), s1).then_inc(kvo, 16)
            for b in range(DB):
                sp.wait_ge(ns_done, b // 2 + 1)
                sp.dma_start(a["ret_sample"][b].rearrange("h d v -> d h v"),
                             state[64 * (b % 2):64 * (b % 2) + 64, b // 2, :, :]).then_inc(kvo, 16)
            load_tile(28, w_o[:, :, 0:BANK])
            load_tile(29, w_o[:, :, BANK:D])
            sp.wait_ge(kvo, 16 * (7 + DB))

            def chunk(e, k):
                if k < 8:
                    return sp.dma_start(ring3[k], a["w_gate_up"][bass.ds(e, 1), k * P:(k + 1) * P, :].rearrange(
                        "a p n -> (a p) n")).then_inc(chunk_here[k], 16)
                r = (k - 8) * 256
                return sp.dma_start(ring3[k].rearrange("p (i n) -> p i n", i=2),
                                    a["w_down"][bass.ds(e, 1), r:r + 256, :].rearrange(
                                        "a (i p) n -> p (a i) n", p=P)).then_inc(chunk_here[k], 16)

            for k in range(8):
                chunk(0, k)
            sp.wait_ge(h2_done, 3)
            sp.dma_start(bdn[0:NE], a["b_down"]).then_inc(late_here, 16)
            sp.dma_start(gfin, a["norm_final_g"].partition_broadcast(P)).then_inc(late_here, 16)
            sp.wait_ge(tile_done, 29)
            chunk(0, 8)
            chunk(0, 9)
            sp.wait_ge(tile_done, 30)
            chunk(0, 10)
            chunk(0, 11)
            sp.wait_ge(lg_mm, 1)
            sp.dma_start(bgu, a["b_gate_up"]).then_inc(bias_here, 16)
            with sp.Fori(1, NE) as e:
                for k in range(12):
                    sp.wait_ge(chunk_used, e * 12 + (k - 11))
                    chunk(e, k)
            sp.wait_ge(flag_done, 1)
            more = sp.value_load(pt[0:1, 0:1], min_val=0, max_val=XBLK)
            with sp.If(more > 0):
                sp.wait_ge(flag_done, 2)
                with sp.Fori(0, XBLK) as i:
                    e = sp.value_load(pt[0:1, bass.ds(i + 8, 1)], min_val=0, max_val=NE - 1)
                    for k in range(12):
                        sp.wait_ge(chunk_used, i * 12 + (12 * NE + k - 11))
                        chunk(e, k)
            for t in range(3):
                sp.wait_ge(yf_done, t + 1)
                dst = a["y_prompt"][t * P:(t + 1) * P, :] if t < 2 else a["y_sample"]
                sp.dma_start(dst, x3[0:TOK[t], t, :]).then_inc(o_sem, 16)
            sp.wait_ge(o_sem, 48)

        @block.gpsimd
        def _(pool):
            nc.gpsimd.memset(st[:, :], 1.0).then_inc(zeroed, 1)

            pool.wait_ge(g_here, 32)
            for b in range(DB):
                nc.gpsimd.tensor_scalar(rep_b[0:NS, b * NS:(b + 1) * NS], const("rept")[0:NS], const("bm")[0:NS, b:b + 1],
                                        None, ALU.mult).then_inc(rep_done, 1)
            for t in range(2):
                w = (t + 1) * P
                pool.wait_ge(psc_done, t + 1)
                nc.gpsimd.affine_select(out=sc_p[:, t, 0:w], in_=sc_p[:, t, 0:w], compare_op=ALU.is_ge, fill=NEG,
                                        base=t * P, pattern=[[-1, w]], channel_multiplier=1).then_inc(pcap_done, 1)
            pool.wait_ge(z_done, 5)
            pool.wait_ge(psc_done, 2)
            n_pool = 0
            for t in range(3):
                v = z3[:, t, CRQ:CRV].rearrange("p (h d) -> p h d", d=64)
                x1, x2 = v[:, :, 0:32], v[:, :, 32:64]
                cos, sin = (const(n).rearrange("p (t n) -> p t n", t=3)[:, t, :].unsqueeze(1).broadcast_to([P, 16, 32])
                            for n in ("cosr", "sinr"))
                for dst, x, w in ((rot[0], x1, cos), (rot[1], x2, sin), (rot[2], x2, cos), (rot[3], x1, sin)):
                    nc.gpsimd.tensor_tensor(dst, x, w, ALU.mult).then_inc(pool_step, 1)
                n_pool += 4
                pool.wait_ge(pool_step, n_pool)
                nc.gpsimd.tensor_tensor(x1, rot[0], rot[1], ALU.subtract).then_inc(pool_step, 1)
                nc.gpsimd.tensor_tensor(x2, rot[2], rot[3], ALU.add).then_inc(rot_done, 1)
                n_pool += 1
                pool.wait_ge(rot_done, t + 1)
            for t in range(2):
                w = (t + 1) * P
                pool.wait_ge(pmask_raw, t + 1)
                nc.gpsimd.affine_select(out=mask_p[:, t, 0:w], in_=mask_p[:, t, 0:w], compare_op=ALU.is_ge, fill=NEG,
                                        base=t * P, pattern=[[-1, w]], channel_multiplier=1).then_inc(pcap_done, 1)

            pool.wait_ge(spv_done, DB)
            for t in range(3):
                n = TOK[t]
                if t:
                    pool.wait_ge(r_st, t)
                kd = const("kdec").rearrange("p (t h) -> p t h", t=3)[0:n, t, :].unsqueeze(2).broadcast_to([n, 8, 64])
                nc.gpsimd.tensor_tensor(rkd[0:n], z3[0:n, t, CRK:CRV].rearrange("p (h d) -> p h d", d=64), kd,
                                        ALU.mult).then_inc(rkd_done, 1)
            pool.wait_ge(rkd_done, 3)
            for e in range(4):
                if e >= 2:
                    pool.wait_ge(ns_mm, e - 1)
                for b in range(2):
                    last = nc.gpsimd.tensor_scalar(km[e % 2][0:NS, :, b, :], rkd[0:NS], const("bm")[0:NS, 2 * e + b:2 * e + b + 1],
                                                   None, ALU.mult)
                last.then_inc(km_done, 1)
                if e == 1:
                    pool.wait_ge(r_o, 3)
                    g8 = const("qdecs").rearrange("p (h t) -> p h t", h=8)[:, :, 7].unsqueeze(2).broadcast_to([P, 8, P])
                    for q in range(4):
                        nc.gpsimd.tensor_tensor(state[:, q], state[:, q], g8, ALU.mult).then_inc(st_scaled, 1)

        @block.scalar
        def _(act):
            act.dma_start(cT[:, :], a["cT"]).then_inc(c_here, 16)
            act.dma_start(cst[:, :], a["const"]).then_inc(g_here, 16)
            act.dma_start(pt[0:1, :], a["page_table"]).then_inc(pt_here, 16)
            for t in range(2):
                act.dma_start(x3[:, t, :], a["x_prompt"][0, t * P:(t + 1) * P, :]).then_inc(x_here, 16)
            act.dma_start(x3[0:NS, 2, :], a["x_sample"].rearrange("b t d -> (b t) d")).then_inc(x_here, 16)
            act.dma_start(gmix, a["norm_mix_g"].partition_broadcast(P)).then_inc(g_here, 16)
            act.wait_ge(c_here, 16)
            nc.scalar.activation(junk[:, 0:256], cT[:, :], ACT.Sigmoid).then_inc(ct_sig, 1)
            act.wait_ge(x_here, 48)
            act.wait_ge(ct_done, 1)
            act.wait_ge(zeroed, 1)
            for t in range(3):
                n = TOK[t]
                nc.scalar.activation(junk[0:n, :], x3[0:n, t, :], ACT.Square,
                                     accum_out=st[0:n, t:t + 1]).then_inc(ss_done, 1)
                act.wait_ge(ss_done, t + 1)
            act.wait_ge(part_done, 4)
            act.dma_start(partA[9:10, :], a["b_ada"][:, 0:2048]).then_inc(b_here, 16)
            act.wait_ge(var_done, 1)
            nc.scalar.activation(st[:, 3:6], st[:, 0:3], ACT.Sqrt).then_inc(rstd_done, 1)
            for t in range(3):
                n = TOK[t]
                b = (4, 6, 0)[t]
                for k in range(2):
                    act.wait_ge(hT_ready, 2 * t + k + 1)
                    nc.scalar.activation(
                        hT[:, 4 * k:4 * k + 4, t * P:t * P + n],
                        bank(b + k)[:, :].rearrange("p (k n) -> p k n", k=4)[:, :, 0:n],
                        ACT.Copy).then_inc(hT_done, 1)
            def evac(col, b, w):
                h = w // 2
                nc.scalar.activation(z3[:, 0, col(0, w)], bank(b)[:, 0:w], ACT.Copy)
                nc.scalar.activation(z3[:, 1, col(0, w)], bank(b + 1)[:, 0:w], ACT.Copy)
                nc.scalar.activation(z3[0:NS, 2, col(0, h)], bank(b + 2)[0:NS, 0:h], ACT.Copy)
                nc.scalar.activation(z3[0:NS, 2, col(h, h)], bank(b + 2)[NS:P, 0:h],
                                     ACT.Copy).then_inc(z_done, 1)
            act.wait_ge(z_zeroed, 1)

            def evac_tiles(first, last):
                with act.Fori(first, last) as it:
                    for s in range(2):
                        act.wait_ge(tile_done, it * 2 + (5 + s))
                        evac(lambda o, n: bass.ds(it * 1024 + (s * BANK + o), n), 3 * s, BANK)

            evac_tiles(0, 3)
            for i, (n, dst, b, w) in enumerate(((1, ikTn, 2, NTOK), (2, z3[:, 0, CIQ:CIK], 0, 512), (3, z3[:, 1, CIQ:CIK], 1, 512),
                                                (5, z3[:, 0, CQ:CK], 4, 512), (6, z3[:, 1, CQ:CK], 5, 512),
                                                (8, kTn, 7, NTOK))):
                act.wait_ge(tr_done, n)
                nc.scalar.activation(dst, bank(b)[:, 0:w], ACT.Copy).then_inc(tr_act, 1)
            act.wait_ge(pdot_done, 1)
            nc.scalar.activation(rel_p[0], bank(0, 2).rearrange("p (h n) -> p h n", h=8), ACT.Relu).then_inc(prel_done, 1)
            act.wait_ge(pdot_done, 2)
            nc.scalar.activation(rel_p[1], bank(4, 4).rearrange("p (h n) -> p h n", h=8), ACT.Relu).then_inc(prel_done, 1)
            for b in range(DB):
                if b >= 2:
                    act.wait_ge(sdot_done, b - 1)
                nc.scalar.activation(ikT[b % 2][:, PAST:KEYS], ikTn[:, SEQ + b * DS:SEQ + (b + 1) * DS], ACT.Copy)
                for i in range(2):
                    act.wait_ge(ikt_tr, 2 * b + i + 1)
                    nc.scalar.activation(ikT[b % 2][:, i * BANK:(i + 1) * BANK], bank(6 + i), ACT.Copy).then_inc(ikt_done, 1)
            act.wait_ge(ssel_done, DB)
            nc.scalar.activation(sc_s[0:NS], ps[0:NS, 0:KEYS], ACT.Copy).then_inc(ssc_done, 1)
            evac_tiles(3, 6)
            act.wait_ge(z_done, 12)
            for t in range(3):
                n = TOK[t]
                nc.scalar.activation(z3[0:n, t, CRG:CGA], z3[0:n, t, CRG:CGA], ACT.Silu).then_inc(gates_done, 1)
            for t in range(3):
                n = TOK[t]
                nc.scalar.activation(z3[0:n, t, CGA:CGB], z3[0:n, t, CGA:CGB], ACT.Sigmoid).then_inc(gates_done, 1)
            act.wait_ge(tile_done, 17)
            evac(lambda o, n: slice(12 * BANK + o, 12 * BANK + o + n), 0, LASTW)

            def keys_out(b):
                if b >= 2:
                    act.wait_ge(ssc2_done, b - 1)
                nc.scalar.activation(kT[b % 2][:, PAST:KEYS], kTn[:, SEQ + b * DS:SEQ + (b + 1) * DS], ACT.Copy)
                for i in range(2):
                    act.wait_ge(kt_tr, 2 * b + i + 1)
                    nc.scalar.activation(kT[b % 2][:, i * BANK:(i + 1) * BANK], bank(6 + i), ACT.Copy).then_inc(kt_done, 1)

            for t in range(2):
                w = (t + 1) * P
                act.wait_ge(pmx_done, t + 1)
                if t:
                    act.wait_ge(ppt_tr, 1)
                for g in range(8):
                    nc.scalar.activation(p_p[:, g, 0:w], p_p[:, g, 0:w], ACT.Exp, bias=nm[:, g:g + 1], scale=ATT_SCALE,
                                         accum_out=rs[:, g:g + 1]).then_inc(pexp_done, 1)
                act.wait_ge(ppt_tr, t + 1)
                b0 = (4, 0)[t]
                if t:
                    act.wait_ge(ppv_done, 1)
                nc.scalar.activation(pT_p[:, 0:t + 1, :, :], bank(b0, 2 * (t + 1)).rearrange("p (s h n) -> p s h n", h=8, n=P),
                                     ACT.Copy).then_inc(ppt_done, 1)
                act.wait_ge(ppv_done, t + 1)
                b0 = (6, 4)[t]
                v = bank(b0, 2).rearrange("p (c j n) -> p c j n", c=4, j=2)
                nc.scalar.activation(aT3[0:64, :, t * P:(t + 1) * P], v[0:64, :, 0, :], ACT.Copy)
                nc.scalar.activation(aT3[64:P, :, t * P:(t + 1) * P], v[64:P, :, 1, :], ACT.Copy).then_inc(pa_done, 1)
            keys_out(0)
            for b in range(DB):
                act.wait_ge(smx_done, b + 1)
                if b:
                    act.wait_ge(spt_tr, b)
                nc.scalar.activation(p_s[0:NS], ps[0:NS, 0:KEYS], ACT.Exp, bias=nm[0:NS, 0:1], scale=ATT_SCALE,
                                     accum_out=rs[0:NS, 0:1]).then_inc(sexp_done, 1)
                if b + 1 < DB:
                    keys_out(b + 1)
                act.wait_ge(spv_done, b + 1)
                v = bank(5)[:, 0:NS].rearrange("p (j c t) -> p j c t", j=2, c=4)
                o = aT3[:, :, SEQ + b * DS:SEQ + (b + 1) * DS]
                nc.scalar.activation(o[0:64], v[0:64, 0], ACT.Copy)
                nc.scalar.activation(o[64:P], v[64:P, 1], ACT.Copy).then_inc(sa_done, 1)

            for t in range(3):
                n = TOK[t]
                nc.scalar.activation(z3[0:n, t, CGB:DIN], z3[0:n, t, CGB:DIN], ACT.Sigmoid).then_inc(gb_sig, 1)
            for t in range(3):
                n = TOK[t]
                if t:
                    act.wait_ge(r_sc, t)
                else:
                    act.wait_ge(spv_done, DB)
                act.wait_ge(r_tr, 2 * t + 2)
                nc.scalar.activation(rkT[:, :, 0:n], bank(1)[:, 0:4 * n].rearrange("p (c n) -> p c n", c=4),
                                     ACT.Copy).then_inc(r_kT, 1)
                act.wait_ge(gn_var, t + 1)
                nc.scalar.activation(st[0:n, 24:32], st[0:n, 16:24], ACT.Sqrt).then_inc(rstd_done, 1)

            def transposed_out(turn, dst):
                for t in range(3):
                    n, b = TOK[t], (0, 2, 6)[t]
                    for i in range(2):
                        act.wait_ge(rows_tr, 6 * turn + 2 * t + i + 1)
                        nc.scalar.activation(dst[:, 4 * i:4 * i + 4, t * P:t * P + n],
                                             bank(b + i).rearrange("p (k n) -> p k n", k=4)[:, :, 0:n],
                                             ACT.Copy).then_inc(rows_done, 1)

            transposed_out(0, rT)
            for i, (dst, n) in enumerate(((gt1p, P), (gt1s, NS), (sh2p, P), (sh2s, NS), (a2p, P), (a2s, NS))):
                act.wait_ge(tb_mm, i + 1)
                nc.scalar.activation(dst[0:n], bank((0, 6)[i % 2], 2)[0:n], ACT.Copy).then_inc(tb_out, 1)
            transposed_out(1, hT)
            act.wait_ge(x1_done, 1)
            for t in range(3):
                n = TOK[t]
                nc.scalar.activation(z3[0:n, t, CGA:CGB], x3[0:n, t, :], ACT.Square,
                                     accum_out=st[0:n, 8 + t:9 + t]).then_inc(ss2_done, 1)
            act.wait_ge(var_done, 2)
            nc.scalar.activation(st[:, 11:14], st[:, 8:11], ACT.Sqrt).then_inc(rstd_done, 1)
            transposed_out(2, hT)
            act.wait_ge(m0_done, 1)
            for t in range(3):
                n = TOK[t]
                nc.scalar.activation(ex[0:n, t, :], lgt[0:n, t, :], ACT.Exp, bias=nmr[0:n, t:t + 1]).then_inc(ex_done, 1)
            act.wait_ge(gT_tr, 1)
            nc.scalar.activation(gT[0:NE], bank(7)[0:NE, 0:3 * P], ACT.Copy).then_inc(gT_done, 1)
            act.wait_ge(ainit_mm, 1)
            for t in range(3):
                nc.scalar.activation(acc[0:TOK[t], t, :], bank(2 * t, 2)[0:TOK[t]], ACT.Copy).then_inc(acc_done, 1)
            act.wait_ge(g2_mm, 1)
            nc.scalar.activation(gt2p, bank(6, 2), ACT.Copy).then_inc(g2_done, 1)
            act.wait_ge(g2_mm, 2)
            nc.scalar.activation(gt2s[0:NS], bank(0, 2)[0:NS], ACT.Copy).then_inc(g2_done, 1)

            def x_out(n):
                act.wait_ge(x_mm, n + 1)
                nc.scalar.activation(xg, bank(3), ACT.Copy).then_inc(xg_done, 1)

            def xt_out(n):
                act.wait_ge(xt_tr, n + 1)
                nc.scalar.activation(xT, bank(5), ACT.Copy).then_inc(xt_done, 1)

            def gather_out(n):
                act.wait_ge(sgt_tr, n + 1)
                nc.scalar.activation(SgT[0:NS, :], bank(4)[0:NS, 0:NTOK], ACT.Copy).then_inc(sgt_done, 1)

            def expert(n, first, last):
                if not first:
                    gather_out(n - 1)
                act.wait_ge(g_done, n + 1)
                nc.scalar.activation(sgm, gb, ACT.Sigmoid, scale=1.702).then_inc(sig_done, 1)
                if not last:
                    x_out(n + 1)
                    xt_out(n + 1)
                act.wait_ge(at_tr, n + 1)
                nc.scalar.activation(aTt, bank(4), ACT.Copy).then_inc(at_done, 1)
                act.wait_ge(chunk_used, n * 12 + 12)
                if not first:
                    act.wait_ge(cmb_mm, n * 5)
                nc.scalar.activation(ysb[0:NS, 0:512], bank(2)[0:NS], ACT.Copy)
                nc.scalar.activation(ysb[0:NS, 512:D], bank(2)[NS:P], ACT.Copy).then_inc(y_done, 1)

            def experts(count, base):
                x_out(base)
                xt_out(base)
                expert(base, True, False)
                with act.Fori(1, count - 1) as i:
                    expert(i + base, False, False)
                expert(base + count - 1, False, True)
                gather_out(base + count - 1)

            experts(NE, 0)
            act.wait_ge(flag_done, 1)
            more = act.value_load(pt[0:1, 0:1], min_val=0, max_val=XBLK)
            with act.If(more > 0):
                experts(XBLK, NE)
            act.wait_ge(x1_done, 2)
            for t in range(3):
                n = TOK[t]
                nc.scalar.activation(z3[0:n, t, CGA:CGB], x3[0:n, t, :], ACT.Square,
                                     accum_out=st[0:n, 8 + t:9 + t]).then_inc(ssf_done, 1)
            act.wait_ge(var_done, 3)
            nc.scalar.activation(st[:, 11:14], st[:, 8:11], ACT.Sqrt).then_inc(rstd_done, 1)

        @block.tensor
        def _(pe):
            pe.wait_ge(ct_done, 1)
            for i in range(4):
                pe.wait_ge(w_here[i % 2], 16 * (i // 2 + 1))
                for k in range(KT):
                    g = k % 4
                    last = nc.tensor.matmul(bank(i)[32 * g:32 * g + 32, :], cT3[:, k, :], wt[i % 2][:, k, :],
                                            start=k < 4, stop=k >= 4)
                last.then_inc(tile_done, 1)
            pe.wait_ge(b_here, 16)
            pe.wait_ge(g_here, 32)
            for sel, rows, b0 in ((const("selp"), P, 4), (const("sels"), NS, 0)):
                for j in range(4):
                    src = (j + 2) % 4
                    nc.tensor.matmul(bank(b0 + j)[0:rows, :], sel, partA[:, src * BANK:(src + 1) * BANK],
                                     start=True, stop=True).then_inc(tab_done, 1)
            for t in range(3):
                n = TOK[t]
                b = (4, 6, 0)[t]
                pe.wait_ge(h_done, t + 1)
                for k in range(KT):
                    last = nc.tensor.transpose(bank(b + k // 4)[:, (k % 4) * P:(k % 4) * P + n],
                                               hrow[0:n, t, k * P:(k + 1) * P], ident[0:n, 0:n])
                    if k % 4 == 3:
                        last.then_inc(hT_ready, 1)
            pe.wait_ge(hT_done, 6)

            def project(wtile, b, w, x=hT, kt=KT, done=tile_done):
                h = w // 2
                for k in range(kt):
                    se = dict(start=k == 0, stop=k == kt - 1)
                    nc.tensor.matmul(bank(b)[:, 0:w], x[:, k, 0:P], wtile[:, k, 0:w], **se)
                    nc.tensor.matmul(bank(b + 1)[:, 0:w], x[:, k, P:2 * P], wtile[:, k, 0:w], **se)
                    nc.tensor.matmul(bank(b + 2)[0:NS, 0:h], x[:, k, 2 * P:NTOK], wtile[:, k, 0:h], **se)
                    last = nc.tensor.matmul(bank(b + 2)[NS:P, 0:h], x[:, k, 2 * P:NTOK], wtile[:, k, h:w], **se)
                last.then_inc(done, 1)

            def project_tiles(first, last):
                with pe.Fori(first, last) as it:
                    for s in range(2):
                        pe.wait_ge(w_here[s], it * 16 + 48)
                        if first or s:
                            pe.wait_ge(z_done, it * 2 - (1 - s))
                        project(wt[s], 3 * s, BANK)

            pe.wait_ge(w_here[0], 48)
            project(wt[0], 0, BANK)
            pe.wait_ge(w_here[1], 48)
            project(wt[1], 3, BANK)
            project_tiles(1, 3)
            pe.wait_ge(z_done, 6)
            pe.wait_ge(ikd_done, 1)
            pe.wait_ge(qk_roped, 1)
            for t in range(3):
                n = TOK[t]
                last = nc.tensor.transpose(bank(2)[:, t * P:t * P + n], ikd[0:n, t, :], ident[0:n, 0:n])
            last.then_inc(tr_done, 1)
            for col, banks in ((CIQ, (0, 1, 3)), (CQ, (4, 5, 6))):
                for t in range(3):
                    n = TOK[t]
                    for c in range(4):
                        last = nc.tensor.transpose(bank(banks[t])[:, c * n:(c + 1) * n],
                                                   z3[0:n, t, col + c * P:col + (c + 1) * P], ident[0:n, 0:n])
                    last.then_inc(tr_done, 1)
            for t in range(3):
                n = TOK[t]
                last = nc.tensor.transpose(bank(7)[:, t * P:t * P + n], z3[0:n, t, CK:CV], ident[0:n, 0:n])
            last.then_inc(tr_done, 1)
            pe.wait_ge(tr_dve, 1)
            pe.wait_ge(tr_act, 3)
            for c in range(4):
                last = nc.tensor.matmul(bank(c // 2)[:, (c % 2) * 256:(c % 2 + 1) * 256],
                                        z3[:, 0, CIQ + c * P:CIQ + (c + 1) * P], ikbd[:, :, 0:P],
                                        start=True, stop=True)
            last.then_inc(pdot_done, 1)
            pe.wait_ge(tr_act, 6)
            pe.wait_ge(tr_dve, 3)
            for c in range(4):
                last = nc.tensor.matmul(bank(4 + c), z3[:, 1, CIQ + c * P:CIQ + (c + 1) * P], ikbd[:, :, :],
                                        start=True, stop=True)
            last.then_inc(pdot_done, 1)
            pe.wait_ge(iwx_done, 1)
            nc.tensor.matmul(bank(3)[0:NS, 0:DB], iwx[0:NS], const("bm")[0:NS], start=True, stop=True).then_inc(iw_mm, 1)

            def index_transpose(b):
                pe.wait_ge(ik_here[b % 2], 16 * NPAGES * (b // 2 + 1))
                for i in range(2):
                    if b:
                        pe.wait_ge(ikt_done, 2 * b - 1 + i)
                    else:
                        pe.wait_ge(prel_done, 2)
                    for n in range(4):
                        last = nc.tensor.transpose(bank(6 + i)[:, n * P:(n + 1) * P],
                                                   ikn[b % 2][:, 4 * i + n, :, :].rearrange("p j d -> p (j d)"), ident)
                    last.then_inc(ikt_tr, 1)

            iq_s = z3[:, 2, CIQ:CIK]
            index_transpose(0)
            pe.wait_ge(iw_done, 1)
            for b in range(DB):
                pe.wait_ge(ikt_done, 2 * b + 2)
                if b:
                    pe.wait_ge(srel_done, b)
                for i, w in ((0, BANK), (1, BANK), (2, DS)):
                    last = nc.tensor.matmul(bank(3 + i)[0:NS, 0:w], iq_s[:, b * NS:(b + 1) * NS],
                                            ikT[b % 2][:, i * BANK:i * BANK + w], start=True, stop=True)
                last.then_inc(sdot_done, 1)
                if b + 1 < DB:
                    index_transpose(b + 1)
                pe.wait_ge(srel_done, b + 1)
                for i, w in ((0, BANK), (1, BANK), (2, DS)):
                    last = nc.tensor.matmul(bank(i)[0:NS, 0:w], const("selw")[0:NS, 56 - DS * b:56 - DS * b + NS],
                                            rel_s[0:NS, i * BANK:i * BANK + w], start=b == 0, stop=b == DB - 1)
                last.then_inc(ssel_done, 1)
            pe.wait_ge(ssc_done, 1)
            project_tiles(3, 6)
            pe.wait_ge(w_here[0], 16 * 9)
            pe.wait_ge(z_done, 11)
            project(wt[0], 0, LASTW)

            def prompt_scores(t, b0):
                w = (t + 1) * P
                for c in range(4):
                    last = nc.tensor.matmul(ps[:, b0 * BANK + c * 2 * w:b0 * BANK + (c + 1) * 2 * w],
                                            z3[:, t, CQ + c * P:CQ + (c + 1) * P], kbd[:, :, 0:w], start=True, stop=True)
                last.then_inc(psc2_done, 1)

            def prompt_values(t, b0, b1):
                pe.wait_ge(pp_done, t + 1)
                for s in range(t + 1):
                    for g in range(8):
                        last = nc.tensor.transpose(ps[:, b0 * BANK + (8 * s + g) * P:b0 * BANK + (8 * s + g + 1) * P],
                                                   p_p[:, g, s * P:(s + 1) * P], ident)
                last.then_inc(ppt_tr, 1)
                pe.wait_ge(ppt_done, t + 1)
                for c in range(4):
                    for s in range(t + 1):
                        last = nc.tensor.matmul(ps[:, b1 * BANK + c * 256:b1 * BANK + (c + 1) * 256],
                                                z3[:, s, CV:CIQ], pT_p[:, s, 2 * c:2 * c + 2, :], start=s == 0, stop=s == t)
                last.then_inc(ppv_done, 1)

            pe.wait_ge(tr_dve, 4)
            pe.wait_ge(ikt_done, 2 * DB)
            prompt_scores(0, 6)
            pe.wait_ge(z_done, NZT)
            prompt_scores(1, 0)
            prompt_values(0, 4, 6)
            prompt_values(1, 0, 4)

            def key_transpose(b):
                pe.wait_ge(kv_here[b % 4], 16 * NPAGES * (b // 4 + 1))
                for i in range(2):
                    if b:
                        pe.wait_ge(kt_done, 2 * b - 1 + i)
                    else:
                        pe.wait_ge(pa_done, 1)
                    for n in range(4):
                        last = nc.tensor.transpose(bank(6 + i)[:, n * P:(n + 1) * P], kvn[b % 4][:, 4 * i + n, 0:P], ident)
                    last.then_inc(kt_tr, 1)

            key_transpose(0)
            pe.wait_ge(masks_done, 1)
            pe.wait_ge(rep_done, DB)
            pe.wait_ge(ppt_done, 2)
            pe.wait_ge(pa_done, 2)
            pe.wait_ge(vnew_here, 16 * DB)
            for b in range(DB):
                pe.wait_ge(kt_done, 2 * b + 2)
                if b:
                    pe.wait_ge(sexp_done, b)
                for i, w in ((0, BANK), (1, BANK), (2, DS)):
                    nc.tensor.matmul(bank(i)[0:NS, 0:w], z3[:, 2, CQ + b * NS:CQ + (b + 1) * NS],
                                     kT[b % 2][:, i * BANK:i * BANK + w], start=True, stop=False)
                    last = nc.tensor.matmul(bank(i)[0:NS, 0:w], rep_b[0:NS, b * NS:(b + 1) * NS],
                                            mask_s[0:NS, i * BANK:i * BANK + w], start=False, stop=True)
                last.then_inc(ssc2_done, 1)
                n = 17 + b
                pe.wait_ge(w_here[n % 2], 16 * (n // 2 + 1))
                if b:
                    pe.wait_ge(partb_done, b)
                for k in range(KT):
                    g = k % 4
                    last = nc.tensor.matmul(bank(4)[32 * g:32 * g + 32, :], cT3[:, k, :], wt[n % 2][:, k, :],
                                            start=k < 4, stop=k >= 4)
                last.then_inc(tile_done, 1)
                if b + 1 < DB:
                    key_transpose(b + 1)
                pe.wait_ge(sp_done, b + 1)
                if b:
                    pe.wait_ge(sa_done, b)
                for n in range(NPAGES):
                    nc.tensor.transpose(bank(3)[:, n * NS:(n + 1) * NS], p_s[0:NS, n * P:(n + 1) * P], ident[0:NS, 0:NS])
                nc.tensor.transpose(bank(5)[0:DS, NS:2 * NS], p_s[0:NS, PAST:KEYS], ident[0:NS, 0:NS]).then_inc(spt_tr, 1)
                pe.wait_ge(spt_done, b + 1)
                for n in range(NPAGES):
                    nc.tensor.matmul(bank(5)[:, 0:NS], kvn[b % 4][:, n, P:2 * P], pT_s[:, n, :], start=n == 0, stop=False)
                nc.tensor.matmul(bank(5)[:, 0:NS], vnew[0:DS, b, :], pT_s[0:DS, NPAGES, :],
                                 start=False, stop=True).then_inc(spv_done, 1)

            pe.wait_ge(sa_done, DB)
            pe.wait_ge(sp_done, DB)
            pe.wait_ge(w_here[1], 16 * 13)
            wt_a = ring[:, 4096:8192].rearrange("p (c n) -> p c n", c=4)
            project(wt_a[:, :, 0:BANK], 0, BANK, aT3, 4, ya_mm)
            project(wt_a[:, :, BANK:D], 3, BANK, aT3, 4)
            pe.wait_ge(ya_done, 2)
            for t in range(3):
                n = TOK[t]
                if t:
                    pe.wait_ge(r_ops, t)
                    pe.wait_ge(r_kT, t)
                for b, col in ((0, CRQ), (1, CRK)):
                    for c in range(4):
                        last = nc.tensor.transpose(bank(b)[:, c * n:(c + 1) * n], z3[0:n, t, col + c * P:col + (c + 1) * P],
                                                   ident[0:n, 0:n])
                    last.then_inc(r_tr, 1)
                if t < 2:
                    pe.wait_ge(rkd_done, t + 1)
                    if t:
                        pe.wait_ge(r_s1, 1)
                    for c in range(4):
                        last = nc.tensor.matmul(ps[:, 6 * BANK + 256 * c:6 * BANK + 256 * (c + 1)], rkd[:, 2 * c:2 * c + 2, :].rearrange("p h d -> p (h d)"),
                                                z3[:, t, CRV + 256 * c:CRV + 256 * (c + 1)], start=True, stop=True)
                    last.then_inc(r_st, 1)
                pe.wait_ge(r_ops, t + 1)
                pe.wait_ge(r_kT, t + 1)
                if t:
                    pe.wait_ge(r_sT, t)
                for c in range(4):
                    last = nc.tensor.matmul(ps[0:n, 2 * BANK + 2 * c * n:2 * BANK + 2 * (c + 1) * n], rkT[:, c, 0:n],
                                            rbd[:, c, :, 0:n], start=True, stop=True)
                last.then_inc(r_sc, 1)
                if t:
                    pe.wait_ge(r_gn, t)
                if t == 2:
                    pe.wait_ge(st_here, 16 * DB)
                pe.wait_ge(r_sT, t + 1)
                for c in range(4):
                    o = ps[0:n, 4 * BANK + 256 * c:4 * BANK + 256 * (c + 1)]
                    if t == 1:
                        nc.tensor.matmul(o, rqdec[:, c, :], sbd[:, c, :, :], start=True, stop=False)
                    for h in (2 * c, 2 * c + 1):
                        oh_ = o[:, (h % 2) * P:(h % 2 + 1) * P]
                        if t == 2:
                            for e in range(4):
                                nc.tensor.matmul(oh_, qm[:, h, e, :], state[:, e, h, :], start=e == 0, stop=False)
                        last = nc.tensor.matmul(oh_, sT[0:n, h, 0:n], z3[0:n, t, CRV + h * P:CRV + (h + 1) * P],
                                                start=t == 0, stop=t != 1 or h % 2 == 1)
                last.then_inc(r_o, 1)
            for e in range(4):
                pe.wait_ge(km_done, e + 1)
                b = (6, 0)[e % 2]
                if e == 0:
                    pe.wait_ge(retp_done, 1)
                if e >= 2:
                    pe.wait_ge(ns_done, e - 1)
                for h in range(8):
                    last = nc.tensor.matmul(ps[:, b * BANK + P * h:b * BANK + P * (h + 1)],
                                            km[e % 2][0:NS, h, :, :].rearrange("p b d -> p (b d)"),
                                            z3[0:NS, 2, CRV + h * P:CRV + (h + 1) * P], start=True, stop=True)
                last.then_inc(ns_mm, 1)
            pe.wait_ge(r_gn, 3)
            pe.wait_ge(ns_done, 4)

            def transpose_rows(src):
                for t in range(3):
                    n, b = TOK[t], (0, 2, 6)[t]
                    for k in range(KT):
                        last = nc.tensor.transpose(bank(b + k // 4)[:, (k % 4) * P:(k % 4) * P + n],
                                                   src[0:n, t, k * P:(k + 1) * P], ident[0:n, 0:n])
                        if k % 4 == 3:
                            last.then_inc(rows_tr, 1)

            transpose_rows(h2)
            pe.wait_ge(b2_here, 16 * 8)
            pe.wait_ge(rows_done, 6)
            for i in range(6):
                sel, n = ((const("selp"), P), (const("sels"), NS))[i % 2]
                if i >= 2:
                    pe.wait_ge(tb_out, i - 1)
                for k in range(2):
                    last = nc.tensor.matmul(bank((0, 6)[i % 2] + k)[0:n, :], sel, partB[2 * (i // 2) + k], start=True, stop=True)
                last.then_inc(tb_mm, 1)
            pe.wait_ge(tb_out, 6)
            pe.wait_ge(w_here[0], 16 * 14)
            project(wt[0], 0, BANK, rT)
            pe.wait_ge(w_here[1], 16 * 14)
            project(wt[1], 3, BANK, rT)
            pe.wait_ge(yb_done, 2)
            transpose_rows(z3[:, :, CGA:CGB])
            pe.wait_ge(rows_done, 12)
            pe.wait_ge(w_here[0], 16 * 15)
            project(wt[0], 0, BANK)
            pe.wait_ge(w_here[1], 16 * 15)
            project(wt[1], 3, BANK)
            pe.wait_ge(h2_done, 3)
            transpose_rows(h2)
            pe.wait_ge(rows_done, 18)
            pe.wait_ge(rw_here, 32)
            for t in range(3):
                n = TOK[t]
                for k in range(KT):
                    last = nc.tensor.matmul(bank(5)[0:n, t * NE:(t + 1) * NE], hT[:, k, t * P:t * P + n], wr[:, k, :],
                                            start=k == 0, stop=k == KT - 1)
            last.then_inc(lg_mm, 1)
            pe.wait_ge(selm_done, 1)
            for t in range(4):
                for i in range(min(t, 2) + 1):
                    last = nc.tensor.matmul(bank(6)[:, t * NE:(t + 1) * NE], const("tri") if i == t else const("ones"),
                                            sel_m[:, i, :], start=i == 0, stop=i == min(t, 2))
            last.then_inc(pos_mm, 1)
            pe.wait_ge(gate_done, 1)
            for t in range(3):
                last = nc.tensor.transpose(bank(7)[0:NE, t * P:(t + 1) * P], gate_r[:, t, :], ident)
            last.then_inc(gT_tr, 1)
            pe.wait_ge(gT_done, 1)
            pe.wait_ge(late_here, 32)
            for t in range(3):
                n = TOK[t]
                for i in range(2):
                    last = nc.tensor.matmul(bank(2 * t + i)[0:n, :], gT[0:NE, t * P:t * P + n], bdn[0:NE, i * BANK:(i + 1) * BANK],
                                            start=True, stop=True)
            last.then_inc(ainit_mm, 1)
            pe.wait_ge(flag_done, 1)
            for i in range(2):
                last = nc.tensor.matmul(bank(6 + i), const("selp"), partB[6 + i], start=True, stop=True)
            last.then_inc(g2_mm, 1)
            pe.wait_ge(acc_done, 3)
            for i in range(2):
                last = nc.tensor.matmul(bank(i)[0:NS, :], const("sels"), partB[6 + i], start=True, stop=True)
            last.then_inc(g2_mm, 1)
            pe.wait_ge(g2_done, 2)
            pe.wait_ge(bias_here, 16)

            def x_rows(n, n_zero=False):
                pe.wait_ge(s_done, n + 1)
                if not n_zero:
                    pe.wait_ge(xg_done, n)
                for t in range(3):
                    for i in range(2):
                        last = nc.tensor.matmul(bank(3)[64 * i:64 * i + 64, :], S[:, t, :], h2[:, t, i * BANK:(i + 1) * BANK],
                                                start=t == 0, stop=t == 2)
                last.then_inc(x_mm, 1)

            def x_transpose(n):
                pe.wait_ge(xg_done, n + 1)
                for c in range(4):
                    last = nc.tensor.transpose(bank(5)[:, c * P:(c + 1) * P], xg[:, c * P:(c + 1) * P], ident)
                last.then_inc(xt_tr, 1)

            def combine(n, gate_tr):
                if gate_tr:
                    pe.wait_ge(sg_done, n + 1)
                    pe.wait_ge(at_done, n + 1)
                    for t in range(3):
                        last = nc.tensor.transpose(bank(4)[:, t * P:t * P + TOK[t]], Sg[0:TOK[t], t, :],
                                                   ident[0:TOK[t], 0:TOK[t]])
                    last.then_inc(sgt_tr, 1)
                    return
                pe.wait_ge(y_done, n + 1)
                pe.wait_ge(sgt_done, n + 1)
                for i, (t, half) in enumerate(PIECES):
                    if i == 0:
                        pe.wait_ge(acc_done, n * 5 + 3)
                    if i >= 2:
                        pe.wait_ge(acc_done, n * 5 + (i + 2))
                    b = 6 + i % 2
                    if t < 2:
                        nc.tensor.matmul(bank(b), SgT[0:NS, t * P:(t + 1) * P], ysb[0:NS, half * BANK:(half + 1) * BANK],
                                         start=True, stop=True).then_inc(cmb_mm, 1)
                    else:
                        for half in range(2):
                            last = nc.tensor.matmul(bank(b)[64 * half:64 * half + 64, :], SgT[0:NS, 2 * P:NTOK],
                                                    ysb[0:NS, half * BANK:(half + 1) * BANK], start=True, stop=True)
                        last.then_inc(cmb_mm, 1)

            def expert(n, here, first, last_one):
                pe.wait_ge(ebuf_done, n + 1)
                pe.wait_ge(xt_done, n + 1)
                if not first:
                    pe.wait_ge(u_done, n)
                for q in range(4):
                    nc.tensor.matmul(bank(q // 2)[64 * (q % 2):64 * (q % 2) + 64, :], ebuf[:, q, :], bgu, start=True, stop=False)
                for k in range(8):
                    pe.wait_ge(chunk_here[k], here)
                    lhs = xT[:, (k % 4) * P + 64 * (k // 4):(k % 4) * P + 64 * (k // 4) + 64]
                    for q in range(4):
                        last = nc.tensor.matmul(bank(q // 2)[64 * (q % 2):64 * (q % 2) + 64, :], lhs,
                                                ring3[k][:, q * BANK:(q + 1) * BANK], start=False, stop=k == 7)
                    last.then_inc(chunk_used, 1)
                if not first:
                    combine(n - 1, True)
                if not last_one:
                    x_rows(n + 1)
                if not first:
                    combine(n - 1, False)
                if not last_one:
                    x_transpose(n + 1)
                pe.wait_ge(act_done, n + 1)
                if not first:
                    pe.wait_ge(at_done, n)
                for c in range(4):
                    last = nc.tensor.transpose(bank(4)[:, c * P:(c + 1) * P], gb[:, c * P:(c + 1) * P], ident)
                last.then_inc(at_tr, 1)
                pe.wait_ge(at_done, n + 1)
                if not first:
                    pe.wait_ge(y_done, n)
                for k in range(8):
                    if k % 2 == 0:
                        pe.wait_ge(chunk_here[8 + k // 2], here)
                    lhs = aTt[:, (k % 4) * P + 64 * (k // 4):(k % 4) * P + 64 * (k // 4) + 64]
                    for q in range(2):
                        last = nc.tensor.matmul(bank(2)[64 * q:64 * q + 64, :], lhs,
                                                ring3[8 + k // 2][:, (k % 2) * D + q * BANK:(k % 2) * D + (q + 1) * BANK],
                                                start=k == 0, stop=k == 7)
                    if k % 2:
                        last.then_inc(chunk_used, 1)

            def experts(count, base):
                x_rows(base, base == 0)
                x_transpose(base)
                expert(base, 16 * (base + 1), True, False)
                with pe.Fori(1, count - 1) as i:
                    expert(i + base, i * 16 + 16 * (base + 1), False, False)
                n = base + count - 1
                expert(n, 16 * (n + 1), False, True)
                combine(n, True)
                combine(n, False)

            experts(NE, 0)
            more = pe.value_load(pt[0:1, 0:1], min_val=0, max_val=XBLK)
            with pe.If(more > 0):
                experts(XBLK, NE)

        @block.vector
        def _(dve):
            steps = [0]

            def step(ins):
                steps[0] += 1
                ins.then_inc(dve_step, 1)
                dve.wait_ge(dve_step, steps[0])

            def rstd(var, root, n, m=[0]):
                m[0] += 1
                v, y, e = st[:, var:var + n], st[:, root:root + n], st[:, 80:80 + n]
                dve.wait_ge(rstd_done, m[0])
                step(nc.vector.reciprocal(y, y))
                step(nc.vector.tensor_tensor(e, y, y, ALU.mult))
                step(nc.vector.tensor_tensor(e, e, v, ALU.mult))
                step(nc.vector.tensor_scalar(e, e, -0.5, 1.5, ALU.mult, ALU.add))
                step(nc.vector.tensor_tensor(y, y, e, ALU.mult))

            nc.vector.memset(z3[NS:P, 2, :], 0.0).then_inc(z_zeroed, 1)
            dve.wait_ge(ct_sig, 1)
            nc.vector.tensor_tensor(cT[:, :], cT[:, :], junk[:, 0:256], ALU.mult).then_inc(ct_done, 1)
            dve.wait_ge(ss_done, 3)
            nc.vector.tensor_scalar(st[:, 0:3], st[:, 0:3], 1.0 / D, EPS, ALU.mult, ALU.add).then_inc(var_done, 1)
            for i in range(4):
                dve.wait_ge(tile_done, i + 1)
                nc.vector.tensor_copy(partA[:, i * BANK:(i + 1) * BANK], bank(i)).then_inc(part_done, 1)
            dve.wait_ge(tab_done, 2)
            dve.wait_ge(g_here, 32)
            step(nc.vector.scalar_tensor_tensor(a1p, bank(4, 2), 1.0, gmix, ALU.add, ALU.mult))
            rstd(0, 3, 3)
            for t in range(3):
                n = TOK[t]
                am, sh = (a1p, bank(6, 2)) if t < 2 else (a1s, bank(2, 2))
                if t == 0:
                    dve.wait_ge(tab_done, 4)
                if t == 2:
                    dve.wait_ge(tab_done, 8)
                    step(nc.vector.scalar_tensor_tensor(a1s[0:n], bank(0, 2)[0:n], 1.0, gmix[0:n], ALU.add, ALU.mult))
                step(nc.vector.scalar_tensor_tensor(hrow[0:n, t, :], x3[0:n, t, :], st[0:n, 3 + t:4 + t], am[0:n],
                                                    ALU.mult, ALU.mult))
                nc.vector.tensor_tensor(hrow[0:n, t, :], hrow[0:n, t, :], sh[0:n], ALU.add).then_inc(h_done, 1)

            def rotate(cols, heads, signal):
                v = z3[:, :, cols:cols + 64 * heads].rearrange("p t (h d) -> p t h d", d=64)
                x1, x2 = v[:, :, :, 0:8], v[:, :, :, 8:16]
                cos, sin = (const(n).rearrange("p (t n) -> p t n", t=3).unsqueeze(2).broadcast_to([P, 3, heads, 8])
                            for n in ("cosq", "sinq"))
                a1, a2, a3, a4 = (m[:, :, 0:heads, :] for m in (t1, t2, t3, t4))
                nc.vector.tensor_tensor(a1, x1, cos, ALU.mult)
                nc.vector.tensor_tensor(a2, x2, sin, ALU.mult)
                nc.vector.tensor_tensor(a3, x2, cos, ALU.mult)
                step(nc.vector.tensor_tensor(a4, x1, sin, ALU.mult))
                nc.vector.tensor_tensor(x1, a1, a2, ALU.subtract)
                ins = nc.vector.tensor_tensor(x2, a3, a4, ALU.add)
                if signal is None:
                    step(ins)
                else:
                    ins.then_inc(signal, 1)

            step(nc.vector.memset(ikbd, 0.0))
            step(nc.vector.memset(kbd, 0.0))
            dve.wait_ge(z_done, 3)
            rotate(CIQ, 9, None)
            for j in range(2):
                last = nc.vector.tensor_copy(ikd[:, :, 64 * j:64 * j + 64], z3[:, :, CIK:CIW])
            last.then_inc(ikd_done, 1)
            rotate(CQ, 10, qk_roped)
            for j in range(2):
                last = nc.vector.tensor_tensor(
                    iwx[0:NS, 32 * j:32 * j + 32].rearrange("p (h t) -> p h t", t=DS),
                    z3[0:NS, 2, CIW:CRQ].rearrange("p (c j) -> p j c", j=2)[:, j, :].unsqueeze(2).broadcast_to([NS, 4, DS]),
                    const("dm")[0:NS].unsqueeze(1).broadcast_to([NS, 4, DS]), ALU.mult)
            last.then_inc(iwx_done, 1)
            dve.wait_ge(tr_act, 1)
            nc.vector.tensor_copy(ikbd[0:64, 0, :], ikTn[0:64, 0:SEQ])
            nc.vector.tensor_copy(ikbd[64:P, 1, :], ikTn[64:P, 0:SEQ]).then_inc(tr_dve, 1)
            for n, col, b in ((4, CIQ, 3), (7, CQ, 6)):
                dve.wait_ge(tr_done, n)
                bd = z3[:, 2, col:col + 512]
                step(nc.vector.memset(bd, 0.0))
                bd = bd.rearrange("p (b j c t) -> p j b c t", b=DB, j=2, c=4)
                src = bank(b)[:, 0:256].rearrange("p (c b t) -> p b c t", c=4, b=DB)
                nc.vector.tensor_copy(bd[0:64, 0], src[0:64])
                nc.vector.tensor_copy(bd[64:P, 1], src[64:P]).then_inc(tr_dve, 1)
            dve.wait_ge(tr_act, 6)
            nc.vector.tensor_copy(kbd[0:64, 0, :], kTn[0:64, 0:SEQ])
            nc.vector.tensor_copy(kbd[64:P, 1, :], kTn[64:P, 0:SEQ]).then_inc(tr_dve, 1)
            dve.wait_ge(iw_mm, 1)
            nc.vector.tensor_copy(iwcol[0:NS], bank(3)[0:NS, 0:DB]).then_inc(iw_done, 1)
            dve.wait_ge(iw_done, 1)

            def prompt_index(t):
                w = (t + 1) * P
                dve.wait_ge(prel_done, t + 1)
                for h in range(8):
                    if h == 0:
                        ins = nc.vector.tensor_scalar(sc_p[:, t, 0:w], rel_p[t][:, 0, 0:w], z3[:, t, CIW:CIW + 1], None, ALU.mult)
                    else:
                        ins = nc.vector.scalar_tensor_tensor(sc_p[:, t, 0:w], rel_p[t][:, h, 0:w],
                                                             z3[:, t, CIW + h:CIW + h + 1], sc_p[:, t, 0:w], ALU.mult, ALU.add)
                    if h < 7:
                        step(ins)
                ins.then_inc(psc_done, 1)

            for b in range(DB):
                dve.wait_ge(sdot_done, b + 1)
                if b:
                    dve.wait_ge(ssel_done, b)
                nc.vector.tensor_scalar(rel_s[0:NS], ps[0:NS, 3 * BANK:3 * BANK + KEYS], 0.0, iwcol[0:NS, b:b + 1],
                                        ALU.max, ALU.mult).then_inc(srel_done, 1)
            prompt_index(0)
            prompt_index(1)

            def top(v, k):
                m8 = st[0:v.shape[0], 40:48]
                for _ in range(k // 8):
                    step(nc.vector.max(m8, v))
                    step(nc.vector.match_replace(v, m8, v, TAKEN))

            for t in range(2):
                w = (t + 1) * P
                dve.wait_ge(pcap_done, t + 1)
                top(sc_p[:, t, 0:w], min(256, SEQ // 4))
                nc.vector.tensor_scalar(mask_p[:, t, 0:w], sc_p[:, t, 0:w], -2.0e38, NEG, ALU.is_gt, ALU.mult).then_inc(pmask_raw, 1)
            dve.wait_ge(ssc_done, 1)
            caps = const("caps")[0:NS]
            step(nc.vector.tensor_tensor(sc_s[0:NS, PAST:KEYS], sc_s[0:NS, PAST:KEYS], caps, ALU.min))
            top(sc_s[0:NS], min(256, KEYS // 4))
            step(nc.vector.tensor_scalar(mask_s[0:NS], sc_s[0:NS], -2.0e38, NEG, ALU.is_gt, ALU.mult))
            nc.vector.tensor_tensor(mask_s[0:NS, PAST:KEYS], mask_s[0:NS, PAST:KEYS], caps, ALU.min).then_inc(masks_done, 1)

            dve.wait_ge(rot_done, 3)
            dve.wait_ge(pcap_done, 4)
            for t in range(2):
                w = (t + 1) * P
                b0 = (6, 0)[t]
                dve.wait_ge(psc2_done, t + 1)
                if t:
                    dve.wait_ge(ppt_tr, 1)
                mask = mask_p[:, t, 0:w].unsqueeze(1).broadcast_to([P, 8, w])
                step(nc.vector.tensor_tensor(p_p[:, :, 0:w], ps[:, b0 * BANK:b0 * BANK + 8 * w].rearrange("p (h n) -> p h n", h=8),
                                             mask, ALU.add))
                step(nc.vector.tensor_reduce(mx, p_p[:, :, 0:w], AX.X, ALU.max))
                nc.vector.tensor_scalar(nm, mx, -ATT_SCALE, None, ALU.mult).then_inc(pmx_done, 1)
                dve.wait_ge(pexp_done, 8 * (t + 1))
                step(nc.vector.reciprocal(rs, rs))
                nc.vector.tensor_tensor(p_p[:, :, 0:w], p_p[:, :, 0:w], rs.unsqueeze(2).broadcast_to([P, 8, w]),
                                        ALU.mult).then_inc(pp_done, 1)
            for b in range(DB):
                dve.wait_ge(ssc2_done, b + 1)
                step(nc.vector.tensor_reduce(mx[0:NS, 0:1], ps[0:NS, 0:KEYS], AX.X, ALU.max))
                nc.vector.tensor_scalar(nm[0:NS, 0:1], mx[0:NS, 0:1], -ATT_SCALE, None, ALU.mult).then_inc(smx_done, 1)
                dve.wait_ge(tile_done, 18 + b)
                nc.vector.tensor_copy(partB[b], bank(4)).then_inc(partb_done, 1)
                dve.wait_ge(sexp_done, b + 1)
                step(nc.vector.reciprocal(rs[0:NS, 0:1], rs[0:NS, 0:1]))
                nc.vector.tensor_scalar(p_s[0:NS], p_s[0:NS], rs[0:NS, 0:1], None, ALU.mult).then_inc(sp_done, 1)
                dve.wait_ge(spt_tr, b + 1)
                if b:
                    dve.wait_ge(spv_done, b)
                nc.vector.tensor_copy(pT_s[0:DS, NPAGES, :], bank(5)[0:DS, NS:2 * NS])
                nc.vector.tensor_copy(pT_s[:, 0:NPAGES, :], bank(3).rearrange("p (n q) -> p n q", q=NS)).then_inc(spt_done, 1)

            dve.wait_ge(gates_done, 6)

            def each_piece(b):
                yield 0, P, bank(b), slice(0, BANK)
                yield 1, P, bank(b + 1), slice(0, BANK)
                yield 2, NS, bank(b + 2)[0:NS, 0:256], slice(0, 256)
                yield 2, NS, bank(b + 2)[NS:P, 0:256], slice(256, BANK)

            def shifted(v, c, i):
                return v[:, i * BANK + c.start:i * BANK + c.stop]

            for i in range(2):
                if i == 0:
                    dve.wait_ge(ya_mm, 1)
                else:
                    dve.wait_ge(tile_done, 26)
                for t, n, src, c in each_piece(3 * i):
                    g = shifted(z3[0:n, t, CGA:CGB], c, i)
                    last = nc.vector.tensor_tensor(g, src, g, ALU.mult)
                last.then_inc(ya_done, 1)
            nc.vector.memset(rbd, 0.0)
            nc.vector.memset(sbd, 0.0)
            step(nc.vector.memset(qm, 0.0))
            dve.wait_ge(dec_here, 64)
            for t in range(3):
                n = TOK[t]
                dve.wait_ge(r_tr, 2 * t + 1)
                if t:
                    dve.wait_ge(r_sc, t)
                src = bank(0)[:, 0:4 * n].rearrange("p (c n) -> p c n", c=4)
                last = None
                if t == 1:
                    nc.vector.tensor_tensor(rqdec, src, qdec_p.rearrange("p (c n) -> p c n", c=4), ALU.mult)
                if t == 2:
                    qd = const("qdecs").rearrange("p (c j t) -> p j c t", c=4, j=2)
                    for j in range(2):
                        for b in range(2):
                            for e in range(4):
                                bb = 2 * e + b
                                nc.vector.tensor_tensor(
                                    qm[64 * b:64 * b + 64, :, e, bb * DS:(bb + 1) * DS].rearrange("p (c j) t -> p j c t", j=2)[:, j],
                                    src[64 * j:64 * j + 64, :, bb * DS:(bb + 1) * DS], qd[64 * b:64 * b + 64, j], ALU.mult)
                nc.vector.tensor_copy(rbd[0:64, :, 0, 0:n], src[0:64])
                nc.vector.tensor_copy(rbd[64:P, :, 1, 0:n], src[64:P]).then_inc(r_ops, 1)
                if t < 2:
                    dve.wait_ge(r_st, t + 1)
                    kvp = bank(6, 2).rearrange("p (c j n) -> p c j n", c=4, j=2)
                    if t == 0:
                        nc.vector.tensor_copy(s1[0:64], kvp[0:64, :, 0])
                        nc.vector.tensor_copy(s1[64:P], kvp[64:P, :, 1])
                        nc.vector.tensor_copy(sbd[0:64, :, 0], kvp[0:64, :, 0])
                        step(nc.vector.tensor_copy(sbd[64:P, :, 1], kvp[64:P, :, 1]))
                        nc.vector.tensor_scalar(st[:, 16:17], st[:, 16:17], 0.0, 1.0, ALU.mult, ALU.add).then_inc(r_s1, 1)
                    else:
                        step(nc.vector.tensor_tensor(s1, s1, const("gchunk").unsqueeze(2).broadcast_to([P, 4, P]), ALU.mult))
                        nc.vector.tensor_tensor(s1[0:64], s1[0:64], kvp[0:64, :, 0], ALU.add)
                        nc.vector.tensor_tensor(s1[64:P], s1[64:P], kvp[64:P, :, 1], ALU.add).then_inc(retp_done, 1)
                dve.wait_ge(r_sc, t + 1)
                if t:
                    dve.wait_ge(r_o, t)
                scp = ps[0:n, 2 * BANK:2 * BANK + 8 * n].rearrange("p (h n) -> p h n", h=8)
                if t < 2:
                    nc.vector.tensor_tensor(sT[:, 0:6, :], scp[:, 0:6], dec_a.rearrange("p (h n) -> p h n", n=P), ALU.mult)
                    nc.vector.tensor_tensor(sT[:, 6:8, :], scp[:, 6:8], dec_b.rearrange("p (h n) -> p h n", n=P),
                                            ALU.mult).then_inc(r_sT, 1)
                else:
                    nc.vector.tensor_tensor(sT[0:n, :, 0:n], scp, dec_s[0:n].rearrange("p (h n) -> p h n", n=NS),
                                            ALU.mult).then_inc(r_sT, 1)
                dve.wait_ge(r_o, t + 1)
                o = bank(4, 2)[0:n].rearrange("p (h v) -> p h v", h=8)
                for h in range(8):
                    last = nc.vector.bn_stats(gst[0:n, h, :], o[:, h, :])
                step(last)
                for h in range(8):
                    last = nc.vector.bn_aggr(gmv[0:n, h, :], gst[0:n, h, :])
                step(last)
                nc.vector.tensor_scalar(st[0:n, 16:24], gmv[0:n, :, 1], 1.0, GN_EPS, ALU.mult, ALU.add).then_inc(gn_var, 1)
                r = z3[0:n, t, CRG:CGA].rearrange("p (h v) -> p h v", h=8)
                for h in range(8):
                    last = nc.vector.scalar_tensor_tensor(r[:, h, :], o[:, h, :], gmv[0:n, h, 0:1], r[:, h, :], ALU.subtract, ALU.mult)
                step(last)
                rstd(16, 24, 8)
                nc.vector.tensor_tensor(r, r, st[0:n, 24:32].unsqueeze(2).broadcast_to([n, 8, P]), ALU.mult).then_inc(r_gn, 1)
            for e in range(4):
                dve.wait_ge(ns_mm, e + 1)
                dve.wait_ge(st_scaled, e + 1)
                nc.vector.tensor_tensor(state[:, e], bank((6, 0)[e % 2], 2).rearrange("p (h v) -> p h v", h=8), state[:, e],
                                        ALU.add).then_inc(ns_done, 1)
            dve.wait_ge(gb_sig, 3)
            for i in range(2):
                dve.wait_ge(tile_done, 27 + i)
                for t, n, src, c in each_piece(3 * i):
                    g = shifted(z3[0:n, t, CGB:DIN], c, i)
                    last = nc.vector.tensor_tensor(g, src, g, ALU.mult)
                step(last)
                for t in range(3):
                    n = TOK[t]
                    ga, gb_ = (z3[0:n, t, c0 + i * BANK:c0 + (i + 1) * BANK] for c0 in (CGA, CGB))
                    last = nc.vector.tensor_tensor(ga, ga, gb_, ALU.add)
                last.then_inc(yb_done, 1)
            dve.wait_ge(tb_out, 6)
            dve.wait_ge(gf_here, 16)
            nc.vector.scalar_tensor_tensor(a2p, a2p, 1.0, gffn, ALU.add, ALU.mult)
            nc.vector.scalar_tensor_tensor(a2s[0:NS], a2s[0:NS], 1.0, gffn[0:NS], ALU.add, ALU.mult)
            for i in range(2):
                dve.wait_ge(tile_done, 29 + i)
                for t, n, src, c in each_piece(3 * i):
                    last = nc.vector.tensor_tensor(shifted(tmp3[0:n, t, :], c, i), src, shifted((gt1s if t == 2 else gt1p)[0:n], c, i), ALU.mult)
                step(last)
                for t in range(3):
                    n = TOK[t]
                    xs = x3[0:n, t, i * BANK:(i + 1) * BANK]
                    last = nc.vector.tensor_tensor(xs, xs, tmp3[0:n, t, i * BANK:(i + 1) * BANK], ALU.add)
                if i:
                    last.then_inc(x1_done, 1)
                else:
                    step(last)
            dve.wait_ge(ss2_done, 3)
            nc.vector.tensor_scalar(st[:, 8:11], st[:, 8:11], 1.0 / D, EPS, ALU.mult, ALU.add).then_inc(var_done, 1)
            rstd(8, 11, 3)
            for t in range(3):
                n = TOK[t]
                am, sh = (a2p, sh2p) if t < 2 else (a2s, sh2s)
                step(nc.vector.scalar_tensor_tensor(h2[0:n, t, :], x3[0:n, t, :], st[0:n, 11 + t:12 + t], am[0:n],
                                                    ALU.mult, ALU.mult))
                nc.vector.tensor_tensor(h2[0:n, t, :], h2[0:n, t, :], sh[0:n], ALU.add).then_inc(h2_done, 1)
            nc.vector.memset(m8s, 3.0e38)
            nc.vector.memset(sel_m, 0.0)
            step(nc.vector.memset(gate_r, 0.0))
            dve.wait_ge(lg_mm, 1)
            for t in range(3):
                n = TOK[t]
                last = nc.vector.tensor_tensor(lgt[0:n, t, :], bank(5)[0:n, t * NE:(t + 1) * NE], br[0:n], ALU.add)
            step(last)
            for t in range(3):
                last = nc.vector.max(m8r[0:TOK[t], 8 * t:8 * t + 8], lgt[0:TOK[t], t, :])
            step(last)
            for t in range(3):
                last = nc.vector.tensor_scalar(nmr[0:TOK[t], t:t + 1], m8r[0:TOK[t], 8 * t:8 * t + 1], -1.0, None, ALU.mult)
            last.then_inc(m0_done, 1)
            for t in range(3):
                n = TOK[t]
                step(nc.vector.tensor_copy(m8s[0:n, 0:4], m8r[0:n, 8 * t:8 * t + 4]))
                step(nc.vector.match_replace(lrep[0:n, t, :], m8s[0:n], lgt[0:n, t, :], TAKEN))
                last = nc.vector.tensor_scalar(sel_m[0:n, t, :], lrep[0:n, t, :], -2.0e38, None, ALU.is_lt)
                if t < 2:
                    step(last)
            last.then_inc(selm_done, 1)
            dve.wait_ge(selm_done, 1)
            dve.wait_ge(ex_done, 3)
            for t in range(3):
                n = TOK[t]
                step(nc.vector.tensor_tensor(ex[0:n, t, :], ex[0:n, t, :], sel_m[0:n, t, :], ALU.mult))
                step(nc.vector.tensor_reduce(srt[0:n, t:t + 1], ex[0:n, t, :], AX.X, ALU.add))
                step(nc.vector.reciprocal(srt[0:n, t:t + 1], srt[0:n, t:t + 1]))
                last = nc.vector.tensor_scalar(gate_r[0:n, t, :], ex[0:n, t, :], srt[0:n, t:t + 1], None, ALU.mult)
            last.then_inc(gate_done, 1)
            dve.wait_ge(pos_mm, 1)
            step(nc.vector.scalar_tensor_tensor(pos_r, bank(6)[:, 0:96].rearrange("p (t e) -> p t e", t=3), 1.0, sel_m, ALU.add, ALU.mult))
            step(nc.vector.tensor_scalar(pos_r, pos_r, -1.0, None, ALU.add))
            step(nc.vector.tensor_copy(cnt, bank(6)[:, 96:128]))
            step(nc.vector.tensor_scalar(extra, cnt, float(CAP), None, ALU.is_gt))
            for r in range(2, NTOK // CAP):
                step(nc.vector.scalar_tensor_tensor(extra, cnt, float(CAP * r), extra, ALU.is_gt, ALU.add))
            run, other, w = extra, cum, 1
            while w < NE:
                step(nc.vector.tensor_copy(other[:, 0:w], run[:, 0:w]))
                step(nc.vector.tensor_tensor(other[:, w:NE], run[:, w:NE], run[:, 0:NE - w], ALU.add))
                run, other = other, (cum2 if other is cum else cum)
                w *= 2
            nc.vector.tensor_copy(pt[0:1, 0:1], run[0:1, NE - 1:NE]).then_inc(flag_done, 1)

            def pick(n, tab, i, n_zero):
                if not n_zero:
                    dve.wait_ge(x_mm, n)
                for t in range(3):
                    last = nc.vector.tensor_scalar(S[:, t, :], const("iota"), tab[:, t, bass.ds(i, 1)], None, ALU.is_equal)
                last.then_inc(s_done, 1)

            def pick_gates(n, tab, gates, i):
                dve.wait_ge(at_tr, n + 1)
                for t in range(3):
                    last = nc.vector.tensor_scalar(Sg[:, t, :].rearrange("p (i n) -> p i n", i=2),
                                                   const("iota").unsqueeze(1).broadcast_to([P, 2, CAP]), tab[:, t, bass.ds(i, 1)],
                                                   gates[:, t, bass.ds(i, 1)], ALU.is_equal, ALU.mult)
                last.then_inc(sg_done, 1)

            def pick_bias(n, sel, i, n_zero):
                if not n_zero:
                    dve.wait_ge(chunk_used, n * 12 - 4)
                nc.vector.tensor_copy(ebuf, sel[:, :, bass.ds(i, 1)].broadcast_to([P, 4, CAP])).then_inc(ebuf_done, 1)

            def add_results(n):
                for i, (t, half) in enumerate(PIECES):
                    dve.wait_ge(cmb_mm, n * 5 + (i + 1))
                    b = 6 + i % 2
                    if t < 2:
                        v = acc[:, t, half * BANK:(half + 1) * BANK]
                        nc.vector.tensor_tensor(v, v, bank(b), ALU.add).then_inc(acc_done, 1)
                    else:
                        for half in range(2):
                            v = acc[0:NS, 2, half * BANK:(half + 1) * BANK]
                            last = nc.vector.tensor_tensor(v, v, bank(b)[64 * half:64 * half + 64, :], ALU.add)
                        last.then_inc(acc_done, 1)

            def expert(n, i, tab, gates, sel, first, last_one):
                if not last_one:
                    pick(n + 1, tab, i + 1, False)
                if not first:
                    pick_gates(n - 1, tab, gates, i - 1)
                dve.wait_ge(chunk_used, n * 12 + 8)
                nc.vector.tensor_scalar(gb, bank(0), 7.0, None, ALU.min).then_inc(g_done, 1)
                nc.vector.tensor_scalar(ub, bank(1), -7.0, 7.0, ALU.max, ALU.min).then_inc(u_done, 1)
                if not last_one:
                    pick_bias(n + 1, sel, i + 1, False)
                dve.wait_ge(sig_done, n + 1)
                nc.vector.tensor_tensor(sgm, sgm, gb, ALU.mult).then_inc(mul_done, 1)
                dve.wait_ge(mul_done, n + 1)
                nc.vector.scalar_tensor_tensor(gb, ub, 1.0, sgm, ALU.add, ALU.mult).then_inc(act_done, 1)
                if not first:
                    add_results(n - 1)

            def experts(count, base, tab, gates, sel):
                pick(base, tab, 0, base == 0)
                pick_bias(base, sel, 0, base == 0)
                expert(base, 0, tab, gates, sel, True, False)
                with dve.Fori(1, count - 1) as i:
                    expert(i + base, i, tab, gates, sel, False, False)
                n = base + count - 1
                expert(n, count - 1, tab, gates, sel, False, True)
                pick_gates(n, tab, gates, count - 1)
                add_results(n)
                dve.wait_ge(acc_done, 5 * (base + count) + 3)

            dve.wait_ge(acc_done, 3)
            experts(NE, 0, pos_r, gate_r, ident.rearrange("p (q e) -> p q e", q=4))
            dve.wait_ge(flag_done, 1)
            more = dve.value_load(pt[0:1, 0:1], min_val=0, max_val=XBLK)
            with dve.If(more > 0):
                iota_x = const("iota")[:, 0:XBLK].unsqueeze(2).broadcast_to([P, XBLK, NE])
                cum_b = run.unsqueeze(1).broadcast_to([P, XBLK, NE])
                nc.vector.memset(tot[:, 0:1], 0.0)
                step(nc.vector.tensor_copy(tot[:, 1:NE], run[:, 0:NE - 1]))
                nc.vector.tensor_tensor(oh, iota_x, tot.unsqueeze(1).broadcast_to([P, XBLK, NE]), ALU.is_ge)
                step(nc.vector.tensor_tensor(oh2, iota_x, cum_b, ALU.is_lt))
                step(nc.vector.tensor_tensor(oh, oh, oh2, ALU.mult))

                def chosen(dst, row):
                    step(nc.vector.tensor_tensor(oh2, oh, row.unsqueeze(1).broadcast_to([P, XBLK, NE]), ALU.mult))
                    step(nc.vector.tensor_reduce(dst, oh2, AX.X, ALU.add))

                chosen(rx, tot)
                chosen(eidx, const("iota")[:, 0:NE])
                step(nc.vector.tensor_tensor(rx, const("iota")[:, 0:XBLK], rx, ALU.subtract))
                step(nc.vector.tensor_scalar(rx, rx, 1.0, float(CAP), ALU.add, ALU.mult))
                for t in range(3):
                    chosen(pos_x[:, t, :], pos_r[:, t, :])
                    step(nc.vector.tensor_tensor(pos_x[:, t, :], pos_x[:, t, :], rx, ALU.subtract))
                    chosen(gate_x[:, t, :], gate_r[:, t, :])
                for q in range(4):
                    step(nc.vector.tensor_scalar(sel_x[:, q, :], eidx, const("pcol")[:, q:q + 1], None, ALU.is_equal))
                nc.vector.tensor_copy(pt[0:1, 8:8 + XBLK], eidx[0:1]).then_inc(flag_done, 1)
                experts(XBLK, NE, pos_x, gate_x, sel_x)
            dve.wait_ge(g2_done, 2)
            for t in range(3):
                n = TOK[t]
                g2 = (gt2s if t == 2 else gt2p)[0:n]
                last = nc.vector.tensor_tensor(acc[0:n, t, :], acc[0:n, t, :], g2, ALU.mult)
            steps2 = last.then_inc(fin_step, 1)
            dve.wait_ge(fin_step, 1)
            for t in range(3):
                n = TOK[t]
                last = nc.vector.tensor_tensor(x3[0:n, t, :], x3[0:n, t, :], acc[0:n, t, :], ALU.add)
            last.then_inc(x1_done, 1)
            dve.wait_ge(ssf_done, 3)
            nc.vector.tensor_scalar(st[:, 8:11], st[:, 8:11], 1.0 / D, EPS, ALU.mult, ALU.add).then_inc(var_done, 1)
            dve.wait_ge(rstd_done, 6)
            v, y, e_ = st[:, 8:11], st[:, 11:14], st[:, 80:83]
            for k, ins in enumerate((lambda: nc.vector.reciprocal(y, y), lambda: nc.vector.tensor_tensor(e_, y, y, ALU.mult),
                                     lambda: nc.vector.tensor_tensor(e_, e_, v, ALU.mult),
                                     lambda: nc.vector.tensor_scalar(e_, e_, -0.5, 1.5, ALU.mult, ALU.add),
                                     lambda: nc.vector.tensor_tensor(y, y, e_, ALU.mult))):
                ins().then_inc(fin_step, 1)
                dve.wait_ge(fin_step, 2 + k)
            dve.wait_ge(late_here, 32)
            for t in range(3):
                n = TOK[t]
                nc.vector.scalar_tensor_tensor(x3[0:n, t, :], x3[0:n, t, :], st[0:n, 11 + t:12 + t], gfin[0:n],
                                               ALU.mult, ALU.mult).then_inc(yf_done, 1)


def kernel(**inputs):
    from concourse import bacc
    from concourse.bass_utils import run_bass_kernel_spmd

    v = {k: np.asarray(x) for k, x in inputs.items()}
    dec_p, dec_s, qdec_p = decay_tables()
    c = np.zeros((32, D), np.float32)
    c[0], c[1:1 + DB] = v["c_prompt"][0], v["c_sample"]
    w_in = v["w_in"][0]
    wq = w_in[:, CQ:CK].reshape(D, 2, 4, 64).transpose(0, 2, 1, 3).reshape(D, CK)
    arrays = {
        "x_prompt": v["x_prompt"], "x_sample": v["x_sample"], "page_table": v["page_table"].reshape(1, -1),
        "norm_mix_g": v["norm_mix_g"][0], "norm_ffn_g": v["norm_ffn_g"][0], "norm_final_g": v["norm_final_g"],
        "cache_kv": np.concatenate([v[n][0].reshape(NPOOL, PAGE, P) for n in ("cache_k", "cache_v")], axis=2),
        "cache_ik": v["cache_ik"][0], "state": v["state_ret"][0],
        "cT": c.reshape(32, KT, P).transpose(2, 1, 0).reshape(P, KT * 32),
        "const": CONST, "dec_p": dec_p, "dec_s": dec_s, "qdec_p": qdec_p,
        "w_ada": v["w_ada"][0], "b_ada": v["b_ada"],
        "w_in": np.concatenate([wq, w_in[:, CK:]], axis=1),
        "w_branch_a": v["w_branch_a"][0].reshape(2, 4, 64, D).transpose(1, 0, 2, 3).reshape(512, D),
        "w_branch_b": v["w_branch_b"][0], "w_out": v["w_out"][0],
        "w_router": v["w_router"][0], "b_router": v["b_router"][0],
        "w_gate_up": v["w_gate_up"][0], "w_down": v["w_down"][0], "b_down": v["b_down"][0],
        "b_gate_up": v["b_gate_up"][0].reshape(NE, 4, BANK).transpose(1, 0, 2).reshape(4 * NE, BANK),
    }
    outputs = {"y_prompt": (SEQ, D), "y_sample": (NS, D), "k_prompt": (SEQ, P), "v_prompt": (SEQ, P), "ik_prompt": (SEQ, 64),
               "ret_prompt": (8, 64, P), "k_sample": (NS, P), "v_sample": (NS, P), "ik_sample": (NS, 64),
               "ret_sample": (DB, 8, 64, P)}
    shapes = {"y_prompt": (1, SEQ, D), "y_sample": (DB, DS, D), "k_prompt": (1, 1, SEQ, 2, 64), "v_prompt": (1, 1, SEQ, 2, 64),
              "ik_prompt": (1, 1, SEQ, 64), "ret_prompt": (1, 1, 8, 64, P), "k_sample": (1, DB, DS, 2, 64),
              "v_sample": (1, DB, DS, 2, 64), "ik_sample": (1, DB, DS, 64), "ret_sample": (1, DB, 8, 64, P)}
    nc = bacc.Bacc("TRN2", target_bir_lowering=False, num_devices=1)
    arrays = {f"in_{k}": np.ascontiguousarray(x) for k, x in arrays.items()}
    a = {k[3:]: nc.dram_tensor(k, x.shape, mybir.dt.from_np(x.dtype), kind="ExternalInput").ap()
         for k, x in arrays.items()}
    for k, s in outputs.items():
        a[k] = nc.dram_tensor(k, s, F32, kind="ExternalOutput").ap()
    kern(nc, a)
    r = run_bass_kernel_spmd(nc, [arrays], core_ids=[0])
    return tuple(np.asarray(r.results[0][k]).reshape(shapes[k]) for k in outputs)
```

```python
from contextlib import ExitStack

import numpy as np

import concourse.bass as bass
from concourse import mybir

F32 = mybir.dt.float32
BF16 = mybir.dt.bfloat16
I32 = mybir.dt.int32
U32 = mybir.dt.uint32
ALU = mybir.AluOpType
ACT = mybir.ActivationFunctionType
AX = mybir.AxisListType

P = 128
D = 1024
KT = D // P
SEQ = 256
DB, DS = 8, 8
NS = DB * DS
NPOOL = 80
PAST, PAGE = 1024, 128
NPAGES = PAST // PAGE
PAIRS = DB // 2
KEYS = PAST + DS
NE, TOPK, DFF = 32, 4, 1024
TOK = (P, P, NS)
NTOK = SEQ + NS
BANK = 512
EPS, GN_EPS = 1e-6, 1e-5
ATT_SCALE = 64 ** -0.5
NEG = -1.0e30
TAKEN = -3.0e38

CQ, CK, CV, CIQ, CIK, CIW, CRQ, CRK, CRV, CRG, CGA, CGB, DIN = (
    0, 512, 640, 768, 1280, 1344, 1352, 1864, 2376, 3400, 4424, 5448, 6472)
NZT = 13
LASTW = DIN - 12 * BANK

CAP = 64
XBLK = (NTOK * TOPK) // (CAP + 1)
NBLK = NE + XBLK


PIECES = ((0, 0), (2, 0), (0, 1), (1, 0), (1, 1))


def lg():
    return np.log(1.0 - 2.0 ** (-5.0 - np.arange(8, dtype=np.float64)))


def constants():
    t = {}
    t["ident"] = np.eye(P)
    pos = np.zeros((P, 3), np.float32)
    pos[:, 0] = np.arange(P)
    pos[:, 1] = P + np.arange(P)
    pos[:NS, 2] = PAST + np.arange(NS) % DS
    def rope(rot, theta):
        half = rot // 2
        inv = (theta ** (-np.arange(half) * 2.0 / rot)).astype(np.float32)
        ang = (pos[:, :, None] * inv).astype(np.float32).astype(np.float64)
        return np.cos(ang).reshape(P, -1), np.sin(ang).reshape(P, -1)
    t["cosq"], t["sinq"] = rope(16, 500000.0)
    t["cosr"], t["sinr"] = rope(64, 10000.0)
    r = np.arange(P)
    t["selp"] = np.tile(((r % 32 == 0) | (r == 9))[:, None], (1, P))
    t["sels"] = ((r % 32)[:, None] == 1 + np.arange(NS)[None, :] // DS) | (r == 9)[:, None]
    i = np.arange(P)
    kdec = np.zeros((P, 3, 8))
    kdec[:, 0] = kdec[:, 1] = np.exp((P - 1.0 - i)[:, None] * lg()) / 8
    kdec[:NS, 2] = np.exp((DS - 1.0 - np.arange(NS) % DS)[:, None] * lg()) / 8
    t["kdec"] = kdec.reshape(P, -1)
    t["qdecs"] = np.tile(np.exp((np.arange(DS) + 1.0)[None, :] * lg()[:, None]).reshape(1, -1), (P, 1))
    gc = np.zeros((P, 4))
    for c in range(4):
        gc[:64, c], gc[64:, c] = np.exp(P * lg()[2 * c]), np.exp(P * lg()[2 * c + 1])
    t["gchunk"] = gc
    bm = np.zeros((P, DB))
    bm[:NS] = np.arange(NS)[:, None] // DS == np.arange(DB)
    t["bm"] = bm
    dm = np.zeros((P, DS))
    dm[:NS] = np.arange(NS)[:, None] % DS == np.arange(DS)
    t["dm"] = dm
    cap = np.full((P, DS), 3.0e38)
    for q in range(NS):
        cap[q, q % DS + 1:] = NEG
    t["caps"] = cap
    sel = np.zeros((P, 120))
    sel[r, 56 + DS * (r // NS) + r % DS] = 1
    t["selw"] = sel
    rep = np.zeros((P, NS))
    rep[:NS] = np.arange(NS)[:, None] % DS == np.arange(NS)[None, :] % DS
    t["rept"] = rep
    t["tri"] = r[:, None] < r[None, :]
    t["ones"] = np.ones((P, P))
    t["iota"] = np.tile(np.arange(CAP)[None, :], (P, 1))
    t["pcol"] = r[:, None] - NE * np.arange(4)[None, :]
    out, at = {}, 0
    cols = []
    for k, v in t.items():
        v = np.asarray(v, np.float32).reshape(P, -1)
        out[k] = (at, v.shape[1])
        cols.append(v)
        at += v.shape[1]
    return out, np.ascontiguousarray(np.concatenate(cols, 1))


CONST_AT, CONST = constants()


def decay_tables():
    i = np.arange(P)
    diff = i[None, :] - i[:, None]
    p = np.where(diff[:, None, :] >= 0, np.exp(np.maximum(diff, 0)[:, None, :] * lg()[None, :, None]), 0.0) / 8
    s = np.zeros((P, 8, NS))
    j = np.arange(NS)
    same = (j[:, None] // DS == j[None, :] // DS) & (j[None, :] >= j[:, None])
    d = np.maximum(j[None, :] - j[:, None], 0)
    s[:NS] = np.where(same[:, None, :], np.exp(d[:, None, :] * lg()[None, :, None]), 0.0) / 8
    q = np.zeros((P, 4, P))
    for c in range(4):
        for h in range(2):
            q[64 * h:64 * h + 64, c] = np.exp((i + 1.0) * lg()[2 * c + h])
    return [np.ascontiguousarray(x.reshape(P, -1), np.float32) for x in (p, s, q)]


def kern(nc, a):
    with ExitStack() as ctx:
        def sb(name, words, dt=F32):
            return ctx.enter_context(nc.sbuf_tensor(name, [P, words], dt))

        def sem(name):
            return ctx.enter_context(nc.semaphore(name))

        ring = sb("ring", 12 * 2048)
        z = sb("z", 3 * DIN)
        xr = sb("xr", 3 * D)
        actT = sb("actT", KT * NTOK)
        aT = sb("aT", 4 * NTOK)
        cst = sb("cst", CONST.shape[1])
        cT = sb("cT", KT * 32)
        st = sb("st", 96)
        rep_b = sb("rep_b", 512, BF16)
        pt = sb("pt", DB * NPAGES, I32)
        ps = ctx.enter_context(nc.psum_tensor("ps", [P, 8 * BANK], F32))

        def const(name):
            at, n = CONST_AT[name]
            return cst[:, at:at + n]

        def bank(b, n=1):
            return ps[:, b * BANK:(b + n) * BANK]

        z3 = z[:, :].rearrange("p (t n) -> p t n", t=3)
        x3 = xr[:, :].rearrange("p (t n) -> p t n", t=3)
        hT = actT[:, :].rearrange("p (k n) -> p k n", k=KT)
        cT3 = cT[:, :].rearrange("p (k n) -> p k n", k=KT)
        wt = [ring[:, s * 4096:(s + 1) * 4096].rearrange("p (k n) -> p k n", k=KT) for s in range(2)]
        S0 = 8192
        def scr(at, n):
            return ring[:, S0 + at:S0 + at + n]
        partA = scr(0, 2048)
        a1p, a1s = scr(2048, 1024), scr(3072, 1024)
        hrow = scr(4096, 3072).rearrange("p (t n) -> p t n", t=3)
        gmix = scr(7168, 1024)
        junk = scr(8192, 1024)
        ident = const("ident")
        sc_s = scr(0, KEYS)
        sc_p = scr(1032, 512).rearrange("p (t n) -> p t n", t=2)
        mask_s = scr(1544, 516).bitcast(BF16)
        mask_p = scr(2060, 512).rearrange("p (t n) -> p t n", t=2)
        kbd = scr(2572, 512).rearrange("p (j n) -> p j n", j=2)
        ikbd = scr(3084, 512).rearrange("p (j n) -> p j n", j=2)
        ikTn = scr(3596, NTOK)
        kTn = scr(3916, NTOK)
        iwx, iwcol = scr(4236, 64), scr(4300, 8)
        vnew = scr(4308, 1024).rearrange("p (b n) -> p b n", b=DB)
        ikn = [scr(5332 + 1024 * s, 1024).rearrange("p (n j d) -> p n j d", n=NPAGES, j=2) for s in range(2)]
        ikT = [scr(7380 + KEYS * s, KEYS) for s in range(2)]
        rel_s = scr(9444, KEYS)
        rel_p = [scr(12288, 1024).rearrange("p (h n) -> p h n", h=8), scr(13312, 2048).rearrange("p (h n) -> p h n", h=8)]
        aT3 = aT[:, :].rearrange("p (c n) -> p c n", c=4)
        kbuf = [scr(at, 1024) for at in (5332, 6356)]
        vbuf = [scr(9444, 1024), scr(10468, 1024), actT[:, 0:1024], actT[:, 1024:2048], scr(12288, 1024), scr(13312, 1024)]
        kn = [kbuf[b % 2].rearrange("p (n d) -> p n d", n=NPAGES) for b in range(DB)]
        vn = [vbuf[b % 6].rearrange("p (n d) -> p n d", n=NPAGES) for b in range(DB)]
        kT = [scr(7380 + KEYS * s, KEYS) for s in range(2)]
        p_s = scr(0, KEYS)
        pT_s, o_s = scr(2572, 1152).rearrange("p (n q) -> p n q", q=P), scr(3724, P)
        p_p = scr(12288, 2048).rearrange("p (h n) -> p h n", h=8)
        pT_p = scr(14336, 2048).rearrange("p (s h n) -> p s h n", s=2, h=8)
        rot = [scr(12288 + 512 * i, 512).rearrange("p (h n) -> p h n", h=16) for i in range(4)]
        mx, nm, rs = st[:, 48:56], st[:, 56:64], st[:, 64:72]
        partB = [z3[:, 2, 768:1280]] + [scr(14336 + 512 * i, 512) for i in range(4)] + [
            actT[:, 2048:2560]] + [
            z3[:, 0, 768:1280], z3[:, 1, 768:1280]]
        qm = scr(0, 2048).rearrange("p (h e n) -> p h e n", h=8, e=4)
        km = [scr(2048 + 1024 * i, 1024).rearrange("p (h b d) -> p h b d", h=8, b=2) for i in range(2)]
        state = scr(4096, 4096).rearrange("p (e h v) -> p e h v", e=4, h=8)
        rbd = scr(8192, 1024).rearrange("p (c j n) -> p c j n", c=4, j=2)
        rkT = scr(9216, 512).rearrange("p (c n) -> p c n", c=4)
        rqdec = scr(9728, 512).rearrange("p (c n) -> p c n", c=4)
        sT = scr(10240, 1024).rearrange("p (h n) -> p h n", h=8)
        sbd = scr(11264, 1024).rearrange("p (c j n) -> p c j n", c=4, j=2)
        s1 = scr(12288, 512).rearrange("p (c n) -> p c n", c=4)
        rkd = scr(12800, 512).rearrange("p (h d) -> p h d", h=8)
        rT = hT
        gst, gmv = scr(13312, 48).rearrange("p (h n) -> p h n", h=8), scr(13360, 16).rearrange("p (h n) -> p h n", h=8)
        dec_a, dec_b, qdec_p, dec_s = z3[:, 0, 0:768], z3[:, 1, 0:256], z3[:, 1, 256:768], z3[:, 2, 0:512]
        gt1p, a2p = z3[:, 0, 1352:2376], z3[:, 0, 2376:3400]
        sh2p, gt1s = z3[:, 1, 1352:2376], z3[:, 1, 2376:3400]
        a2s, sh2s = z3[:, 2, 1352:2376], z3[:, 2, 2376:3400]
        gt2p, gt2s = a2s, sh2s
        gffn, gfin = aT[:, 0:1024], sh2p
        h2 = z3[:, :, CRG:CGA]
        tmp3 = z3[:, :, CGB:DIN]
        wr = cT3
        br = aT[:, 1024:1024 + NE]
        def rt(at, n):
            return z3[:, 1, 2376 + at:2376 + at + n]
        lgt, lrep, ex, sel_m, gate_r = (rt(96 * i, 96).rearrange("p (t e) -> p t e", t=3) for i in range(5))
        m8r, m8s, nmr, srt = rt(480, 24), rt(504, 8), rt(512, 3), rt(516, 3)
        cnt, extra, cum, cum2, tot = rt(520, 32), rt(552, 32), rt(584, 32), rt(616, 32), rt(648, 32)
        rx, eidx = rt(680, XBLK), rt(700, XBLK)
        pos_x = rt(720, 3 * XBLK).rearrange("p (t i) -> p t i", t=3)
        gate_x = rt(780, 3 * XBLK).rearrange("p (t i) -> p t i", t=3)
        sel_x = rt(840, 4 * XBLK).rearrange("p (q i) -> p q i", q=4)
        oh = z3[:, 0, 1352:1352 + XBLK * NE].rearrange("p (i e) -> p i e", i=XBLK)
        oh2 = z3[:, 0, 0:XBLK * NE].rearrange("p (i e) -> p i e", i=XBLK)
        gT = aT[:, 0:3 * P]
        bdn = a2p
        ring3 = [ring[:, 2048 * ((k + 4) % 12):2048 * ((k + 4) % 12 + 1)] for k in range(12)]
        acc = tmp3
        xT, xg, aTt, ysb = z3[:, 0, CGA:CGA + 512], z3[:, 1, CGA:CGA + 512], z3[:, 1, CGA + 512:CGB], z3[:, 2, CGA:CGB]
        gb, ub, sgm, bgu = (actT[:, 512 * i:512 * i + 512] for i in range(4))
        ebuf = actT[:, 2048:2304].rearrange("p (q n) -> p q n", q=4)
        S = actT[:, 2304:2496].rearrange("p (t n) -> p t n", t=3)
        Sg = aT[:, 384:768].rearrange("p (t n) -> p t n", t=3)
        SgT = aT[:, 768:1088]
        pos_r = aT[:, 1088:1184].rearrange("p (t e) -> p t e", t=3)
        ikd = scr(15360, 384).rearrange("p (t n) -> p t n", t=3)
        t1, t2, t3, t4 = (scr(10500 + 240 * i, 240).rearrange("p (t h n) -> p t h n", t=3, n=8) for i in range(4))

        w_here = [sem("w_here0"), sem("w_here1")]
        c_here, x_here, g_here, b_here = sem("c_here"), sem("x_here"), sem("g_here"), sem("b_here")
        zeroed, z_zeroed = sem("zeroed"), sem("z_zeroed")
        ct_sig, ct_done = sem("ct_sig"), sem("ct_done")
        tile_done = sem("tile_done")
        part_done, tab_done = sem("part_done"), sem("tab_done")
        ss_done, var_done, rstd_done = sem("ss_done"), sem("var_done"), sem("rstd_done")
        dve_step = sem("dve_step")
        h_done, hT_ready, hT_done = sem("h_done"), sem("hT_ready"), sem("hT_done")
        z_done = sem("z_done")
        sa_tr, so_done, r_done, r_zero = sem("sa_tr"), sem("so_done"), sem("r_done"), sem("r_zero")
        pt_here = sem("pt_here")
        ik_here = [sem("ik_here0"), sem("ik_here1")]
        ikd_done, qk_roped = sem("ikd_done"), sem("qk_roped")
        tr_done, tr_act, tr_dve = sem("tr_done"), sem("tr_act"), sem("tr_dve")
        iwx_done, iw_mm, iw_done = sem("iwx_done"), sem("iw_mm"), sem("iw_done")
        pdot_done, prel_done, psc_done, pcap_done = sem("pdot_done"), sem("prel_done"), sem("psc_done"), sem("pcap_done")
        ikt_tr, ikt_done, sdot_done, srel_done, ssel_done = (
            sem("ikt_tr"), sem("ikt_done"), sem("sdot_done"), sem("srel_done"), sem("ssel_done"))
        ssc_done, pmask_raw, masks_done = sem("ssc_done"), sem("pmask_raw"), sem("masks_done")
        rep_done = sem("rep_done")
        kv_here = [sem(f"kv_here{i}") for i in range(4)]
        vnew_here = sem("vnew_here")
        rot_done, pool_step = sem("rot_done"), sem("pool_step")
        psc2_done, pmx_done, pexp_done, pp_done = sem("psc2_done"), sem("pmx_done"), sem("pexp_done"), sem("pp_done")
        ppt_tr, ppt_done, ppv_done, pa_done = sem("ppt_tr"), sem("ppt_done"), sem("ppv_done"), sem("pa_done")
        kt_tr, kt_done, ssc2_done, smx_done, sexp_done = (
            sem("kt_tr"), sem("kt_done"), sem("ssc2_done"), sem("smx_done"), sem("sexp_done"))
        spt_tr, spt_done, spv_done, sa_done = sem("spt_tr"), sem("spt_done"), sem("spv_done"), sem("sa_done")
        partb_done, gates_done = sem("partb_done"), sem("gates_done")

        ya_mm, ya_done, yb_done = sem("ya_mm"), sem("ya_done"), sem("yb_done")
        out_here, dec_here, st_here, b2_here = sem("out_here"), sem("dec_here"), sem("st_here"), sem("b2_here")
        r_tr, r_ops, r_kT, r_sc, r_sT, r_o, r_gn = (sem(n) for n in ("r_tr", "r_ops", "r_kT", "r_sc", "r_sT", "r_o", "r_gn"))
        rkd_done, r_st, r_s1, gn_var, km_done, ns_mm, ns_done, st_scaled, retp_done = (sem(n) for n in (
            "rkd_done", "r_st", "r_s1", "gn_var", "km_done", "ns_mm", "ns_done", "st_scaled", "retp_done"))
        rows_tr, rows_done, tb_mm, tb_out = sem("rows_tr"), sem("rows_done"), sem("tb_mm"), sem("tb_out")
        gb_sig, x1_done, ss2_done = sem("gb_sig"), sem("x1_done"), sem("ss2_done")
        rw_here, h2_done = sem("rw_here"), sem("h2_done")
        lg_mm, m0_done, ex_done, selm_done, pos_mm, gate_done = (sem(n) for n in (
            "lg_mm", "m0_done", "ex_done", "selm_done", "pos_mm", "gate_done"))
        h2s_done, rstd2_done, gT_tr, gT_done, ainit_mm, g2_mm, g2_done, late_here, flag_done = (sem(n) for n in (
            "h2s_done", "rstd2_done", "gT_tr", "gT_done", "ainit_mm", "g2_mm", "g2_done", "late_here", "flag_done"))
        chunk_here = [sem(f"chunk_here{k}") for k in range(12)]
        chunk_used = sem("chunk_used")
        s_done, sg_done, ebuf_done, x_mm, xg_done, xt_tr, xt_done = (sem(n) for n in (
            "s_done", "sg_done", "ebuf_done", "x_mm", "xg_done", "xt_tr", "xt_done"))
        sgt_tr, sgt_done, g_done, u_done, sig_done, act_done, at_tr, at_done, y_done, cmb_mm, acc_done = (sem(n) for n in (
            "sgt_tr", "sgt_done", "g_done", "u_done", "sig_done", "act_done", "at_tr", "at_done", "y_done", "cmb_mm", "acc_done"))
        yf_done, mul_done, fin_step = sem("yf_done"), sem("mul_done"), sem("fin_step")

        w_ada = a["w_ada"].rearrange("(k p) n -> p k n", p=P)
        w_in = a["w_in"].rearrange("(k p) n -> p k n", p=P)

        def load_attention_keys(q, b):
            def pages(*parts):
                for n in range(NPAGES):
                    page = q.value_load(pt[0:1, b * NPAGES + n:b * NPAGES + n + 1], min_val=0, max_val=NPOOL - 1)
                    src = a["cache_kv"][bass.ds(page, 1)].rearrange("a s d -> (a s) d")
                    if len(parts) == 2:
                        k, v = (x[:, n, :] for x in parts)
                        dst = bass.AP(k.tensor, k.offset, [k.ap[0], [v.offset - k.offset, 2], [1, P]])
                        q.dma_start(dst, src.rearrange("s (i d) -> s i d", i=2)).then_inc(kv_here[b % 4], 16)
                    else:
                        c = 0 if parts[0] is kn[b] else P
                        q.dma_start(parts[0][:, n, :], src[:, c:c + P]).then_inc(kv_here[b % 4], 16)

            if b == 0:
                q.wait_ge(ikt_tr, 2 * DB)
            if b < 2:
                q.wait_ge(ssel_done, PAIRS)
            elif b < 4:
                q.wait_ge(tile_done, 17)
                pages(vn[b])
                q.wait_ge(kt_tr, 2 * (b - 1))
                pages(kn[b])
                return
            else:
                q.wait_ge(kt_tr, 2 * (b - 1))
            if b in (4, 5):
                q.wait_ge(ppv_done, 2)
            if b >= 6:
                q.wait_ge(spv_done, (b - 6) // 2 + 1)
            pages(kn[b], vn[b])

        block = ctx.enter_context(nc.Block())

        @block.sync
        def _(sp):
            for i in range(4):
                if i >= 2:
                    sp.wait_ge(tile_done, i - 1)
                sp.dma_start(wt[i % 2], w_ada[:, :, i * BANK:(i + 1) * BANK]).then_inc(w_here[i % 2], 16)
            def load_z_tiles(first, last):
                with sp.Fori(first, last) as it:
                    for s in range(2):
                        sp.wait_ge(tile_done, it * 2 + (3 + s))
                        sp.dma_start(wt[s], w_in[:, :, bass.ds(it * 1024 + s * BANK, BANK)]).then_inc(w_here[s], 16)

            def load_index_keys(b):
                if b == 0:
                    sp.wait_ge(pt_here, 16)
                if b >= 2:
                    sp.wait_ge(ikt_tr, 2 * (b - 1))
                for n in range(NPAGES):
                    page = sp.value_load(pt[0:1, b * NPAGES + n:b * NPAGES + n + 1], min_val=0, max_val=NPOOL - 1)
                    src = a["cache_ik"][bass.ds(page, 1)].rearrange("a s d -> (a s) d")
                    sp.dma_start(ikn[b % 2][:, n, :, :], src.unsqueeze(1).broadcast_to([P, 2, 64])).then_inc(
                        ik_here[b % 2], 16)

            load_z_tiles(0, 1)
            sp.wait_ge(hT_ready, 6)
            load_index_keys(0)
            load_index_keys(1)
            load_z_tiles(1, 4)
            for b in range(2, DB):
                load_index_keys(b)
            load_z_tiles(4, 6)
            sp.wait_ge(tile_done, 15)
            sp.dma_start(wt[0][:, :, 0:LASTW], w_in[:, :, 12 * BANK:DIN]).then_inc(w_here[0], 16)

            def load_tile(n, src, dst=None):
                sp.wait_ge(tile_done, n - 1)
                sp.dma_start(wt[n % 2] if dst is None else dst, src).then_inc(w_here[n % 2], 16)

            for b in range(DB):
                sp.dma_start(vnew[0:DS, b, :], z3[b * DS:(b + 1) * DS, 2, CV:CIQ]).then_inc(vnew_here, 16)
            for dst, c0, c1 in (("k", CK, CV), ("v", CV, CIQ), ("ik", CIK, CIW)):
                sp.dma_start(a[dst + "_prompt"].rearrange("(t p) n -> p t n", p=P), z3[:, 0:2, c0:c1]).then_inc(out_here, 16)
                sp.dma_start(a[dst + "_sample"], z3[0:NS, 2, c0:c1]).then_inc(out_here, 16)
            load_attention_keys(sp, 0)
            for i in range(PAIRS):
                load_tile(17 + i, w_ada[:, :, (4 + i) * BANK:(5 + i) * BANK])
                if i + 1 < PAIRS:
                    load_attention_keys(sp, 2 * i + 2)
            load_tile(21, a["w_branch_a"].rearrange("(c p) n -> p c n", p=P), ring[:, 4096:8192].rearrange("p (c n) -> p c n", c=4))
            sp.wait_ge(out_here, 96)
            sp.wait_ge(ssc2_done, PAIRS)
            sp.dma_start(dec_a, a["dec_p"][:, 0:768]).then_inc(dec_here, 16)
            sp.dma_start(dec_b, a["dec_p"][:, 768:1024]).then_inc(dec_here, 16)
            sp.dma_start(qdec_p, a["qdec_p"]).then_inc(dec_here, 16)
            sp.dma_start(dec_s, a["dec_s"]).then_inc(dec_here, 16)
            load_tile(22, w_ada[:, :, 8 * BANK:9 * BANK])
            load_tile(23, w_ada[:, :, 9 * BANK:10 * BANK])
            sp.wait_ge(spv_done, PAIRS)
            for b in range(DB):
                sp.dma_start(state[64 * (b % 2):64 * (b % 2) + 64, b // 2, :, :],
                             a["state"][b].rearrange("h d v -> d h v")).then_inc(st_here, 16)
            load_tile(24, w_ada[:, :, 10 * BANK:11 * BANK])
            load_tile(25, w_ada[:, :, 11 * BANK:12 * BANK])
            w_b = a["w_branch_b"].rearrange("(k p) n -> p k n", p=P)
            w_o = a["w_out"].rearrange("(k p) n -> p k n", p=P)
            load_tile(26, w_b[:, :, 0:BANK])
            for i in range(8):
                sp.wait_ge(partb_done, i + 1)
                sp.dma_start(partB[i][9:10, :], a["b_ada"][:, (4 + i) * BANK:(5 + i) * BANK]).then_inc(b2_here, 16)
            load_tile(27, w_b[:, :, BANK:D])
            sp.dma_start(wr, a["w_router"].rearrange("(k p) e -> p k e", p=P)).then_inc(rw_here, 16)
            sp.dma_start(br, a["b_router"].partition_broadcast(P)).then_inc(rw_here, 16)
            sp.dma_start(gffn, a["norm_ffn_g"].partition_broadcast(P)).then_inc(rw_here, 16)
            sp.wait_ge(retp_done, 1)
            sp.dma_start(a["ret_prompt"].rearrange("(c j) d v -> (j d) c v", j=2), s1).then_inc(out_here, 16)
            for b in range(DB):
                sp.wait_ge(ns_done, b // 2 + 1)
                sp.dma_start(a["ret_sample"][b].rearrange("h d v -> d h v"),
                             state[64 * (b % 2):64 * (b % 2) + 64, b // 2, :, :]).then_inc(out_here, 16)
            load_tile(28, w_o[:, :, 0:BANK])
            load_tile(29, w_o[:, :, BANK:D])
            sp.wait_ge(out_here, 16 * (7 + DB))

            def chunk(e, k):
                if k < 8:
                    return sp.dma_start(ring3[k], a["w_gate_up"][bass.ds(e, 1), k * P:(k + 1) * P, :].rearrange(
                        "a p n -> (a p) n")).then_inc(chunk_here[k], 16)
                r = (k - 8) * 256
                return sp.dma_start(ring3[k].rearrange("p (i n) -> p i n", i=2),
                                    a["w_down"][bass.ds(e, 1), r:r + 256, :].rearrange(
                                        "a (i p) n -> p (a i) n", p=P)).then_inc(chunk_here[k], 16)

            for k in range(8):
                chunk(0, k)
            sp.wait_ge(h2_done, 2)
            sp.wait_ge(h2s_done, 1)
            sp.dma_start(bdn[0:NE], a["b_down"]).then_inc(late_here, 16)
            sp.dma_start(gfin, a["norm_final_g"].partition_broadcast(P)).then_inc(late_here, 16)
            sp.wait_ge(lg_mm, 1)
            sp.dma_start(bgu, a["b_gate_up"]).then_inc(late_here, 16)
            sp.wait_ge(tile_done, 29)
            chunk(0, 8)
            chunk(0, 9)
            sp.wait_ge(tile_done, 30)
            chunk(0, 10)
            chunk(0, 11)
            with sp.Fori(1, NE) as e:
                for k in range(12):
                    sp.wait_ge(chunk_used, e * 12 + (k - 11))
                    chunk(e, k)
            sp.wait_ge(flag_done, 1)
            more = sp.value_load(pt[0:1, 0:1], min_val=0, max_val=XBLK)
            with sp.If(more > 0):
                sp.wait_ge(flag_done, 2)
                with sp.Fori(0, XBLK) as i:
                    e = sp.value_load(pt[0:1, bass.ds(i + 8, 1)], min_val=0, max_val=NE - 1)
                    for k in range(12):
                        sp.wait_ge(chunk_used, i * 12 + (12 * NE + k - 11))
                        chunk(e, k)
            for t in range(3):
                sp.wait_ge(yf_done, t + 1)
                dst = a["y_prompt"][t * P:(t + 1) * P, :] if t < 2 else a["y_sample"]
                sp.dma_start(dst, x3[0:TOK[t], t, :]).then_inc(out_here, 16)
            sp.wait_ge(out_here, 16 * (7 + DB + 3))

        @block.gpsimd
        def _(pool):
            nc.gpsimd.memset(st[:, :], 1.0).then_inc(zeroed, 1)

            pool.wait_ge(g_here, 32)
            for b in range(DB):
                nc.gpsimd.tensor_scalar(rep_b[0:NS, b * NS:(b + 1) * NS], const("rept")[0:NS], const("bm")[0:NS, b:b + 1],
                                        None, ALU.mult).then_inc(rep_done, 1)
            for t in range(2):
                w = (t + 1) * P
                pool.wait_ge(psc_done, t + 1)
                nc.gpsimd.affine_select(out=sc_p[:, t, 0:w], in_=sc_p[:, t, 0:w], compare_op=ALU.is_ge, fill=NEG,
                                        base=t * P, pattern=[[-1, w]], channel_multiplier=1).then_inc(pcap_done, 1)
            pool.wait_ge(z_done, 5)
            pool.wait_ge(psc_done, 2)
            n_pool = 0
            for t in range(3):
                v = z3[:, t, CRQ:CRV].rearrange("p (h d) -> p h d", d=64)
                x1, x2 = v[:, :, 0:32], v[:, :, 32:64]
                cos, sin = (const(n).rearrange("p (t n) -> p t n", t=3)[:, t, :].unsqueeze(1).broadcast_to([P, 16, 32])
                            for n in ("cosr", "sinr"))
                for dst, x, w in ((rot[0], x1, cos), (rot[1], x2, sin), (rot[2], x2, cos), (rot[3], x1, sin)):
                    nc.gpsimd.tensor_tensor(dst, x, w, ALU.mult).then_inc(pool_step, 1)
                n_pool += 4
                pool.wait_ge(pool_step, n_pool)
                nc.gpsimd.tensor_tensor(x1, rot[0], rot[1], ALU.subtract).then_inc(pool_step, 1)
                nc.gpsimd.tensor_tensor(x2, rot[2], rot[3], ALU.add).then_inc(rot_done, 1)
                n_pool += 1
                pool.wait_ge(rot_done, t + 1)
            for t in range(2):
                w = (t + 1) * P
                pool.wait_ge(pmask_raw, t + 1)
                nc.gpsimd.affine_select(out=mask_p[:, t, 0:w], in_=mask_p[:, t, 0:w], compare_op=ALU.is_ge, fill=NEG,
                                        base=t * P, pattern=[[-1, w]], channel_multiplier=1).then_inc(pcap_done, 1)

            pool.wait_ge(pt_here, 16)
            for b in range(1, DB, 2):
                load_attention_keys(pool, b)
            pool.wait_ge(spv_done, PAIRS)
            for t in range(3):
                n = TOK[t]
                if t == 1:
                    nc.gpsimd.memset(qm, 0.0).then_inc(r_zero, 1)
                if t:
                    pool.wait_ge(r_st, t)
                kd = const("kdec").rearrange("p (t h) -> p t h", t=3)[0:n, t, :].unsqueeze(2).broadcast_to([n, 8, 64])
                nc.gpsimd.tensor_tensor(rkd[0:n], z3[0:n, t, CRK:CRV].rearrange("p (h d) -> p h d", d=64), kd,
                                        ALU.mult).then_inc(rkd_done, 1)
                if t == 0:
                    nc.gpsimd.memset(sbd, 0.0).then_inc(r_zero, 1)
            pool.wait_ge(rkd_done, 3)
            for e in range(4):
                if e >= 2:
                    pool.wait_ge(ns_mm, e - 1)
                for b in range(2):
                    last = nc.gpsimd.tensor_scalar(km[e % 2][0:NS, :, b, :], rkd[0:NS], const("bm")[0:NS, 2 * e + b:2 * e + b + 1],
                                                   None, ALU.mult)
                last.then_inc(km_done, 1)
                if e == 1:
                    pool.wait_ge(r_o, 3)
                    g8 = const("qdecs").rearrange("p (h t) -> p h t", h=8)[:, :, 7].unsqueeze(2).broadcast_to([P, 8, P])
                    for q in range(4):
                        nc.gpsimd.tensor_tensor(state[:, q], state[:, q], g8, ALU.mult).then_inc(st_scaled, 1)
            pool.wait_ge(rstd2_done, 1)
            nc.gpsimd.tensor_scalar(h2[0:NS, 2, :], x3[0:NS, 2, :], st[0:NS, 13:14], None, ALU.mult).then_inc(pool_step, 1)
            pool.wait_ge(pool_step, n_pool + 1)
            nc.gpsimd.tensor_tensor(h2[0:NS, 2, :], h2[0:NS, 2, :], a2s[0:NS], ALU.mult).then_inc(pool_step, 1)
            pool.wait_ge(pool_step, n_pool + 2)
            nc.gpsimd.tensor_tensor(h2[0:NS, 2, :], h2[0:NS, 2, :], sh2s[0:NS], ALU.add).then_inc(h2s_done, 1)

        @block.scalar
        def _(act):
            act.dma_start(cT[:, :], a["cT"]).then_inc(c_here, 16)
            act.dma_start(cst[:, :], a["const"]).then_inc(g_here, 16)
            act.dma_start(pt[0:1, :], a["page_table"]).then_inc(pt_here, 16)
            for t in range(2):
                act.dma_start(x3[:, t, :], a["x_prompt"][0, t * P:(t + 1) * P, :]).then_inc(x_here, 16)
            act.dma_start(x3[0:NS, 2, :], a["x_sample"].rearrange("b t d -> (b t) d")).then_inc(x_here, 16)
            act.dma_start(gmix, a["norm_mix_g"].partition_broadcast(P)).then_inc(g_here, 16)
            act.wait_ge(c_here, 16)
            nc.scalar.activation(junk[:, 0:256], cT[:, :], ACT.Sigmoid).then_inc(ct_sig, 1)
            act.wait_ge(x_here, 48)
            act.wait_ge(ct_done, 1)
            act.wait_ge(zeroed, 1)
            for t in range(3):
                n = TOK[t]
                nc.scalar.activation(junk[0:n, :], x3[0:n, t, :], ACT.Square,
                                     accum_out=st[0:n, t:t + 1]).then_inc(ss_done, 1)
                act.wait_ge(ss_done, t + 1)
            act.wait_ge(part_done, 4)
            act.dma_start(partA[9:10, :], a["b_ada"][:, 0:2048]).then_inc(b_here, 16)
            act.wait_ge(var_done, 1)
            nc.scalar.activation(st[:, 3:6], st[:, 0:3], ACT.Sqrt).then_inc(rstd_done, 1)
            for t in range(3):
                n = TOK[t]
                b = (4, 6, 0)[t]
                for k in range(2):
                    act.wait_ge(hT_ready, 2 * t + k + 1)
                    nc.scalar.activation(
                        hT[:, 4 * k:4 * k + 4, t * P:t * P + n],
                        bank(b + k)[:, :].rearrange("p (k n) -> p k n", k=4)[:, :, 0:n],
                        ACT.Copy).then_inc(hT_done, 1)
            def evac(col, b, w):
                h = w // 2
                nc.scalar.activation(z3[:, 0, col(0, w)], bank(b)[:, 0:w], ACT.Copy)
                nc.scalar.activation(z3[:, 1, col(0, w)], bank(b + 1)[:, 0:w], ACT.Copy)
                nc.scalar.activation(z3[0:NS, 2, col(0, h)], bank(b + 2)[0:NS, 0:h], ACT.Copy)
                nc.scalar.activation(z3[0:NS, 2, col(h, h)], bank(b + 2)[NS:P, 0:h],
                                     ACT.Copy).then_inc(z_done, 1)
            act.wait_ge(z_zeroed, 1)

            def evac_tiles(first, last):
                with act.Fori(first, last) as it:
                    for s in range(2):
                        act.wait_ge(tile_done, it * 2 + (5 + s))
                        evac(lambda o, n: bass.ds(it * 1024 + (s * BANK + o), n), 3 * s, BANK)

            evac_tiles(0, 3)
            for i, (n, dst, b, w) in enumerate(((1, ikTn, 2, NTOK), (2, z3[:, 0, CIQ:CIK], 0, 512), (3, z3[:, 1, CIQ:CIK], 1, 512),
                                                (5, z3[:, 0, CQ:CK], 4, 512), (6, z3[:, 1, CQ:CK], 5, 512),
                                                (8, kTn, 7, NTOK))):
                act.wait_ge(tr_done, n)
                nc.scalar.activation(dst, bank(b)[:, 0:w], ACT.Copy).then_inc(tr_act, 1)
            act.wait_ge(pdot_done, 1)
            nc.scalar.activation(rel_p[0], bank(0, 2).rearrange("p (h n) -> p h n", h=8), ACT.Relu).then_inc(prel_done, 1)
            act.wait_ge(pdot_done, 2)
            nc.scalar.activation(rel_p[1], bank(4, 4).rearrange("p (h n) -> p h n", h=8), ACT.Relu).then_inc(prel_done, 1)
            for b in range(DB):
                if b >= 2:
                    act.wait_ge(sdot_done, b // 2)
                nc.scalar.activation(ikT[b % 2][:, PAST:KEYS], ikTn[:, SEQ + b * DS:SEQ + (b + 1) * DS], ACT.Copy)
                for i in range(2):
                    act.wait_ge(ikt_tr, 2 * b + i + 1)
                    nc.scalar.activation(ikT[b % 2][:, i * BANK:(i + 1) * BANK], bank(6 + i), ACT.Copy).then_inc(ikt_done, 1)
            act.wait_ge(ssel_done, PAIRS)
            nc.scalar.activation(sc_s[0:NS], ps[0:NS, 0:KEYS], ACT.Copy).then_inc(ssc_done, 1)
            evac_tiles(3, 6)
            act.wait_ge(z_done, 12)
            for t in range(3):
                n = TOK[t]
                nc.scalar.activation(z3[0:n, t, CRG:CGA], z3[0:n, t, CRG:CGA], ACT.Silu).then_inc(gates_done, 1)
            for t in range(3):
                n = TOK[t]
                nc.scalar.activation(z3[0:n, t, CGA:CGB], z3[0:n, t, CGA:CGB], ACT.Sigmoid).then_inc(gates_done, 1)
            act.wait_ge(tile_done, 17)
            evac(lambda o, n: slice(12 * BANK + o, 12 * BANK + o + n), 0, LASTW)

            def keys_out(b):
                if b >= 2:
                    act.wait_ge(ssc2_done, b // 2)
                nc.scalar.activation(kT[b % 2][:, PAST:KEYS], kTn[:, SEQ + b * DS:SEQ + (b + 1) * DS], ACT.Copy)
                for i in range(2):
                    act.wait_ge(kt_tr, 2 * b + i + 1)
                    nc.scalar.activation(kT[b % 2][:, i * BANK:(i + 1) * BANK], bank(6 + i), ACT.Copy).then_inc(kt_done, 1)

            for t in range(2):
                w = (t + 1) * P
                if t:
                    keys_out(0)
                    keys_out(1)
                act.wait_ge(pmx_done, t + 1)
                if t:
                    act.wait_ge(ppt_tr, 1)
                for g in range(8):
                    nc.scalar.activation(p_p[:, g, 0:w], p_p[:, g, 0:w], ACT.Exp, bias=nm[:, g:g + 1], scale=ATT_SCALE,
                                         accum_out=rs[:, g:g + 1]).then_inc(pexp_done, 1)
                act.wait_ge(ppt_tr, t + 1)
                b0 = (4, 0)[t]
                if t:
                    act.wait_ge(ppv_done, 1)
                nc.scalar.activation(pT_p[:, 0:t + 1, :, :], bank(b0, 2 * (t + 1)).rearrange("p (s h n) -> p s h n", h=8, n=P),
                                     ACT.Copy).then_inc(ppt_done, 1)
                act.wait_ge(ppv_done, t + 1)
                b0 = (6, 4)[t]
                v = bank(b0, 2).rearrange("p (c j n) -> p c j n", c=4, j=2)
                nc.scalar.activation(aT3[0:64, :, t * P:(t + 1) * P], v[0:64, :, 0, :], ACT.Copy)
                nc.scalar.activation(aT3[64:P, :, t * P:(t + 1) * P], v[64:P, :, 1, :], ACT.Copy).then_inc(pa_done, 1)
            def sample_rows_out(i):
                act.wait_ge(sa_tr, i + 1)
                v = bank(5)[:, P:2 * P].rearrange("p (s j c t) -> p j c s t", s=2, j=2, c=4)
                o = aT3[:, :, SEQ + 2 * i * DS:SEQ + 2 * (i + 1) * DS].rearrange("p c (s t) -> p c s t", s=2)
                nc.scalar.activation(o[0:64], v[0:64, 0], ACT.Copy)
                nc.scalar.activation(o[64:P], v[64:P, 1], ACT.Copy).then_inc(sa_done, 1)

            for i in range(PAIRS):
                act.wait_ge(smx_done, i + 1)
                if i:
                    act.wait_ge(spt_tr, i)
                if i >= 2:
                    act.wait_ge(so_done, i - 1)
                nc.scalar.activation(p_s, ps[:, 0:KEYS], ACT.Exp, bias=nm[:, 0:1], scale=ATT_SCALE,
                                     accum_out=rs[:, i % 2:i % 2 + 1]).then_inc(sexp_done, 1)
                if i + 1 < PAIRS:
                    keys_out(2 * i + 2)
                    keys_out(2 * i + 3)
                if i:
                    sample_rows_out(i - 1)
            sample_rows_out(PAIRS - 1)
            for t in range(3):
                n = TOK[t]
                nc.scalar.activation(z3[0:n, t, CGB:DIN], z3[0:n, t, CGB:DIN], ACT.Sigmoid).then_inc(gb_sig, 1)
            def ret_keys_out(t):
                n = TOK[t]
                if t:
                    act.wait_ge(r_sc, t)
                else:
                    act.wait_ge(spv_done, PAIRS)
                act.wait_ge(r_tr, 2 * t + 2)
                nc.scalar.activation(rkT[:, :, 0:n], bank(1)[:, 0:4 * n].rearrange("p (c n) -> p c n", c=4),
                                     ACT.Copy).then_inc(r_kT, 1)

            ret_keys_out(0)
            act.wait_ge(r_s1, 1)
            act.wait_ge(r_zero, 1)
            kvp = bank(6, 2).rearrange("p (c j n) -> p c j n", c=4, j=2)
            nc.scalar.activation(sbd[0:64, :, 0], kvp[0:64, :, 0], ACT.Copy)
            nc.scalar.activation(sbd[64:P, :, 1], kvp[64:P, :, 1], ACT.Copy).then_inc(r_s1, 1)
            for t in range(3):
                if t < 2:
                    ret_keys_out(t + 1)
                n = TOK[t]
                act.wait_ge(gn_var, t + 1)
                nc.scalar.activation(st[0:n, 24:32], st[0:n, 16:24], ACT.Sqrt).then_inc(rstd_done, 1)

            def transposed_out(turn, dst):
                for t in range(3):
                    n, b = TOK[t], (0, 2, 6)[t]
                    for i in range(2):
                        act.wait_ge(rows_tr, 6 * turn + 2 * t + i + 1)
                        nc.scalar.activation(dst[:, 4 * i:4 * i + 4, t * P:t * P + n],
                                             bank(b + i).rearrange("p (k n) -> p k n", k=4)[:, :, 0:n],
                                             ACT.Copy).then_inc(rows_done, 1)

            for i, (dst, n) in enumerate(((gt1p, P), (gt1s, NS), (sh2p, P), (sh2s, NS), (a2p, P), (a2s, NS))):
                act.wait_ge(tb_mm, i + 1)
                nc.scalar.activation(dst[0:n], bank((0, 6)[i % 2], 2)[0:n], ACT.Copy).then_inc(tb_out, 1)
            transposed_out(0, rT)
            transposed_out(1, hT)
            for t in range(3):
                n = TOK[t]
                act.wait_ge(x1_done, t + 1)
                nc.scalar.activation(z3[0:n, t, CGA:CGB], x3[0:n, t, :], ACT.Square,
                                     accum_out=st[0:n, 8 + t:9 + t]).then_inc(ss2_done, 1)
            act.wait_ge(var_done, 2)
            nc.scalar.activation(st[:, 11:14], st[:, 8:11], ACT.Sqrt).then_inc(rstd_done, 1)
            transposed_out(2, hT)
            act.wait_ge(g2_mm, 1)
            nc.scalar.activation(gt2p, bank(0, 2), ACT.Copy).then_inc(g2_done, 1)
            act.wait_ge(g2_mm, 2)
            nc.scalar.activation(gt2s[0:NS, 0:BANK], bank(2)[0:NS], ACT.Copy)
            nc.scalar.activation(gt2s[0:NS, BANK:D], bank(4)[0:NS], ACT.Copy).then_inc(g2_done, 1)
            act.wait_ge(m0_done, 1)
            for t in range(3):
                n = TOK[t]
                nc.scalar.activation(ex[0:n, t, :], lgt[0:n, t, :], ACT.Exp, bias=nmr[0:n, t:t + 1]).then_inc(ex_done, 1)
            act.wait_ge(gT_tr, 1)
            nc.scalar.activation(gT[0:NE], bank(7)[0:NE, 0:3 * P], ACT.Copy).then_inc(gT_done, 1)
            def x_out(n):
                act.wait_ge(x_mm, n + 1)
                nc.scalar.activation(xg, bank(3), ACT.Copy).then_inc(xg_done, 1)

            def xt_out(n):
                act.wait_ge(xt_tr, n + 1)
                nc.scalar.activation(xT, bank(5), ACT.Copy).then_inc(xt_done, 1)

            def gather_out(n):
                act.wait_ge(sgt_tr, n + 1)
                nc.scalar.activation(SgT[0:NS, :], bank(4)[0:NS, 0:NTOK], ACT.Copy).then_inc(sgt_done, 1)

            def expert(n, first, last):
                if not first:
                    gather_out(n - 1)
                act.wait_ge(g_done, n + 1)
                nc.scalar.activation(sgm, gb, ACT.Sigmoid, scale=1.702).then_inc(sig_done, 1)
                if not last:
                    x_out(n + 1)
                    xt_out(n + 1)
                act.wait_ge(at_tr, n + 1)
                nc.scalar.activation(aTt, bank(4), ACT.Copy).then_inc(at_done, 1)
                act.wait_ge(chunk_used, n * 12 + 12)
                if not first:
                    act.wait_ge(cmb_mm, n * 5)
                nc.scalar.activation(ysb[0:NS, 0:512], bank(2)[0:NS], ACT.Copy)
                nc.scalar.activation(ysb[0:NS, 512:D], bank(2)[NS:P], ACT.Copy).then_inc(y_done, 1)

            def sum_out(t, banks):
                act.wait_ge(ainit_mm, t + 1)
                for i in range(2):
                    last = nc.scalar.activation(acc[0:TOK[t], t, i * BANK:(i + 1) * BANK], bank(banks[i])[0:TOK[t]], ACT.Copy)
                last.then_inc(acc_done, 1)

            def experts(count, base):
                x_out(base)
                if base == 0:
                    sum_out(0, (0, 1))
                    sum_out(1, (2, 4))
                xt_out(base)
                if base == 0:
                    sum_out(2, (6, 7))
                expert(base, True, False)
                with act.Fori(1, count - 1) as i:
                    expert(i + base, False, False)
                expert(base + count - 1, False, True)
                gather_out(base + count - 1)

            experts(NE, 0)
            act.wait_ge(flag_done, 1)
            more = act.value_load(pt[0:1, 0:1], min_val=0, max_val=XBLK)
            with act.If(more > 0):
                experts(XBLK, NE)
            for t in range(3):
                n = TOK[t]
                act.wait_ge(x1_done, t + 4)
                nc.scalar.activation(z3[0:n, t, CGA:CGB], x3[0:n, t, :], ACT.Square,
                                     accum_out=st[0:n, 8 + t:9 + t]).then_inc(ss2_done, 1)
            act.wait_ge(var_done, 3)
            nc.scalar.activation(st[:, 11:14], st[:, 8:11], ACT.Sqrt).then_inc(rstd_done, 1)

        @block.tensor
        def _(pe):
            pe.wait_ge(ct_done, 1)
            for i in range(4):
                pe.wait_ge(w_here[i % 2], 16 * (i // 2 + 1))
                for k in range(KT):
                    g = k % 4
                    last = nc.tensor.matmul(bank(i)[32 * g:32 * g + 32, :], cT3[:, k, :], wt[i % 2][:, k, :],
                                            start=k < 4, stop=k >= 4)
                last.then_inc(tile_done, 1)
            pe.wait_ge(b_here, 16)
            pe.wait_ge(g_here, 32)
            for sel, rows, b0 in ((const("selp"), P, 4), (const("sels"), NS, 0)):
                for j in range(4):
                    src = (j + 2) % 4
                    nc.tensor.matmul(bank(b0 + j)[0:rows, :], sel, partA[:, src * BANK:(src + 1) * BANK],
                                     start=True, stop=True).then_inc(tab_done, 1)
            for t in range(3):
                n = TOK[t]
                b = (4, 6, 0)[t]
                pe.wait_ge(h_done, t + 1)
                for k in range(KT):
                    last = nc.tensor.transpose(bank(b + k // 4)[:, (k % 4) * P:(k % 4) * P + n],
                                               hrow[0:n, t, k * P:(k + 1) * P], ident[0:n, 0:n])
                    if k % 4 == 3:
                        last.then_inc(hT_ready, 1)
            pe.wait_ge(hT_done, 6)

            def project(wtile, b, w, x=hT, kt=KT, done=tile_done):
                h = w // 2
                for k in range(kt):
                    se = dict(start=k == 0, stop=k == kt - 1)
                    nc.tensor.matmul(bank(b)[:, 0:w], x[:, k, 0:P], wtile[:, k, 0:w], **se)
                    nc.tensor.matmul(bank(b + 1)[:, 0:w], x[:, k, P:2 * P], wtile[:, k, 0:w], **se)
                    nc.tensor.matmul(bank(b + 2)[0:NS, 0:h], x[:, k, 2 * P:NTOK], wtile[:, k, 0:h], **se)
                    last = nc.tensor.matmul(bank(b + 2)[NS:P, 0:h], x[:, k, 2 * P:NTOK], wtile[:, k, h:w], **se)
                last.then_inc(done, 1)

            def project_tiles(first, last):
                with pe.Fori(first, last) as it:
                    for s in range(2):
                        pe.wait_ge(w_here[s], it * 16 + 48)
                        if first or s:
                            pe.wait_ge(z_done, it * 2 - (1 - s))
                        project(wt[s], 3 * s, BANK)

            pe.wait_ge(w_here[0], 48)
            project(wt[0], 0, BANK)
            pe.wait_ge(w_here[1], 48)
            project(wt[1], 3, BANK)
            project_tiles(1, 3)
            pe.wait_ge(z_done, 6)
            pe.wait_ge(ikd_done, 1)
            pe.wait_ge(qk_roped, 1)
            for t in range(3):
                n = TOK[t]
                last = nc.tensor.transpose(bank(2)[:, t * P:t * P + n], ikd[0:n, t, :], ident[0:n, 0:n])
            last.then_inc(tr_done, 1)
            for col, banks in ((CIQ, (0, 1, 3)), (CQ, (4, 5, 6))):
                for t in range(3):
                    n = TOK[t]
                    for c in range(4):
                        last = nc.tensor.transpose(bank(banks[t])[:, c * n:(c + 1) * n],
                                                   z3[0:n, t, col + c * P:col + (c + 1) * P], ident[0:n, 0:n])
                    last.then_inc(tr_done, 1)
            for t in range(3):
                n = TOK[t]
                last = nc.tensor.transpose(bank(7)[:, t * P:t * P + n], z3[0:n, t, CK:CV], ident[0:n, 0:n])
            last.then_inc(tr_done, 1)
            pe.wait_ge(tr_dve, 1)
            pe.wait_ge(tr_act, 3)
            for c in range(4):
                last = nc.tensor.matmul(bank(c // 2)[:, (c % 2) * 256:(c % 2 + 1) * 256],
                                        z3[:, 0, CIQ + c * P:CIQ + (c + 1) * P], ikbd[:, :, 0:P],
                                        start=True, stop=True)
            last.then_inc(pdot_done, 1)
            pe.wait_ge(tr_act, 6)
            pe.wait_ge(tr_dve, 3)
            for c in range(4):
                last = nc.tensor.matmul(bank(4 + c), z3[:, 1, CIQ + c * P:CIQ + (c + 1) * P], ikbd[:, :, :],
                                        start=True, stop=True)
            last.then_inc(pdot_done, 1)
            pe.wait_ge(iwx_done, 1)
            for h in range(2):
                last = nc.tensor.matmul(bank(3)[NS * h:NS * h + NS, 0:PAIRS], iwx[0:NS],
                                        const("bm")[0:NS].rearrange("p (i h) -> p h i", h=2)[:, h, :], start=True, stop=True)
            last.then_inc(iw_mm, 1)

            def index_transpose(b):
                pe.wait_ge(ik_here[b % 2], 16 * NPAGES * (b // 2 + 1))
                for i in range(2):
                    if b:
                        pe.wait_ge(ikt_done, 2 * b - 1 + i)
                    else:
                        pe.wait_ge(prel_done, 2)
                    for n in range(4):
                        last = nc.tensor.transpose(bank(6 + i)[:, n * P:(n + 1) * P],
                                                   ikn[b % 2][:, 4 * i + n, :, :].rearrange("p j d -> p (j d)"), ident)
                    last.then_inc(ikt_tr, 1)

            iq_s = z3[:, 2, CIQ:CIK]
            index_transpose(0)
            index_transpose(1)
            pe.wait_ge(iw_done, 1)
            for i in range(PAIRS):
                pe.wait_ge(ikt_done, 4 * i + 4)
                if i:
                    pe.wait_ge(srel_done, i)
                for k, w in ((0, BANK), (1, BANK), (2, DS)):
                    for h in range(2):
                        b = 2 * i + h
                        last = nc.tensor.matmul(bank(3 + k)[NS * h:NS * h + NS, 0:w], iq_s[:, b * NS:(b + 1) * NS],
                                                ikT[h][:, k * BANK:k * BANK + w], start=True, stop=True)
                last.then_inc(sdot_done, 1)
                if i + 1 < PAIRS:
                    index_transpose(2 * i + 2)
                    index_transpose(2 * i + 3)
                pe.wait_ge(srel_done, i + 1)
                for k, w in ((0, BANK), (1, BANK), (2, DS)):
                    last = nc.tensor.matmul(bank(k)[0:NS, 0:w], const("selw")[:, 56 - 2 * DS * i:56 - 2 * DS * i + NS],
                                            rel_s[:, k * BANK:k * BANK + w], start=i == 0, stop=i == PAIRS - 1)
                last.then_inc(ssel_done, 1)
            pe.wait_ge(ssc_done, 1)
            project_tiles(3, 6)
            pe.wait_ge(w_here[0], 16 * 9)
            pe.wait_ge(z_done, 11)
            project(wt[0], 0, LASTW)

            def prompt_scores(t, b0):
                w = (t + 1) * P
                for c in range(4):
                    last = nc.tensor.matmul(ps[:, b0 * BANK + c * 2 * w:b0 * BANK + (c + 1) * 2 * w],
                                            z3[:, t, CQ + c * P:CQ + (c + 1) * P], kbd[:, :, 0:w], start=True, stop=True)
                last.then_inc(psc2_done, 1)

            def prompt_values(t, b0, b1):
                pe.wait_ge(pp_done, t + 1)
                for s in range(t + 1):
                    for g in range(8):
                        last = nc.tensor.transpose(ps[:, b0 * BANK + (8 * s + g) * P:b0 * BANK + (8 * s + g + 1) * P],
                                                   p_p[:, g, s * P:(s + 1) * P], ident)
                last.then_inc(ppt_tr, 1)
                pe.wait_ge(ppt_done, t + 1)
                for c in range(4):
                    for s in range(t + 1):
                        last = nc.tensor.matmul(ps[:, b1 * BANK + c * 256:b1 * BANK + (c + 1) * 256],
                                                z3[:, s, CV:CIQ], pT_p[:, s, 2 * c:2 * c + 2, :], start=s == 0, stop=s == t)
                last.then_inc(ppv_done, 1)

            pe.wait_ge(tr_dve, 4)
            pe.wait_ge(ikt_done, 2 * DB)
            prompt_scores(0, 6)
            pe.wait_ge(z_done, NZT)
            prompt_scores(1, 0)
            prompt_values(0, 4, 6)

            def key_transpose(b):
                pe.wait_ge(kv_here[b % 4], 16 * NPAGES * (b // 4 + 1 + (b % 4 >= 2)))
                for i in range(2):
                    if b:
                        pe.wait_ge(kt_done, 2 * b - 1 + i)
                    else:
                        pe.wait_ge(pa_done, 1)
                    for n in range(4):
                        last = nc.tensor.transpose(bank(6 + i)[:, n * P:(n + 1) * P], kn[b][:, 4 * i + n, :], ident)
                    last.then_inc(kt_tr, 1)

            key_transpose(0)
            key_transpose(1)
            prompt_values(1, 0, 4)
            pe.wait_ge(masks_done, 1)
            pe.wait_ge(rep_done, DB)
            pe.wait_ge(ppt_done, 2)
            pe.wait_ge(pa_done, 2)
            pe.wait_ge(vnew_here, 16 * DB)

            def modulation_tile(n, b):
                pe.wait_ge(w_here[n % 2], 16 * (n // 2 + 1))
                for k in range(KT):
                    g = k % 4
                    last = nc.tensor.matmul(bank(b)[32 * g:32 * g + 32, :], cT3[:, k, :], wt[n % 2][:, k, :],
                                            start=k < 4, stop=k >= 4)
                last.then_inc(tile_done, 1)

            def sample_rows(i):
                pe.wait_ge(so_done, i + 1)
                nc.tensor.transpose(bank(5)[:, P:2 * P], o_s, ident).then_inc(sa_tr, 1)

            for i in range(PAIRS):
                pe.wait_ge(kt_done, 4 * i + 4)
                if i:
                    pe.wait_ge(sexp_done, i)
                for k, w in ((0, BANK), (1, BANK), (2, DS)):
                    for h in range(2):
                        b = 2 * i + h
                        nc.tensor.matmul(bank(k)[NS * h:NS * h + NS, 0:w], z3[:, 2, CQ + b * NS:CQ + (b + 1) * NS],
                                         kT[h][:, k * BANK:k * BANK + w], start=True, stop=False)
                    for h in range(2):
                        b = 2 * i + h
                        last = nc.tensor.matmul(bank(k)[NS * h:NS * h + NS, 0:w], rep_b[0:NS, b * NS:(b + 1) * NS],
                                                mask_s[0:NS, k * BANK:k * BANK + w], start=False, stop=True)
                last.then_inc(ssc2_done, 1)
                if i + 1 < PAIRS:
                    key_transpose(2 * i + 2)
                    key_transpose(2 * i + 3)
                if i:
                    pe.wait_ge(spt_done, i)
                modulation_tile(17 + i, 3)
                if i:
                    sample_rows(i - 1)
                pe.wait_ge(sexp_done, i + 1)
                pe.wait_ge(partb_done, i + 1)
                for n in range(NPAGES):
                    nc.tensor.transpose(bank(3 + n // 4)[:, (n % 4) * P:(n % 4 + 1) * P], p_s[:, n * P:(n + 1) * P], ident)
                nc.tensor.transpose(bank(2)[0:DS, P:2 * P], p_s[:, PAST:KEYS], ident).then_inc(spt_tr, 1)
                pe.wait_ge(spt_done, i + 1)
                if i:
                    pe.wait_ge(sa_done, i)
                for n in range(NPAGES + 1):
                    for h in range(2):
                        b = 2 * i + h
                        kk = P if n < NPAGES else DS
                        v = vn[b][:, n, :] if n < NPAGES else vnew[0:DS, b, :]
                        last = nc.tensor.matmul(bank(5)[NS * h:NS * h + NS, 0:P], pT_s[0:kk, n, NS * h:NS * h + NS], v,
                                                start=n == 0, stop=n == NPAGES)
                last.then_inc(spv_done, 1)
            sample_rows(PAIRS - 1)
            pe.wait_ge(sa_done, PAIRS)
            pe.wait_ge(w_here[1], 16 * 11)
            wt_a = ring[:, 4096:8192].rearrange("p (c n) -> p c n", c=4)
            project(wt_a[:, :, 0:BANK], 0, BANK, aT3, 4, ya_mm)
            project(wt_a[:, :, BANK:D], 3, BANK, aT3, 4)
            for h in range(2):
                modulation_tile(22 + h, 6 + h)
            pe.wait_ge(ya_done, 2)
            def ret_transposes(t):
                n = TOK[t]
                for b, col in ((0, CRQ), (1, CRK)):
                    for c in range(4):
                        last = nc.tensor.transpose(bank(b)[:, c * n:(c + 1) * n], z3[0:n, t, col + c * P:col + (c + 1) * P],
                                                   ident[0:n, 0:n])
                    last.then_inc(r_tr, 1)

            def ret_state(t):
                pe.wait_ge(rkd_done, t + 1)
                for c in range(4):
                    last = nc.tensor.matmul(ps[:, 6 * BANK + 256 * c:6 * BANK + 256 * (c + 1)],
                                            rkd[:, 2 * c:2 * c + 2, :].rearrange("p h d -> p (h d)"),
                                            z3[:, t, CRV + 256 * c:CRV + 256 * (c + 1)], start=True, stop=True)
                last.then_inc(r_st, 1)

            ret_transposes(0)
            pe.wait_ge(partb_done, 6)
            ret_state(0)
            for t in range(3):
                n = TOK[t]
                pe.wait_ge(r_ops, t + 1)
                pe.wait_ge(r_kT, t + 1)
                if t == 2:
                    pe.wait_ge(partb_done, 7)
                for c in range(4):
                    last = nc.tensor.matmul(ps[0:n, 2 * BANK + 2 * c * n:2 * BANK + 2 * (c + 1) * n], rkT[:, c, 0:n],
                                            rbd[:, c, :, 0:n], start=True, stop=True)
                last.then_inc(r_sc, 1)
                if t < 2:
                    ret_transposes(t + 1)
                pe.wait_ge(r_sT, t + 1)
                if t == 1:
                    pe.wait_ge(r_s1, 2)
                    ret_state(1)
                if t:
                    modulation_tile(23 + t, 2)
                    pe.wait_ge(r_gn, t)
                if t == 2:
                    pe.wait_ge(st_here, 16 * DB)
                for c in range(4):
                    o = ps[0:n, 4 * BANK + 256 * c:4 * BANK + 256 * (c + 1)]
                    if t == 1:
                        nc.tensor.matmul(o, rqdec[:, c, :], sbd[:, c, :, :], start=True, stop=False)
                    for h in (2 * c, 2 * c + 1):
                        oh_ = o[:, (h % 2) * P:(h % 2 + 1) * P]
                        if t == 2:
                            for e in range(4):
                                nc.tensor.matmul(oh_, qm[:, h, e, :], state[:, e, h, :], start=e == 0, stop=False)
                        last = nc.tensor.matmul(oh_, sT[0:n, h, 0:n], z3[0:n, t, CRV + h * P:CRV + (h + 1) * P],
                                                start=t == 0, stop=t != 1 or h % 2 == 1)
                last.then_inc(r_o, 1)
            for e in range(4):
                pe.wait_ge(km_done, e + 1)
                b = (6, 0)[e % 2]
                if e == 0:
                    pe.wait_ge(retp_done, 1)
                if e >= 2:
                    pe.wait_ge(ns_done, e - 1)
                for h in range(8):
                    last = nc.tensor.matmul(ps[:, b * BANK + P * h:b * BANK + P * (h + 1)],
                                            km[e % 2][0:NS, h, :, :].rearrange("p b d -> p (b d)"),
                                            z3[0:NS, 2, CRV + h * P:CRV + (h + 1) * P], start=True, stop=True)
                last.then_inc(ns_mm, 1)
            pe.wait_ge(r_done, 3)
            pe.wait_ge(ns_done, 4)

            def transpose_rows(src, waits=()):
                for t in range(3):
                    if waits:
                        pe.wait_ge(*waits[t])
                    n, b = TOK[t], (0, 2, 6)[t]
                    for k in range(KT):
                        last = nc.tensor.transpose(bank(b + k // 4)[:, (k % 4) * P:(k % 4) * P + n],
                                                   src[0:n, t, k * P:(k + 1) * P], ident[0:n, 0:n])
                        if k % 4 == 3:
                            last.then_inc(rows_tr, 1)

            pe.wait_ge(b2_here, 16 * 8)
            for i in range(6):
                sel, n = ((const("selp"), P), (const("sels"), NS))[i % 2]
                if i >= 2:
                    pe.wait_ge(tb_out, i - 1)
                for k in range(2):
                    last = nc.tensor.matmul(bank((0, 6)[i % 2] + k)[0:n, :], sel, partB[2 * (i // 2) + k], start=True, stop=True)
                last.then_inc(tb_mm, 1)
            pe.wait_ge(tb_out, 6)
            transpose_rows(h2)
            pe.wait_ge(rows_done, 6)
            pe.wait_ge(w_here[0], 16 * 14)
            project(wt[0], 0, BANK, rT)
            pe.wait_ge(w_here[1], 16 * 14)
            project(wt[1], 3, BANK, rT)
            pe.wait_ge(yb_done, 2)
            transpose_rows(z3[:, :, CGA:CGB])
            pe.wait_ge(rows_done, 12)
            pe.wait_ge(w_here[0], 16 * 15)
            project(wt[0], 0, BANK)
            pe.wait_ge(w_here[1], 16 * 15)
            project(wt[1], 3, BANK)
            transpose_rows(h2, ((h2_done, 1), (h2_done, 2), (h2s_done, 1)))
            pe.wait_ge(rows_done, 18)
            pe.wait_ge(rw_here, 48)
            for t in range(3):
                n = TOK[t]
                for k in range(KT):
                    last = nc.tensor.matmul(bank(5)[0:n, t * NE:(t + 1) * NE], hT[:, k, t * P:t * P + n], wr[:, k, :],
                                            start=k == 0, stop=k == KT - 1)
            last.then_inc(lg_mm, 1)
            for (sel, n), banks in (((const("selp"), P), (0, 1)), ((const("sels"), NS), (2, 4))):
                for i in range(2):
                    last = nc.tensor.matmul(bank(banks[i])[0:n, :], sel, partB[6 + i], start=True, stop=True)
                last.then_inc(g2_mm, 1)
            pe.wait_ge(selm_done, 1)
            for t in range(4):
                for i in range(min(t, 2) + 1):
                    last = nc.tensor.matmul(bank(6)[:, t * NE:(t + 1) * NE], const("tri") if i == t else const("ones"),
                                            sel_m[:, i, :], start=i == 0, stop=i == min(t, 2))
            last.then_inc(pos_mm, 1)
            pe.wait_ge(gate_done, 1)
            for t in range(3):
                last = nc.tensor.transpose(bank(7)[0:NE, t * P:(t + 1) * P], gate_r[:, t, :], ident)
            last.then_inc(gT_tr, 1)

            def start_sum(t, banks):
                n = TOK[t]
                for i in range(2):
                    last = nc.tensor.matmul(bank(banks[i])[0:n, :], gT[0:NE, t * P:t * P + n], bdn[0:NE, i * BANK:(i + 1) * BANK],
                                            start=True, stop=True)
                last.then_inc(ainit_mm, 1)

            def x_rows(n, n_zero=False):
                pe.wait_ge(s_done, n + 1)
                if not n_zero:
                    pe.wait_ge(xg_done, n)
                for t in range(3):
                    for i in range(2):
                        last = nc.tensor.matmul(bank(3)[64 * i:64 * i + 64, :], S[:, t, :], h2[:, t, i * BANK:(i + 1) * BANK],
                                                start=t == 0, stop=t == 2)
                last.then_inc(x_mm, 1)

            def x_transpose(n):
                pe.wait_ge(xg_done, n + 1)
                for c in range(4):
                    last = nc.tensor.transpose(bank(5)[:, c * P:(c + 1) * P], xg[:, c * P:(c + 1) * P], ident)
                last.then_inc(xt_tr, 1)

            def combine(n, gate_tr):
                if gate_tr:
                    pe.wait_ge(sg_done, n + 1)
                    pe.wait_ge(at_done, n + 1)
                    for t in range(3):
                        last = nc.tensor.transpose(bank(4)[:, t * P:t * P + TOK[t]], Sg[0:TOK[t], t, :],
                                                   ident[0:TOK[t], 0:TOK[t]])
                    last.then_inc(sgt_tr, 1)
                    return
                pe.wait_ge(y_done, n + 1)
                pe.wait_ge(sgt_done, n + 1)
                for i, (t, half) in enumerate(PIECES):
                    if i == 0:
                        pe.wait_ge(acc_done, n * 5 + 3)
                    if i >= 2:
                        pe.wait_ge(acc_done, n * 5 + (i + 2))
                    b = 6 + i % 2
                    if t < 2:
                        nc.tensor.matmul(bank(b), SgT[0:NS, t * P:(t + 1) * P], ysb[0:NS, half * BANK:(half + 1) * BANK],
                                         start=True, stop=True).then_inc(cmb_mm, 1)
                    else:
                        for half in range(2):
                            last = nc.tensor.matmul(bank(b)[64 * half:64 * half + 64, :], SgT[0:NS, 2 * P:NTOK],
                                                    ysb[0:NS, half * BANK:(half + 1) * BANK], start=True, stop=True)
                        last.then_inc(cmb_mm, 1)

            def expert(n, here, first, last_one):
                pe.wait_ge(ebuf_done, n + 1)
                pe.wait_ge(xt_done, n + 1)
                if not first:
                    pe.wait_ge(u_done, n)
                for q in range(4):
                    nc.tensor.matmul(bank(q // 2)[64 * (q % 2):64 * (q % 2) + 64, :], ebuf[:, q, :], bgu, start=True, stop=False)
                for k in range(8):
                    pe.wait_ge(chunk_here[k], here)
                    lhs = xT[:, (k % 4) * P + 64 * (k // 4):(k % 4) * P + 64 * (k // 4) + 64]
                    for q in range(4):
                        last = nc.tensor.matmul(bank(q // 2)[64 * (q % 2):64 * (q % 2) + 64, :], lhs,
                                                ring3[k][:, q * BANK:(q + 1) * BANK], start=False, stop=k == 7)
                    last.then_inc(chunk_used, 1)
                if not first:
                    combine(n - 1, True)
                if not last_one:
                    x_rows(n + 1)
                if not first:
                    combine(n - 1, False)
                if not last_one:
                    x_transpose(n + 1)
                pe.wait_ge(act_done, n + 1)
                if not first:
                    pe.wait_ge(at_done, n)
                for c in range(4):
                    last = nc.tensor.transpose(bank(4)[:, c * P:(c + 1) * P], gb[:, c * P:(c + 1) * P], ident)
                last.then_inc(at_tr, 1)
                pe.wait_ge(at_done, n + 1)
                if not first:
                    pe.wait_ge(y_done, n)
                for k in range(8):
                    if k % 2 == 0:
                        pe.wait_ge(chunk_here[8 + k // 2], here)
                    lhs = aTt[:, (k % 4) * P + 64 * (k // 4):(k % 4) * P + 64 * (k // 4) + 64]
                    for q in range(2):
                        last = nc.tensor.matmul(bank(2)[64 * q:64 * q + 64, :], lhs,
                                                ring3[8 + k // 2][:, (k % 2) * D + q * BANK:(k % 2) * D + (q + 1) * BANK],
                                                start=k == 0, stop=k == 7)
                    if k % 2:
                        last.then_inc(chunk_used, 1)

            def experts(count, base):
                x_rows(base, base == 0)
                if base == 0:
                    pe.wait_ge(gT_done, 1)
                    pe.wait_ge(late_here, 48)
                    pe.wait_ge(g2_done, 2)
                    start_sum(0, (0, 1))
                    start_sum(1, (2, 4))
                x_transpose(base)
                if base == 0:
                    pe.wait_ge(flag_done, 1)
                    start_sum(2, (6, 7))
                    pe.wait_ge(acc_done, 3)
                expert(base, 16 * (base + 1), True, False)
                with pe.Fori(1, count - 1) as i:
                    expert(i + base, i * 16 + 16 * (base + 1), False, False)
                n = base + count - 1
                expert(n, 16 * (n + 1), False, True)
                combine(n, True)
                combine(n, False)

            experts(NE, 0)
            more = pe.value_load(pt[0:1, 0:1], min_val=0, max_val=XBLK)
            with pe.If(more > 0):
                experts(XBLK, NE)

        @block.vector
        def _(dve):
            steps = [0]

            def step(ins):
                steps[0] += 1
                ins.then_inc(dve_step, 1)
                dve.wait_ge(dve_step, steps[0])

            def rstd(var, root, n, signal=None, m=[0]):
                m[0] += 1
                v, y, e = st[:, var:var + n], st[:, root:root + n], st[:, 80:80 + n]
                dve.wait_ge(rstd_done, m[0])
                step(nc.vector.reciprocal(y, y))
                step(nc.vector.tensor_tensor(e, y, y, ALU.mult))
                step(nc.vector.tensor_tensor(e, e, v, ALU.mult))
                step(nc.vector.tensor_scalar(e, e, -0.5, 1.5, ALU.mult, ALU.add))
                last = nc.vector.tensor_tensor(y, y, e, ALU.mult)
                if signal is None:
                    step(last)
                else:
                    last.then_inc(signal, 1)
                    dve.wait_ge(signal, 1)

            nc.vector.memset(z3[NS:P, 2, :], 0.0).then_inc(z_zeroed, 1)
            dve.wait_ge(ct_sig, 1)
            nc.vector.tensor_tensor(cT[:, :], cT[:, :], junk[:, 0:256], ALU.mult).then_inc(ct_done, 1)
            dve.wait_ge(ss_done, 3)
            nc.vector.tensor_scalar(st[:, 0:3], st[:, 0:3], 1.0 / D, EPS, ALU.mult, ALU.add).then_inc(var_done, 1)
            for i in range(4):
                dve.wait_ge(tile_done, i + 1)
                nc.vector.tensor_copy(partA[:, i * BANK:(i + 1) * BANK], bank(i)).then_inc(part_done, 1)
            dve.wait_ge(tab_done, 2)
            dve.wait_ge(g_here, 32)
            step(nc.vector.scalar_tensor_tensor(a1p, bank(4, 2), 1.0, gmix, ALU.add, ALU.mult))
            rstd(0, 3, 3)
            for t in range(3):
                n = TOK[t]
                am, sh = (a1p, bank(6, 2)) if t < 2 else (a1s, bank(2, 2))
                if t == 0:
                    dve.wait_ge(tab_done, 4)
                if t == 2:
                    dve.wait_ge(tab_done, 8)
                    step(nc.vector.scalar_tensor_tensor(a1s[0:n], bank(0, 2)[0:n], 1.0, gmix[0:n], ALU.add, ALU.mult))
                step(nc.vector.scalar_tensor_tensor(hrow[0:n, t, :], x3[0:n, t, :], st[0:n, 3 + t:4 + t], am[0:n],
                                                    ALU.mult, ALU.mult))
                nc.vector.tensor_tensor(hrow[0:n, t, :], hrow[0:n, t, :], sh[0:n], ALU.add).then_inc(h_done, 1)

            def rotate(cols, heads, signal):
                v = z3[:, :, cols:cols + 64 * heads].rearrange("p t (h d) -> p t h d", d=64)
                x1, x2 = v[:, :, :, 0:8], v[:, :, :, 8:16]
                cos, sin = (const(n).rearrange("p (t n) -> p t n", t=3).unsqueeze(2).broadcast_to([P, 3, heads, 8])
                            for n in ("cosq", "sinq"))
                a1, a2, a3, a4 = (m[:, :, 0:heads, :] for m in (t1, t2, t3, t4))
                nc.vector.tensor_tensor(a1, x1, cos, ALU.mult)
                nc.vector.tensor_tensor(a2, x2, sin, ALU.mult)
                nc.vector.tensor_tensor(a3, x2, cos, ALU.mult)
                step(nc.vector.tensor_tensor(a4, x1, sin, ALU.mult))
                nc.vector.tensor_tensor(x1, a1, a2, ALU.subtract)
                ins = nc.vector.tensor_tensor(x2, a3, a4, ALU.add)
                if signal is None:
                    step(ins)
                else:
                    ins.then_inc(signal, 1)

            step(nc.vector.memset(ikbd, 0.0))
            step(nc.vector.memset(kbd, 0.0))
            dve.wait_ge(z_done, 3)
            rotate(CIQ, 9, None)
            for j in range(2):
                last = nc.vector.tensor_copy(ikd[:, :, 64 * j:64 * j + 64], z3[:, :, CIK:CIW])
            last.then_inc(ikd_done, 1)
            rotate(CQ, 10, qk_roped)
            for j in range(2):
                last = nc.vector.tensor_tensor(
                    iwx[0:NS, 32 * j:32 * j + 32].rearrange("p (h t) -> p h t", t=DS),
                    z3[0:NS, 2, CIW:CRQ].rearrange("p (c j) -> p j c", j=2)[:, j, :].unsqueeze(2).broadcast_to([NS, 4, DS]),
                    const("dm")[0:NS].unsqueeze(1).broadcast_to([NS, 4, DS]), ALU.mult)
            last.then_inc(iwx_done, 1)
            dve.wait_ge(tr_act, 1)
            nc.vector.tensor_copy(ikbd[0:64, 0, :], ikTn[0:64, 0:SEQ])
            nc.vector.tensor_copy(ikbd[64:P, 1, :], ikTn[64:P, 0:SEQ]).then_inc(tr_dve, 1)
            for n, col, b in ((4, CIQ, 3), (7, CQ, 6)):
                dve.wait_ge(tr_done, n)
                bd = z3[:, 2, col:col + 512]
                step(nc.vector.memset(bd, 0.0))
                bd = bd.rearrange("p (b j c t) -> p j b c t", b=DB, j=2, c=4)
                src = bank(b)[:, 0:256].rearrange("p (c b t) -> p b c t", c=4, b=DB)
                nc.vector.tensor_copy(bd[0:64, 0], src[0:64])
                nc.vector.tensor_copy(bd[64:P, 1], src[64:P]).then_inc(tr_dve, 1)
            dve.wait_ge(tr_act, 6)
            nc.vector.tensor_copy(kbd[0:64, 0, :], kTn[0:64, 0:SEQ])
            nc.vector.tensor_copy(kbd[64:P, 1, :], kTn[64:P, 0:SEQ]).then_inc(tr_dve, 1)
            dve.wait_ge(iw_mm, 1)
            nc.vector.tensor_copy(iwcol[:, 0:PAIRS], bank(3)[:, 0:PAIRS]).then_inc(iw_done, 1)
            dve.wait_ge(iw_done, 1)

            def prompt_index(t):
                w = (t + 1) * P
                dve.wait_ge(prel_done, t + 1)
                for h in range(8):
                    if h == 0:
                        ins = nc.vector.tensor_scalar(sc_p[:, t, 0:w], rel_p[t][:, 0, 0:w], z3[:, t, CIW:CIW + 1], None, ALU.mult)
                    else:
                        ins = nc.vector.scalar_tensor_tensor(sc_p[:, t, 0:w], rel_p[t][:, h, 0:w],
                                                             z3[:, t, CIW + h:CIW + h + 1], sc_p[:, t, 0:w], ALU.mult, ALU.add)
                    if h < 7:
                        step(ins)
                ins.then_inc(psc_done, 1)

            for i in range(PAIRS):
                dve.wait_ge(sdot_done, i + 1)
                if i:
                    dve.wait_ge(ssel_done, i)
                nc.vector.tensor_scalar(rel_s, ps[:, 3 * BANK:3 * BANK + KEYS], 0.0, iwcol[:, i:i + 1],
                                        ALU.max, ALU.mult).then_inc(srel_done, 1)
            prompt_index(0)
            prompt_index(1)

            def top(v, k):
                m8 = st[0:v.shape[0], 40:48]
                for _ in range(k // 8):
                    step(nc.vector.max(m8, v))
                    step(nc.vector.match_replace(v, m8, v, TAKEN))

            for t in range(2):
                w = (t + 1) * P
                dve.wait_ge(pcap_done, t + 1)
                top(sc_p[:, t, 0:w], min(256, SEQ // 4))
                nc.vector.tensor_scalar(mask_p[:, t, 0:w], sc_p[:, t, 0:w], -2.0e38, NEG, ALU.is_gt, ALU.mult).then_inc(pmask_raw, 1)
            dve.wait_ge(ssc_done, 1)
            caps = const("caps")[0:NS]
            step(nc.vector.tensor_tensor(sc_s[0:NS, PAST:KEYS], sc_s[0:NS, PAST:KEYS], caps, ALU.min))
            top(sc_s[0:NS], min(256, KEYS // 4))
            step(nc.vector.tensor_scalar(mask_s[0:NS], sc_s[0:NS], -2.0e38, NEG, ALU.is_gt, ALU.mult))
            nc.vector.tensor_tensor(mask_s[0:NS, PAST:KEYS], mask_s[0:NS, PAST:KEYS], caps, ALU.min).then_inc(masks_done, 1)

            dve.wait_ge(rot_done, 3)
            dve.wait_ge(pcap_done, 4)
            for t in range(2):
                w = (t + 1) * P
                b0 = (6, 0)[t]
                dve.wait_ge(psc2_done, t + 1)
                if t:
                    dve.wait_ge(ppt_tr, 1)
                mask = mask_p[:, t, 0:w].unsqueeze(1).broadcast_to([P, 8, w])
                step(nc.vector.tensor_tensor(p_p[:, :, 0:w], ps[:, b0 * BANK:b0 * BANK + 8 * w].rearrange("p (h n) -> p h n", h=8),
                                             mask, ALU.add))
                step(nc.vector.tensor_reduce(mx, p_p[:, :, 0:w], AX.X, ALU.max))
                nc.vector.tensor_scalar(nm, mx, -ATT_SCALE, None, ALU.mult).then_inc(pmx_done, 1)
                dve.wait_ge(pexp_done, 8 * (t + 1))
                step(nc.vector.reciprocal(rs, rs))
                nc.vector.tensor_tensor(p_p[:, :, 0:w], p_p[:, :, 0:w], rs.unsqueeze(2).broadcast_to([P, 8, w]),
                                        ALU.mult).then_inc(pp_done, 1)
            for i in range(PAIRS):
                dve.wait_ge(ssc2_done, i + 1)
                step(nc.vector.tensor_reduce(mx[:, 0:1], ps[:, 0:KEYS], AX.X, ALU.max))
                nc.vector.tensor_scalar(nm[:, 0:1], mx[:, 0:1], -ATT_SCALE, None, ALU.mult).then_inc(smx_done, 1)
                dve.wait_ge(tile_done, 18 + i)
                nc.vector.tensor_copy(partB[i], bank(3)).then_inc(partb_done, 1)
                dve.wait_ge(spt_tr, i + 1)
                if i:
                    dve.wait_ge(spv_done, i)
                nc.vector.tensor_copy(pT_s[:, 0:NPAGES, :], bank(3, 2).rearrange("p (n q) -> p n q", q=P))
                nc.vector.tensor_copy(pT_s[0:DS, NPAGES, :], bank(2)[0:DS, P:2 * P]).then_inc(spt_done, 1)
                step(nc.vector.reciprocal(rs[:, i % 2:i % 2 + 1], rs[:, i % 2:i % 2 + 1]))
                dve.wait_ge(spv_done, i + 1)
                if i:
                    dve.wait_ge(sa_tr, i)
                nc.vector.tensor_scalar(o_s, bank(5)[:, 0:P], rs[:, i % 2:i % 2 + 1], None, ALU.mult).then_inc(so_done, 1)

            dve.wait_ge(gates_done, 6)

            def each_piece(b):
                yield 0, P, bank(b), slice(0, BANK)
                yield 1, P, bank(b + 1), slice(0, BANK)
                yield 2, NS, bank(b + 2)[0:NS, 0:256], slice(0, 256)
                yield 2, NS, bank(b + 2)[NS:P, 0:256], slice(256, BANK)

            def shifted(v, c, i):
                return v[:, i * BANK + c.start:i * BANK + c.stop]

            for i in range(2):
                if i == 0:
                    dve.wait_ge(ya_mm, 1)
                else:
                    dve.wait_ge(tile_done, 22)
                for t, n, src, c in each_piece(3 * i):
                    g = shifted(z3[0:n, t, CGA:CGB], c, i)
                    last = nc.vector.tensor_tensor(g, src, g, ALU.mult)
                last.then_inc(ya_done, 1)
            for h in range(2):
                dve.wait_ge(tile_done, 23 + h)
                nc.vector.tensor_copy(partB[4 + h], bank(6 + h)).then_inc(partb_done, 1)
            step(nc.vector.memset(rbd, 0.0))
            dve.wait_ge(dec_here, 64)
            kvp = bank(6, 2).rearrange("p (c j n) -> p c j n", c=4, j=2)

            def ret_operands(t):
                n = TOK[t]
                dve.wait_ge(r_tr, 2 * t + 1)
                if t:
                    dve.wait_ge(r_sc, t)
                src = bank(0)[:, 0:4 * n].rearrange("p (c n) -> p c n", c=4)
                if t == 1:
                    nc.vector.tensor_tensor(rqdec, src, qdec_p.rearrange("p (c n) -> p c n", c=4), ALU.mult)
                if t == 2:
                    dve.wait_ge(r_zero, 2)
                    qd = const("qdecs").rearrange("p (c j t) -> p j c t", c=4, j=2)
                    for j in range(2):
                        for b in range(2):
                            for e in range(4):
                                bb = 2 * e + b
                                nc.vector.tensor_tensor(
                                    qm[64 * b:64 * b + 64, :, e, bb * DS:(bb + 1) * DS].rearrange("p (c j) t -> p j c t", j=2)[:, j],
                                    src[64 * j:64 * j + 64, :, bb * DS:(bb + 1) * DS], qd[64 * b:64 * b + 64, j], ALU.mult)
                nc.vector.tensor_copy(rbd[0:64, :, 0, 0:n], src[0:64])
                nc.vector.tensor_copy(rbd[64:P, :, 1, 0:n], src[64:P]).then_inc(r_ops, 1)

            ret_operands(0)
            dve.wait_ge(r_st, 1)
            nc.vector.tensor_copy(s1[0:64], kvp[0:64, :, 0])
            nc.vector.tensor_copy(s1[64:P], kvp[64:P, :, 1]).then_inc(r_s1, 1)
            for t in range(3):
                n = TOK[t]
                dve.wait_ge(r_sc, t + 1)
                if t:
                    dve.wait_ge(r_o, t)
                scp = ps[0:n, 2 * BANK:2 * BANK + 8 * n].rearrange("p (h n) -> p h n", h=8)
                if t < 2:
                    nc.vector.tensor_tensor(sT[:, 0:6, :], scp[:, 0:6], dec_a.rearrange("p (h n) -> p h n", n=P), ALU.mult)
                    nc.vector.tensor_tensor(sT[:, 6:8, :], scp[:, 6:8], dec_b.rearrange("p (h n) -> p h n", n=P),
                                            ALU.mult).then_inc(r_sT, 1)
                else:
                    nc.vector.tensor_tensor(sT[0:n, :, 0:n], scp, dec_s[0:n].rearrange("p (h n) -> p h n", n=NS),
                                            ALU.mult).then_inc(r_sT, 1)
                if t < 2:
                    ret_operands(t + 1)
                if t:
                    dve.wait_ge(tile_done, 24 + t)
                    nc.vector.tensor_copy(partB[5 + t], bank(2)).then_inc(partb_done, 1)
                dve.wait_ge(r_o, t + 1)
                o = bank(4, 2)[0:n].rearrange("p (h v) -> p h v", h=8)
                for h in range(8):
                    last = nc.vector.bn_stats(gst[0:n, h, :], o[:, h, :])
                step(last)
                for h in range(8):
                    last = nc.vector.bn_aggr(gmv[0:n, h, :], gst[0:n, h, :])
                step(last)
                nc.vector.tensor_scalar(st[0:n, 16:24], gmv[0:n, :, 1], 1.0, GN_EPS, ALU.mult, ALU.add).then_inc(gn_var, 1)
                r = z3[0:n, t, CRG:CGA].rearrange("p (h v) -> p h v", h=8)
                for h in range(8):
                    last = nc.vector.scalar_tensor_tensor(r[:, h, :], o[:, h, :], gmv[0:n, h, 0:1], r[:, h, :], ALU.subtract, ALU.mult)
                last.then_inc(r_gn, 1)
                dve.wait_ge(r_gn, t + 1)
                if t == 1:
                    dve.wait_ge(r_st, 2)
                    step(nc.vector.tensor_tensor(s1, s1, const("gchunk").unsqueeze(2).broadcast_to([P, 4, P]), ALU.mult))
                    nc.vector.tensor_tensor(s1[0:64], s1[0:64], kvp[0:64, :, 0], ALU.add)
                    nc.vector.tensor_tensor(s1[64:P], s1[64:P], kvp[64:P, :, 1], ALU.add).then_inc(retp_done, 1)
                rstd(16, 24, 8)
                nc.vector.tensor_tensor(r, r, st[0:n, 24:32].unsqueeze(2).broadcast_to([n, 8, P]), ALU.mult).then_inc(r_done, 1)
            for e in range(4):
                dve.wait_ge(ns_mm, e + 1)
                dve.wait_ge(st_scaled, e + 1)
                nc.vector.tensor_tensor(state[:, e], bank((6, 0)[e % 2], 2).rearrange("p (h v) -> p h v", h=8), state[:, e],
                                        ALU.add).then_inc(ns_done, 1)
            dve.wait_ge(gb_sig, 3)
            for i in range(2):
                dve.wait_ge(tile_done, 27 + i)
                for t, n, src, c in each_piece(3 * i):
                    g = shifted(z3[0:n, t, CGB:DIN], c, i)
                    last = nc.vector.tensor_tensor(g, src, g, ALU.mult)
                step(last)
                for t in range(3):
                    n = TOK[t]
                    ga, gb_ = (z3[0:n, t, c0 + i * BANK:c0 + (i + 1) * BANK] for c0 in (CGA, CGB))
                    last = nc.vector.tensor_tensor(ga, ga, gb_, ALU.add)
                last.then_inc(yb_done, 1)
            dve.wait_ge(tb_out, 6)
            dve.wait_ge(rw_here, 48)
            nc.vector.scalar_tensor_tensor(a2p, a2p, 1.0, gffn, ALU.add, ALU.mult)
            nc.vector.scalar_tensor_tensor(a2s[0:NS], a2s[0:NS], 1.0, gffn[0:NS], ALU.add, ALU.mult)
            for i in range(2):
                dve.wait_ge(tile_done, 29 + i)
                for t, n, src, c in each_piece(3 * i):
                    last = nc.vector.tensor_tensor(shifted(tmp3[0:n, t, :], c, i), src, shifted((gt1s if t == 2 else gt1p)[0:n], c, i), ALU.mult)
                step(last)
                for t in range(3):
                    n = TOK[t]
                    xs = x3[0:n, t, i * BANK:(i + 1) * BANK]
                    last = nc.vector.tensor_tensor(xs, xs, tmp3[0:n, t, i * BANK:(i + 1) * BANK], ALU.add)
                    if i:
                        last.then_inc(x1_done, 1)
                if i == 0:
                    step(last)
            dve.wait_ge(ss2_done, 3)
            nc.vector.tensor_scalar(st[:, 8:11], st[:, 8:11], 1.0 / D, EPS, ALU.mult, ALU.add).then_inc(var_done, 1)
            rstd(8, 11, 3, rstd2_done)
            for t in range(2):
                n, am, sh = TOK[t], a2p, sh2p
                step(nc.vector.scalar_tensor_tensor(h2[0:n, t, :], x3[0:n, t, :], st[0:n, 11 + t:12 + t], am[0:n],
                                                    ALU.mult, ALU.mult))
                nc.vector.tensor_tensor(h2[0:n, t, :], h2[0:n, t, :], sh[0:n], ALU.add).then_inc(h2_done, 1)
            nc.vector.memset(m8s, 3.0e38)
            nc.vector.memset(sel_m, 0.0)
            step(nc.vector.memset(gate_r, 0.0))
            dve.wait_ge(lg_mm, 1)
            for t in range(3):
                n = TOK[t]
                last = nc.vector.tensor_tensor(lgt[0:n, t, :], bank(5)[0:n, t * NE:(t + 1) * NE], br[0:n], ALU.add)
            step(last)
            for t in range(3):
                last = nc.vector.max(m8r[0:TOK[t], 8 * t:8 * t + 8], lgt[0:TOK[t], t, :])
            step(last)
            for t in range(3):
                last = nc.vector.tensor_scalar(nmr[0:TOK[t], t:t + 1], m8r[0:TOK[t], 8 * t:8 * t + 1], -1.0, None, ALU.mult)
            last.then_inc(m0_done, 1)
            for t in range(3):
                n = TOK[t]
                step(nc.vector.tensor_copy(m8s[0:n, 0:4], m8r[0:n, 8 * t:8 * t + 4]))
                step(nc.vector.match_replace(lrep[0:n, t, :], m8s[0:n], lgt[0:n, t, :], TAKEN))
                last = nc.vector.tensor_scalar(sel_m[0:n, t, :], lrep[0:n, t, :], -2.0e38, None, ALU.is_lt)
                if t < 2:
                    step(last)
            last.then_inc(selm_done, 1)
            dve.wait_ge(selm_done, 1)
            dve.wait_ge(ex_done, 3)
            for t in range(3):
                n = TOK[t]
                step(nc.vector.tensor_tensor(ex[0:n, t, :], ex[0:n, t, :], sel_m[0:n, t, :], ALU.mult))
                step(nc.vector.tensor_reduce(srt[0:n, t:t + 1], ex[0:n, t, :], AX.X, ALU.add))
                step(nc.vector.reciprocal(srt[0:n, t:t + 1], srt[0:n, t:t + 1]))
                last = nc.vector.tensor_scalar(gate_r[0:n, t, :], ex[0:n, t, :], srt[0:n, t:t + 1], None, ALU.mult)
            last.then_inc(gate_done, 1)
            dve.wait_ge(pos_mm, 1)
            step(nc.vector.scalar_tensor_tensor(pos_r, bank(6)[:, 0:96].rearrange("p (t e) -> p t e", t=3), 1.0, sel_m, ALU.add, ALU.mult))
            step(nc.vector.tensor_scalar(pos_r, pos_r, -1.0, None, ALU.add))
            ident_q = ident.rearrange("p (q e) -> p q e", q=4)

            def pick(n, tab, i, n_zero):
                if not n_zero:
                    dve.wait_ge(x_mm, n)
                for t in range(3):
                    last = nc.vector.tensor_scalar(S[:, t, :], const("iota"), tab[:, t, bass.ds(i, 1)], None, ALU.is_equal)
                last.then_inc(s_done, 1)

            def pick_gates(n, tab, gates, i):
                dve.wait_ge(at_tr, n + 1)
                for t in range(3):
                    last = nc.vector.tensor_scalar(Sg[:, t, :].rearrange("p (i n) -> p i n", i=2),
                                                   const("iota").unsqueeze(1).broadcast_to([P, 2, CAP]), tab[:, t, bass.ds(i, 1)],
                                                   gates[:, t, bass.ds(i, 1)], ALU.is_equal, ALU.mult)
                last.then_inc(sg_done, 1)

            def pick_bias(n, sel, i, n_zero):
                if not n_zero:
                    dve.wait_ge(chunk_used, n * 12 - 4)
                nc.vector.tensor_copy(ebuf, sel[:, :, bass.ds(i, 1)].broadcast_to([P, 4, CAP])).then_inc(ebuf_done, 1)

            def add_results(n):
                for i, (t, half) in enumerate(PIECES):
                    dve.wait_ge(cmb_mm, n * 5 + (i + 1))
                    b = 6 + i % 2
                    if t < 2:
                        v = acc[:, t, half * BANK:(half + 1) * BANK]
                        nc.vector.tensor_tensor(v, v, bank(b), ALU.add).then_inc(acc_done, 1)
                    else:
                        for half in range(2):
                            v = acc[0:NS, 2, half * BANK:(half + 1) * BANK]
                            last = nc.vector.tensor_tensor(v, v, bank(b)[64 * half:64 * half + 64, :], ALU.add)
                        last.then_inc(acc_done, 1)

            def expert(n, i, tab, gates, sel, first, last_one):
                if not last_one:
                    pick(n + 1, tab, i + 1, False)
                if not first:
                    pick_gates(n - 1, tab, gates, i - 1)
                dve.wait_ge(chunk_used, n * 12 + 8)
                nc.vector.tensor_scalar(gb, bank(0), 7.0, None, ALU.min).then_inc(g_done, 1)
                nc.vector.tensor_scalar(ub, bank(1), -7.0, 7.0, ALU.max, ALU.min).then_inc(u_done, 1)
                if not last_one:
                    pick_bias(n + 1, sel, i + 1, False)
                dve.wait_ge(sig_done, n + 1)
                nc.vector.tensor_tensor(sgm, sgm, gb, ALU.mult).then_inc(mul_done, 1)
                dve.wait_ge(mul_done, n + 1)
                nc.vector.scalar_tensor_tensor(gb, ub, 1.0, sgm, ALU.add, ALU.mult).then_inc(act_done, 1)
                if not first:
                    add_results(n - 1)

            def experts(count, base, tab, gates, sel):
                if base:
                    pick(base, tab, 0, False)
                    pick_bias(base, sel, 0, False)
                expert(base, 0, tab, gates, sel, True, False)
                with dve.Fori(1, count - 1) as i:
                    expert(i + base, i, tab, gates, sel, False, False)
                n = base + count - 1
                expert(n, count - 1, tab, gates, sel, False, True)
                pick_gates(n, tab, gates, count - 1)
                add_results(n)
                dve.wait_ge(acc_done, 5 * (base + count) + 3)

            pick(0, pos_r, 0, True)
            pick_bias(0, ident_q, 0, True)
            step(nc.vector.tensor_copy(cnt, bank(6)[:, 96:128]))
            step(nc.vector.tensor_scalar(extra, cnt, float(CAP), None, ALU.is_gt))
            for r in range(2, NTOK // CAP):
                step(nc.vector.scalar_tensor_tensor(extra, cnt, float(CAP * r), extra, ALU.is_gt, ALU.add))
            run, other, w = extra, cum, 1
            while w < NE:
                step(nc.vector.tensor_copy(other[:, 0:w], run[:, 0:w]))
                step(nc.vector.tensor_tensor(other[:, w:NE], run[:, w:NE], run[:, 0:NE - w], ALU.add))
                run, other = other, (cum2 if other is cum else cum)
                w *= 2
            nc.vector.tensor_copy(pt[0:1, 0:1], run[0:1, NE - 1:NE]).then_inc(flag_done, 1)

            dve.wait_ge(acc_done, 3)
            experts(NE, 0, pos_r, gate_r, ident_q)
            dve.wait_ge(flag_done, 1)
            more = dve.value_load(pt[0:1, 0:1], min_val=0, max_val=XBLK)
            with dve.If(more > 0):
                iota_x = const("iota")[:, 0:XBLK].unsqueeze(2).broadcast_to([P, XBLK, NE])
                cum_b = run.unsqueeze(1).broadcast_to([P, XBLK, NE])
                nc.vector.memset(tot[:, 0:1], 0.0)
                step(nc.vector.tensor_copy(tot[:, 1:NE], run[:, 0:NE - 1]))
                nc.vector.tensor_tensor(oh, iota_x, tot.unsqueeze(1).broadcast_to([P, XBLK, NE]), ALU.is_ge)
                step(nc.vector.tensor_tensor(oh2, iota_x, cum_b, ALU.is_lt))
                step(nc.vector.tensor_tensor(oh, oh, oh2, ALU.mult))

                def chosen(dst, row):
                    step(nc.vector.tensor_tensor(oh2, oh, row.unsqueeze(1).broadcast_to([P, XBLK, NE]), ALU.mult))
                    step(nc.vector.tensor_reduce(dst, oh2, AX.X, ALU.add))

                chosen(rx, tot)
                chosen(eidx, const("iota")[:, 0:NE])
                step(nc.vector.tensor_tensor(rx, const("iota")[:, 0:XBLK], rx, ALU.subtract))
                step(nc.vector.tensor_scalar(rx, rx, 1.0, float(CAP), ALU.add, ALU.mult))
                for t in range(3):
                    chosen(pos_x[:, t, :], pos_r[:, t, :])
                    step(nc.vector.tensor_tensor(pos_x[:, t, :], pos_x[:, t, :], rx, ALU.subtract))
                    chosen(gate_x[:, t, :], gate_r[:, t, :])
                for q in range(4):
                    step(nc.vector.tensor_scalar(sel_x[:, q, :], eidx, const("pcol")[:, q:q + 1], None, ALU.is_equal))
                nc.vector.tensor_copy(pt[0:1, 8:8 + XBLK], eidx[0:1]).then_inc(flag_done, 1)
                experts(XBLK, NE, pos_x, gate_x, sel_x)
            dve.wait_ge(g2_done, 2)
            for t in range(3):
                n = TOK[t]
                g2 = (gt2s if t == 2 else gt2p)[0:n]
                last = nc.vector.tensor_tensor(acc[0:n, t, :], acc[0:n, t, :], g2, ALU.mult)
            steps2 = last.then_inc(fin_step, 1)
            dve.wait_ge(fin_step, 1)
            for t in range(3):
                n = TOK[t]
                nc.vector.tensor_tensor(x3[0:n, t, :], x3[0:n, t, :], acc[0:n, t, :], ALU.add).then_inc(x1_done, 1)
            dve.wait_ge(ss2_done, 6)
            nc.vector.tensor_scalar(st[:, 8:11], st[:, 8:11], 1.0 / D, EPS, ALU.mult, ALU.add).then_inc(var_done, 1)
            dve.wait_ge(rstd_done, 6)
            v, y, e_ = st[:, 8:11], st[:, 11:14], st[:, 80:83]
            for k, ins in enumerate((lambda: nc.vector.reciprocal(y, y), lambda: nc.vector.tensor_tensor(e_, y, y, ALU.mult),
                                     lambda: nc.vector.tensor_tensor(e_, e_, v, ALU.mult),
                                     lambda: nc.vector.tensor_scalar(e_, e_, -0.5, 1.5, ALU.mult, ALU.add),
                                     lambda: nc.vector.tensor_tensor(y, y, e_, ALU.mult))):
                ins().then_inc(fin_step, 1)
                dve.wait_ge(fin_step, 2 + k)
            dve.wait_ge(late_here, 48)
            for t in range(3):
                n = TOK[t]
                nc.vector.scalar_tensor_tensor(x3[0:n, t, :], x3[0:n, t, :], st[0:n, 11 + t:12 + t], gfin[0:n],
                                               ALU.mult, ALU.mult).then_inc(yf_done, 1)


def kernel(**inputs):
    from concourse import bacc
    from concourse.bass_utils import run_bass_kernel_spmd

    v = {k: np.asarray(x) for k, x in inputs.items()}
    dec_p, dec_s, qdec_p = decay_tables()
    c = np.zeros((32, D), np.float32)
    c[0], c[1:1 + DB] = v["c_prompt"][0], v["c_sample"]
    w_in = v["w_in"][0]
    wq = w_in[:, CQ:CK].reshape(D, 2, 4, 64).transpose(0, 2, 1, 3).reshape(D, CK)
    arrays = {
        "x_prompt": v["x_prompt"], "x_sample": v["x_sample"], "page_table": v["page_table"].reshape(1, -1),
        "norm_mix_g": v["norm_mix_g"][0], "norm_ffn_g": v["norm_ffn_g"][0], "norm_final_g": v["norm_final_g"],
        "cache_kv": np.concatenate([v[n][0].reshape(NPOOL, PAGE, P) for n in ("cache_k", "cache_v")], axis=2),
        "cache_ik": v["cache_ik"][0], "state": v["state_ret"][0],
        "cT": c.reshape(32, KT, P).transpose(2, 1, 0).reshape(P, KT * 32),
        "const": CONST, "dec_p": dec_p, "dec_s": dec_s, "qdec_p": qdec_p,
        "w_ada": v["w_ada"][0], "b_ada": v["b_ada"],
        "w_in": np.concatenate([wq, w_in[:, CK:]], axis=1),
        "w_branch_a": v["w_branch_a"][0].reshape(2, 4, 64, D).transpose(1, 0, 2, 3).reshape(512, D),
        "w_branch_b": v["w_branch_b"][0], "w_out": v["w_out"][0],
        "w_router": v["w_router"][0], "b_router": v["b_router"][0],
        "w_gate_up": v["w_gate_up"][0], "w_down": v["w_down"][0], "b_down": v["b_down"][0],
        "b_gate_up": v["b_gate_up"][0].reshape(NE, 4, BANK).transpose(1, 0, 2).reshape(4 * NE, BANK),
    }
    outputs = {"y_prompt": (SEQ, D), "y_sample": (NS, D), "k_prompt": (SEQ, P), "v_prompt": (SEQ, P), "ik_prompt": (SEQ, 64),
               "ret_prompt": (8, 64, P), "k_sample": (NS, P), "v_sample": (NS, P), "ik_sample": (NS, 64),
               "ret_sample": (DB, 8, 64, P)}
    shapes = {"y_prompt": (1, SEQ, D), "y_sample": (DB, DS, D), "k_prompt": (1, 1, SEQ, 2, 64), "v_prompt": (1, 1, SEQ, 2, 64),
              "ik_prompt": (1, 1, SEQ, 64), "ret_prompt": (1, 1, 8, 64, P), "k_sample": (1, DB, DS, 2, 64),
              "v_sample": (1, DB, DS, 2, 64), "ik_sample": (1, DB, DS, 64), "ret_sample": (1, DB, 8, 64, P)}
    nc = bacc.Bacc("TRN2", target_bir_lowering=False, num_devices=1)
    arrays = {f"in_{k}": np.ascontiguousarray(x) for k, x in arrays.items()}
    a = {k[3:]: nc.dram_tensor(k, x.shape, mybir.dt.from_np(x.dtype), kind="ExternalInput").ap()
         for k, x in arrays.items()}
    for k, s in outputs.items():
        a[k] = nc.dram_tensor(k, s, F32, kind="ExternalOutput").ap()
    kern(nc, a)
    r = run_bass_kernel_spmd(nc, [arrays], core_ids=[0])
    return tuple(np.asarray(r.results[0][k]).reshape(shapes[k]) for k in outputs)
```
